# Optimizing a Trainium2 kernel written in Bass

```python
import math
import jax, jax.numpy as jnp
from jax import lax
import numpy as np

D_MODEL = 1024
BATCH = 1
SEQ = 512
DEPTH = 1

RWKV_HEAD = 64
RWKV_HEADS = 8
RWKV_DIM = RWKV_HEADS * RWKV_HEAD
W_LORA = 64
A_LORA = 64
G_LORA = 128
DECAY_SCALE = math.exp(-0.5)
LNX_EPS = 64e-5
ATT_HEADS = 8
ATT_KV_HEADS = 2
ATT_HEAD = 64
ATT_DIM = ATT_HEADS * ATT_HEAD
KV_DIM = ATT_KV_HEADS * ATT_HEAD
WINDOW = 128
BLOCK = 128
NEG_INF = -1e30
N_EXPERTS = 16
CAPACITY_FACTOR = 2
EXPERT_FF = 1024
NORM_EPS = 1e-6

RWKV_SPLITS = (RWKV_DIM, 2 * RWKV_DIM, 3 * RWKV_DIM, 3 * RWKV_DIM + G_LORA,
               3 * RWKV_DIM + G_LORA + W_LORA, 3 * RWKV_DIM + G_LORA + 2 * W_LORA,
               3 * RWKV_DIM + G_LORA + 2 * W_LORA + A_LORA)
RWKV_COLS = 3 * RWKV_DIM + G_LORA + 2 * W_LORA + 2 * A_LORA
ATT_SPLITS = (ATT_DIM, ATT_DIM + KV_DIM, ATT_DIM + 2 * KV_DIM, ATT_DIM + 2 * KV_DIM + D_MODEL)
IN_COLS = RWKV_COLS + ATT_DIM + 2 * KV_DIM + 2 * D_MODEL


def rms_norm(x, g):
    xf = x.astype(jnp.float32)
    y = xf * lax.rsqrt(jnp.mean(xf * xf, axis=-1, keepdims=True) + NORM_EPS)
    return (y * g.astype(jnp.float32)).astype(x.dtype)

def centred_token_shift(u, mu_prev, mu_next):
    prev = jnp.pad(u, ((0, 0), (1, 0), (0, 0)))[:, :-1]
    nxt = jnp.pad(u, ((0, 0), (0, 1), (0, 0)))[:, 1:]
    return u + mu_prev * (prev - u) + mu_next * (nxt - u)

def wkv7_scan(r, decay, k, v, kk, a, reverse):
    B, T, H, N = r.shape
    xs = tuple(jnp.moveaxis(t.astype(jnp.float32), 1, 0) for t in (r, decay, k, v, kk, a))

    def step(S, inp):
        r_t, w_t, k_t, v_t, kk_t, a_t = inp
        s_kk = jnp.einsum('bhij,bhj->bhi', S, kk_t)
        S = (S * w_t[:, :, None, :]
             - s_kk[..., None] * (a_t * kk_t)[:, :, None, :]
             + v_t[..., None] * k_t[:, :, None, :])
        return S, jnp.einsum('bhij,bhj->bhi', S, r_t)

    S0 = jnp.zeros((B, H, N, N), jnp.float32)
    _, y = lax.scan(step, S0, xs, reverse=reverse)
    return jnp.moveaxis(y, 0, 1)

def rwkv7_bidir(u, w0_f, w_up_f, w0_b, w_up_b, a0_f, a_up_f, a0_b, a_up_b, g_up, k_k, k_a, r_k, ln_w, ln_b):
    f32 = jnp.float32
    B, T, _ = u.shape
    r, k, v, g_lo, wf_lo, wb_lo, af_lo, ab_lo = jnp.split(u, RWKV_SPLITS, axis=-1)

    def heads(t):
        return t.reshape(B, T, RWKV_HEADS, RWKV_HEAD)

    def decay(w0, lo, up):
        return jnp.exp(-DECAY_SCALE * jax.nn.sigmoid((w0 + jnp.tanh(lo) @ up).astype(f32)))

    def icl_rate(a0, lo, up):
        return jax.nn.sigmoid((a0 + lo @ up).astype(f32))

    kf = k.astype(f32)
    kk = heads(kf * k_k.astype(f32))
    kk = kk / jnp.maximum(jnp.sqrt(jnp.sum(kk * kk, axis=-1, keepdims=True)), 1e-12)
    a_f = icl_rate(a0_f, af_lo, a_up_f)
    a_b = icl_rate(a0_b, ab_lo, a_up_b)
    k_f = heads(kf * (1.0 + (a_f - 1.0) * k_a.astype(f32)))
    k_b = heads(kf * (1.0 + (a_b - 1.0) * k_a.astype(f32)))
    r4 = heads(r.astype(f32))
    v4 = heads(v.astype(f32))

    wkv = (wkv7_scan(r4, heads(decay(w0_f, wf_lo, w_up_f)), k_f, v4, kk, heads(a_f), False)
           + wkv7_scan(r4, heads(decay(w0_b, wb_lo, w_up_b)), k_b, v4, kk, heads(a_b), True))

    mean = jnp.mean(wkv, axis=-1, keepdims=True)
    var = jnp.mean(jnp.square(wkv - mean), axis=-1, keepdims=True)
    normed = ((wkv - mean) * lax.rsqrt(var + LNX_EPS)).reshape(B, T, RWKV_DIM)
    normed = normed * ln_w.astype(f32) + ln_b.astype(f32)

    rk = r_k.astype(f32)
    bonus = ((jnp.sum(r4 * k_f * rk, axis=-1, keepdims=True)
              + jnp.sum(r4 * k_b * rk, axis=-1, keepdims=True)) * v4).reshape(B, T, RWKV_DIM)
    g = (jax.nn.sigmoid(g_lo) @ g_up).astype(f32)
    return ((normed + bonus) * g).astype(u.dtype)

def alibi_slopes(n_heads):
    return 2.0 ** (-8.0 * np.arange(1, n_heads + 1) / n_heads)

def banded_gqa_attention(q, k, v, sink):
    f32 = jnp.float32
    B, T, HQ, DH = q.shape
    G = HQ // ATT_KV_HEADS
    nb = T // BLOCK
    span = BLOCK + 2 * WINDOW
    q = q.reshape(B, T, ATT_KV_HEADS, G, DH) * (DH ** -0.5)
    kp = jnp.pad(k, ((0, 0), (WINDOW, WINDOW), (0, 0), (0, 0)))
    vp = jnp.pad(v, ((0, 0), (WINDOW, WINDOW), (0, 0), (0, 0)))
    slopes = jnp.asarray(alibi_slopes(HQ), f32).reshape(ATT_KV_HEADS, G)
    sink_l = sink.astype(f32).reshape(1, ATT_KV_HEADS, G, 1, 1)
    l_idx = jnp.arange(BLOCK)
    j_idx = jnp.arange(span)
    rel = j_idx[None, :] - WINDOW - l_idx[:, None]
    in_window = jnp.abs(rel) <= WINDOW
    alibi = -slopes[:, :, None, None] * jnp.abs(rel).astype(f32)

    def one_block(i):
        start = i * BLOCK
        qb = lax.dynamic_slice_in_dim(q, start, BLOCK, axis=1)
        kb = lax.dynamic_slice_in_dim(kp, start, span, axis=1)
        vb = lax.dynamic_slice_in_dim(vp, start, span, axis=1)
        key_pos = start - WINDOW + j_idx
        valid = in_window & ((key_pos >= 0) & (key_pos < T))[None, :]
        s = jnp.einsum('blkgd,bjkd->bkglj', qb, kb).astype(f32) + alibi
        s = jnp.where(valid, s, NEG_INF)
        m = jnp.maximum(jnp.max(s, axis=-1, keepdims=True), sink_l)
        p = jnp.exp(s - m)
        denom = jnp.sum(p, axis=-1, keepdims=True) + jnp.exp(sink_l - m)
        return jnp.einsum('bkglj,bjkd->blkgd', (p / denom).astype(vb.dtype), vb)

    out = lax.map(one_block, jnp.arange(nb))
    return jnp.moveaxis(out, 0, 1).reshape(B, T, HQ * DH)

def expert_choice_moe(h, w_router, w_gate, w_up, w_down):
    B, T, D = h.shape
    cap = CAPACITY_FACTOR * T // N_EXPERTS
    affinity = jax.nn.softmax((h @ w_router).astype(jnp.float32), axis=-1)
    top_vals, top_idx = lax.top_k(jnp.swapaxes(affinity, 1, 2), cap)
    b_idx = jnp.arange(B)[:, None, None]
    xs = h[b_idx, top_idx]
    hid = jax.nn.silu(jnp.einsum('becd,edf->becf', xs, w_gate)) * jnp.einsum('becd,edf->becf', xs, w_up)
    ys = jnp.einsum('becf,efd->becd', hid, w_down) * top_vals[..., None].astype(h.dtype)
    return jnp.zeros_like(h).at[b_idx, top_idx].add(ys)

def first_inputs(seed: int = 0) -> dict:
    key = jax.random.key(seed)
    ks = jax.random.split(key, 32)
    L, D, f32 = DEPTH, D_MODEL, jnp.float32
    nrm = lambda k, shape, s: (jax.random.normal(k, shape, f32) * s)
    return {
        'x': nrm(ks[0], (BATCH, SEQ, D), 1.0),
        'norm_mix_g': 1.0 + nrm(ks[1], (L, D), 0.1),
        'w_in': nrm(ks[2], (L, D, IN_COLS), D ** -0.5),
        'mu_prev': jax.random.uniform(ks[3], (L, RWKV_COLS), f32, 0.05, 0.45),
        'mu_next': jax.random.uniform(ks[4], (L, RWKV_COLS), f32, 0.05, 0.45),
        'w0_f': nrm(ks[5], (L, RWKV_DIM), 1.0),
        'w_up_f': nrm(ks[6], (L, W_LORA, RWKV_DIM), 0.5 * W_LORA ** -0.5),
        'w0_b': nrm(ks[7], (L, RWKV_DIM), 1.0),
        'w_up_b': nrm(ks[8], (L, W_LORA, RWKV_DIM), 0.5 * W_LORA ** -0.5),
        'a0_f': nrm(ks[9], (L, RWKV_DIM), 0.5),
        'a_up_f': nrm(ks[10], (L, A_LORA, RWKV_DIM), 0.5 * A_LORA ** -0.5),
        'a0_b': nrm(ks[11], (L, RWKV_DIM), 0.5),
        'a_up_b': nrm(ks[12], (L, A_LORA, RWKV_DIM), 0.5 * A_LORA ** -0.5),
        'g_up': nrm(ks[13], (L, G_LORA, RWKV_DIM), G_LORA ** -0.5),
        'k_k': 0.85 + nrm(ks[14], (L, RWKV_DIM), 0.05),
        'k_a': 1.0 + nrm(ks[15], (L, RWKV_DIM), 0.05),
        'r_k': nrm(ks[16], (L, RWKV_HEADS, RWKV_HEAD), 0.1),
        'ln_x_w': 1.0 + nrm(ks[17], (L, RWKV_DIM), 0.1),
        'ln_x_b': nrm(ks[18], (L, RWKV_DIM), 0.02),
        'attn_sink': nrm(ks[19], (L, ATT_HEADS), 0.5),
        'w_proj_rwkv': nrm(ks[20], (L, RWKV_DIM, D), RWKV_DIM ** -0.5),
        'w_proj_attn': nrm(ks[21], (L, ATT_DIM, D), ATT_DIM ** -0.5),
        'w_out': nrm(ks[22], (L, D, D), D ** -0.5),
        'norm_ffn_g': 1.0 + nrm(ks[23], (L, D), 0.1),
        'w_router': nrm(ks[24], (L, D, N_EXPERTS), D ** -0.5),
        'exp_w_gate': nrm(ks[25], (L, N_EXPERTS, D, EXPERT_FF), D ** -0.5),
        'exp_w_up': nrm(ks[26], (L, N_EXPERTS, D, EXPERT_FF), D ** -0.5),
        'exp_w_down': nrm(ks[27], (L, N_EXPERTS, EXPERT_FF, D), EXPERT_FF ** -0.5),
        'norm_final_g': 1.0 + nrm(ks[28], (D,), 0.1),
    }

def first_block(x, norm_mix_g, w_in, mu_prev, mu_next, w0_f, w_up_f, w0_b, w_up_b, a0_f, a_up_f, a0_b, a_up_b,
              g_up, k_k, k_a, r_k, ln_x_w, ln_x_b, attn_sink, w_proj_rwkv, w_proj_attn, w_out, norm_ffn_g,
              w_router, exp_w_gate, exp_w_up, exp_w_down, norm_final_g):
    B, T, _ = x.shape
    for layer in range(DEPTH):
        h = rms_norm(x, norm_mix_g[layer])
        u = h @ w_in[layer]
        u_rwkv = centred_token_shift(u[..., :RWKV_COLS], mu_prev[layer], mu_next[layer])
        q, k_att, v_att, gl_rwkv, gl_attn = jnp.split(u[..., RWKV_COLS:], ATT_SPLITS, axis=-1)
        y_rwkv = rwkv7_bidir(u_rwkv, w0_f[layer], w_up_f[layer], w0_b[layer], w_up_b[layer],
                             a0_f[layer], a_up_f[layer], a0_b[layer], a_up_b[layer], g_up[layer],
                             k_k[layer], k_a[layer], r_k[layer], ln_x_w[layer], ln_x_b[layer])
        y_attn = banded_gqa_attention(q.reshape(B, T, ATT_HEADS, ATT_HEAD),
                                      k_att.reshape(B, T, ATT_KV_HEADS, ATT_HEAD),
                                      v_att.reshape(B, T, ATT_KV_HEADS, ATT_HEAD), attn_sink[layer])
        merged = (jax.nn.sigmoid(gl_rwkv) * (y_rwkv @ w_proj_rwkv[layer])
                  + jax.nn.sigmoid(gl_attn) * (y_attn @ w_proj_attn[layer]))
        x = x + merged @ w_out[layer]
        x = x + expert_choice_moe(rms_norm(x, norm_ffn_g[layer]), w_router[layer],
                                  exp_w_gate[layer], exp_w_up[layer], exp_w_down[layer])
    return rms_norm(x, norm_final_g)


MLSTM_HEADS = 4
MLSTM_HEAD_DIM = D_MODEL // MLSTM_HEADS
MLSTM_WIDTH = MLSTM_HEADS * MLSTM_HEAD_DIM
MLSTM_CONV = 4
MLSTM_CHUNK = 128

ATTN_GROUPS = ((128, 1), (512, 4), (2048, 16))
ATTN_HEADS_PER_GROUP = 8
ATTN_HEAD_DIM = 64
ATTN_N_GROUPS = len(ATTN_GROUPS)
ATTN_HEADS = ATTN_N_GROUPS * ATTN_HEADS_PER_GROUP
ATTN_WIDTH = ATTN_HEADS * ATTN_HEAD_DIM
ATTN_OUT = ATTN_HEADS_PER_GROUP * ATTN_HEAD_DIM
ATTN_BLOCK = 128

N_BUCKETS = 32
MAX_DISTANCE = 2048

D_FF = -(-8 * D_MODEL // (3 * 256)) * 256

EPS = 1e-6

IN_SIZES = (MLSTM_WIDTH, MLSTM_WIDTH, MLSTM_WIDTH, 2 * MLSTM_HEADS, MLSTM_WIDTH,
            ATTN_WIDTH, ATTN_WIDTH, ATTN_WIDTH, 2 * D_MODEL)
IN_WIDTH = sum(IN_SIZES)


def _split_points(sizes):
    pts, acc = [], 0
    for s in sizes[:-1]:
        acc += s
        pts.append(acc)
    return pts

def rmsnorm(x, g):
    xf = x.astype(jnp.float32)
    r = lax.rsqrt(jnp.mean(xf * xf, axis=-1, keepdims=True) + EPS)
    return (xf * r * g.astype(jnp.float32)).astype(x.dtype)

def rel_bucket(n):
    max_exact = N_BUCKETS // 2
    nf = jnp.maximum(n, 1).astype(jnp.float32)
    large = max_exact + (jnp.log(nf / max_exact) / math.log(MAX_DISTANCE / max_exact)
                         * (N_BUCKETS - max_exact)).astype(jnp.int32)
    large = jnp.minimum(large, N_BUCKETS - 1)
    return jnp.where(n < max_exact, n, large)

def causal_depthwise_conv(x, w, b):
    c = x.shape[-1]
    y = lax.conv_general_dilated(x, w[:, None, :].astype(x.dtype), window_strides=(1,),
                                 padding=[(MLSTM_CONV - 1, 0)],
                                 dimension_numbers=('NWC', 'WIO', 'NWC'),
                                 feature_group_count=c)
    return y + b.astype(x.dtype)

def _mlstm_chunk_step(carry, inp):
    C, n, m = carry
    q, k, v, ig, lf = inp
    L = q.shape[-2]
    b = jnp.cumsum(lf, axis=-1)
    causal = jnp.tril(jnp.ones((L, L), dtype=bool))
    dmat = jnp.where(causal, b[..., :, None] - b[..., None, :] + ig[..., None, :], -jnp.inf)
    inter = b + m[..., None]
    m_t = jnp.maximum(inter, jnp.max(dmat, axis=-1))
    w_intra = jnp.exp(dmat - m_t[..., None]) * jnp.einsum('bhtd,bhsd->bhts', q, k)
    w_inter = jnp.exp(inter - m_t)
    num = (w_inter[..., None] * jnp.einsum('bhtd,bhde->bhte', q, C)
           + jnp.einsum('bhts,bhse->bhte', w_intra, v))
    den = w_inter * jnp.einsum('bhtd,bhd->bht', q, n) + jnp.sum(w_intra, axis=-1)
    h = num / jnp.maximum(jnp.abs(den), jnp.exp(-m_t))[..., None]
    b_last = b[..., -1]
    a = b_last[..., None] - b + ig
    m_new = jnp.maximum(b_last + m, jnp.max(a, axis=-1))
    decay = jnp.exp(b_last + m - m_new)
    wk = jnp.exp(a - m_new[..., None])
    C_new = decay[..., None, None] * C + jnp.einsum('bhs,bhsd,bhse->bhde', wk, k, v)
    n_new = decay[..., None] * n + jnp.einsum('bhs,bhsd->bhd', wk, k)
    return (C_new, n_new, m_new), h

def mlstm_cell(q, k, v, ig, lf):
    B, S, H, d = q.shape
    nc = S // MLSTM_CHUNK
    to_c = lambda t: t.reshape(B, nc, MLSTM_CHUNK, H, d).transpose(1, 0, 3, 2, 4)
    to_cg = lambda t: t.reshape(B, nc, MLSTM_CHUNK, H).transpose(1, 0, 3, 2)
    init = (jnp.zeros((B, H, d, d), jnp.float32), jnp.zeros((B, H, d), jnp.float32),
            jnp.zeros((B, H), jnp.float32))
    _, hs = lax.scan(_mlstm_chunk_step, init, (to_c(q), to_c(k), to_c(v), to_cg(ig), to_cg(lf)))
    return hs.transpose(1, 0, 3, 2, 4).reshape(B, S, H, d)

def dilated_window_attention(q, k, v, bias_tab, window, dilation):
    B, S, Hg, dh = q.shape
    span = window // dilation
    blk = ATTN_BLOCK
    sd = S // dilation
    nb = -(-sd // blk)
    pad = nb * blk - sd

    def to_blocks(t):
        t = t.reshape(B, sd, dilation, Hg, dh).transpose(0, 2, 3, 1, 4)
        t = jnp.pad(t, ((0, 0), (0, 0), (0, 0), (0, pad), (0, 0)))
        return t.reshape(B, dilation, Hg, nb, blk, dh)

    def with_prev(t):
        prev = jnp.pad(t, ((0, 0), (0, 0), (0, 0), (1, 0), (0, 0), (0, 0)))[:, :, :, :-1]
        return jnp.concatenate([prev, t], axis=-2)

    qb = to_blocks(q)
    kk = with_prev(to_blocks(k))
    vv = with_prev(to_blocks(v))

    q_pos = jnp.arange(blk)[:, None] + blk
    k_pos = jnp.arange(2 * blk)[None, :]
    dist = q_pos - k_pos
    key_idx = jnp.arange(nb)[:, None, None] * blk - blk + k_pos[None]
    valid = (dist >= 0) & (dist <= span) & (key_idx >= 0)
    bias = bias_tab[rel_bucket(jnp.maximum(dist, 0) * dilation)]
    bias = jnp.moveaxis(bias, -1, 0).astype(jnp.float32)[:, None]

    s = jnp.einsum('brhnqd,brhnkd->brhnqk', qb, kk) * (dh ** -0.5) + bias
    s = jnp.where(valid, s, -jnp.inf)
    mx = jnp.max(s, axis=-1, keepdims=True)
    p = jnp.exp(s - mx)
    l = jnp.sum(p, axis=-1)
    o = jnp.einsum('brhnqk,brhnkd->brhnqd', p, vv) / l[..., None]
    lse = mx[..., 0] + jnp.log(l)

    o = o.reshape(B, dilation, Hg, nb * blk, dh)[:, :, :, :sd]
    o = o.transpose(0, 3, 1, 2, 4).reshape(B, S, Hg, dh)
    lse = lse.reshape(B, dilation, Hg, nb * blk)[:, :, :, :sd]
    lse = lse.transpose(0, 3, 1, 2).reshape(B, S, Hg)
    return o, lse

def hybrid_layer(x, rel_bias, norm_mix_g, w_in, b_gate_if, conv_w, conv_b, mlstm_norm_g,
                 w_proj_a, w_proj_b, w_out, norm_ffn_g, w_gate, w_up, w_down):
    B, S, _ = x.shape
    f32 = jnp.float32
    h = rmsnorm(x, norm_mix_g)
    proj = h @ w_in
    q_m, k_m, v_m, if_pre, o_pre, q_a, k_a, v_a, gate_pre = jnp.split(
        proj, _split_points(IN_SIZES), axis=-1)

    qk = jax.nn.silu(causal_depthwise_conv(jnp.concatenate([q_m, k_m], axis=-1), conv_w, conv_b))
    q_m, k_m = jnp.split(qk.astype(f32), 2, axis=-1)
    q_m = q_m.reshape(B, S, MLSTM_HEADS, MLSTM_HEAD_DIM) * (MLSTM_HEAD_DIM ** -0.5)
    k_m = k_m.reshape(B, S, MLSTM_HEADS, MLSTM_HEAD_DIM)
    v_m = v_m.astype(f32).reshape(B, S, MLSTM_HEADS, MLSTM_HEAD_DIM)
    if_pre = if_pre.astype(f32) + b_gate_if.astype(f32)
    ig = if_pre[..., :MLSTM_HEADS]
    lf = jax.nn.log_sigmoid(if_pre[..., MLSTM_HEADS:])
    hm = mlstm_cell(q_m, k_m, v_m, ig, lf)
    mu = jnp.mean(hm, axis=-1, keepdims=True)
    var = jnp.mean(jnp.square(hm - mu), axis=-1, keepdims=True)
    hm = (hm - mu) * lax.rsqrt(var + EPS)
    hm = hm.reshape(B, S, MLSTM_WIDTH) * mlstm_norm_g.astype(f32)
    y_a = (jax.nn.sigmoid(o_pre.astype(f32)) * hm).astype(x.dtype)

    shp = (B, S, ATTN_N_GROUPS, ATTN_HEADS_PER_GROUP, ATTN_HEAD_DIM)
    q_a = q_a.astype(f32).reshape(shp)
    k_a = k_a.astype(f32).reshape(shp)
    v_a = v_a.astype(f32).reshape(shp)
    outs, lses = [], []
    for g, (window, dilation) in enumerate(ATTN_GROUPS):
        tab = rel_bias[:, g * ATTN_HEADS_PER_GROUP:(g + 1) * ATTN_HEADS_PER_GROUP]
        o_g, lse_g = dilated_window_attention(q_a[:, :, g], k_a[:, :, g], v_a[:, :, g],
                                              tab, window, dilation)
        outs.append(o_g)
        lses.append(lse_g)
    wts = jax.nn.softmax(jnp.stack(lses, axis=0), axis=0)
    y_b = jnp.sum(wts[..., None] * jnp.stack(outs, axis=0), axis=0)
    y_b = y_b.reshape(B, S, ATTN_OUT).astype(x.dtype)

    g_a, g_b = jnp.split(jax.nn.sigmoid(gate_pre), 2, axis=-1)
    merged = g_a * (y_a @ w_proj_a) + g_b * (y_b @ w_proj_b)
    x = x + merged @ w_out

    hf = rmsnorm(x, norm_ffn_g)
    x = x + (jax.nn.silu(hf @ w_gate) * (hf @ w_up)) @ w_down
    return x

def second_inputs(seed: int = 0) -> dict:
    key = jax.random.key(seed)
    ks = jax.random.split(key, 20)
    nrm = lambda k, shape, scale: jax.random.normal(k, shape, jnp.float32) * scale
    x = jax.random.normal(ks[0], (BATCH, SEQ, D_MODEL), jnp.float32)
    norm_mix_g = 1.0 + nrm(ks[1], (DEPTH, D_MODEL), 0.02)
    w_in = nrm(ks[2], (DEPTH, D_MODEL, IN_WIDTH), D_MODEL ** -0.5)
    ig_bias = nrm(ks[3], (DEPTH, MLSTM_HEADS), 0.1)
    fg_bias = jnp.linspace(3.0, 6.0, MLSTM_HEADS, dtype=jnp.float32)[None] + nrm(ks[4], (DEPTH, MLSTM_HEADS), 0.1)
    b_gate_if = jnp.concatenate([ig_bias, fg_bias], axis=-1)
    conv_w = nrm(ks[5], (DEPTH, MLSTM_CONV, 2 * MLSTM_WIDTH), MLSTM_CONV ** -0.5)
    conv_b = nrm(ks[6], (DEPTH, 2 * MLSTM_WIDTH), 0.02)
    mlstm_norm_g = 1.0 + nrm(ks[7], (DEPTH, MLSTM_WIDTH), 0.02)
    w_proj_a = nrm(ks[8], (DEPTH, MLSTM_WIDTH, D_MODEL), MLSTM_WIDTH ** -0.5)
    w_proj_b = nrm(ks[9], (DEPTH, ATTN_OUT, D_MODEL), ATTN_OUT ** -0.5)
    w_out = nrm(ks[10], (DEPTH, D_MODEL, D_MODEL), D_MODEL ** -0.5)
    norm_ffn_g = 1.0 + nrm(ks[11], (DEPTH, D_MODEL), 0.02)
    w_gate = nrm(ks[12], (DEPTH, D_MODEL, D_FF), D_MODEL ** -0.5)
    w_up = nrm(ks[13], (DEPTH, D_MODEL, D_FF), D_MODEL ** -0.5)
    w_down = nrm(ks[14], (DEPTH, D_FF, D_MODEL), D_FF ** -0.5)
    rel_bias = nrm(ks[15], (N_BUCKETS, ATTN_HEADS), 0.5)
    norm_final_g = 1.0 + nrm(ks[16], (D_MODEL,), 0.02)
    return {"x": x, "norm_mix_g": norm_mix_g, "w_in": w_in, "b_gate_if": b_gate_if,
            "conv_w": conv_w, "conv_b": conv_b, "mlstm_norm_g": mlstm_norm_g,
            "w_proj_a": w_proj_a, "w_proj_b": w_proj_b, "w_out": w_out,
            "norm_ffn_g": norm_ffn_g, "w_gate": w_gate, "w_up": w_up, "w_down": w_down,
            "rel_bias": rel_bias, "norm_final_g": norm_final_g}

def second_block(x, norm_mix_g, w_in, b_gate_if, conv_w, conv_b, mlstm_norm_g, w_proj_a,
              w_proj_b, w_out, norm_ffn_g, w_gate, w_up, w_down, rel_bias, norm_final_g):
    for layer in range(DEPTH):
        x = hybrid_layer(x, rel_bias, norm_mix_g[layer], w_in[layer], b_gate_if[layer],
                         conv_w[layer], conv_b[layer], mlstm_norm_g[layer], w_proj_a[layer],
                         w_proj_b[layer], w_out[layer], norm_ffn_g[layer], w_gate[layer],
                         w_up[layer], w_down[layer])
    return rmsnorm(x, norm_final_g)


def setup_inputs(seed=0):
    out = dict(first_inputs(seed))
    for name, value in second_inputs(seed + 1).items():
        if name != "x":
            out[name + "_2"] = value
    return out


def reference(
    x, norm_mix_g, w_in, mu_prev, mu_next, w0_f, w_up_f, w0_b, w_up_b, a0_f, a_up_f, a0_b,
    a_up_b, g_up, k_k, k_a, r_k, ln_x_w, ln_x_b, attn_sink, w_proj_rwkv, w_proj_attn, w_out,
    norm_ffn_g, w_router, exp_w_gate, exp_w_up, exp_w_down, norm_final_g, norm_mix_g_2, w_in_2,
    b_gate_if_2, conv_w_2, conv_b_2, mlstm_norm_g_2, w_proj_a_2, w_proj_b_2, w_out_2,
    norm_ffn_g_2, w_gate_2, w_up_2, w_down_2, rel_bias_2, norm_final_g_2,
):
    x = first_block(
        x, norm_mix_g, w_in, mu_prev, mu_next, w0_f, w_up_f, w0_b, w_up_b, a0_f, a_up_f, a0_b,
        a_up_b, g_up, k_k, k_a, r_k, ln_x_w, ln_x_b, attn_sink, w_proj_rwkv, w_proj_attn, w_out,
        norm_ffn_g, w_router, exp_w_gate, exp_w_up, exp_w_down, norm_final_g,
    )
    return second_block(
        x, norm_mix_g_2, w_in_2, b_gate_if_2, conv_w_2, conv_b_2, mlstm_norm_g_2, w_proj_a_2,
        w_proj_b_2, w_out_2, norm_ffn_g_2, w_gate_2, w_up_2, w_down_2, rel_bias_2,
        norm_final_g_2,
    )


_drawn_inputs = setup_inputs


def setup_inputs(seed=0):
    import zlib

    import numpy as np

    out = dict(_drawn_inputs(seed))
    spreads = {}
    factors = {'w_up_f': 3.151,
     'w_up_b': 2.829,
     'k_k': 4.717,
     'ln_x_b': 4.686,
     'attn_sink': 6.644,
     'norm_mix_g_2': 5.207,
     'conv_b_2': 64.0,
     'mlstm_norm_g_2': 23.293,
     'norm_ffn_g_2': 10.256,
     'norm_final_g_2': 20.402}
    for name, (base, spread) in spreads.items():
        noise = np.random.default_rng([zlib.crc32(name.encode()), seed]).standard_normal(out[name].shape)
        drawn = base * np.exp(spread * noise) if base else spread * noise
        out[name] = __import__('jax').numpy.asarray(drawn.astype(out[name].dtype))
    for name, factor in factors.items():
        out[name] = (out[name] * factor).astype(out[name].dtype)
    return out
```

```python
import numpy as np
from contextlib import ExitStack

import concourse.bass as bass
from concourse import mybir

F32 = mybir.dt.float32
U32 = mybir.dt.uint32
ALU = mybir.AluOpType
ACT = mybir.ActivationFunctionType
AX = mybir.AxisListType.X

P = 128
T = 512
D = 1024
NT = T // P
KD = D // P
EPS = 1e-6

R_HEADS, R_N = 8, 64
RW = R_HEADS * R_N
RWKV_COLS = 3 * RW + 128 + 4 * 64
RC = RWKV_COLS // P
CHUNK = 64
NCH = T // CHUNK
DECAY = float(np.exp(-0.5))
LNX_EPS = 64e-5
A_HEADS, A_DH = 8, 64
N_EXP, CAP, FF1 = 16, 64, 1024

M_HEADS, M_DH = 4, 256
G2_HEADS = 8
WINDOWS = ((128, 1), (512, 4), (2048, 16))
Q_M, K_M, V_M, IF_M = 0, 1024, 2048, 3072
O_M = IF_M + 2 * M_HEADS
Q_A = O_M + 1024
K_A = Q_A + 1536
V_A = K_A + 1536
G_A = V_A + 1536
FF2 = 2816

RING = 4
SLOT = KD * 512


class Ring:

    def __init__(self, nc, ctx):
        self.buf = ctx.enter_context(nc.sbuf_tensor("ring", [P, RING, SLOT], F32))
        self.full = [ctx.enter_context(nc.semaphore(f"ring_full{i}")) for i in range(RING)]
        self.loads = []
        self.issued = 0
        self.used = {}

    def plan(self, src, k, w):
        self.loads.append((src, k, w))
        return len(self.loads) - 1

    def tile(self, n):
        _, k, w = self.loads[n]
        return self.buf[:, n % RING, 0:k * w].rearrange("p (k w) -> p k w", k=k)

    def load(self, eng, upto, more=False):
        for n in range(self.issued, min(upto, len(self.loads))):
            if n - RING in self.used:
                eng.wait_ge(*self.used[n - RING])
            src, k, w = self.loads[n]
            eng.dma_start(self.tile(n), src.rearrange("(k p) w -> p k w", p=P)).then_inc(self.full[n % RING], 16)
            self.issued = n + 1
        if not more:
            self.used = {}

    def wait(self, pe, n):
        pe.wait_ge(self.full[n % RING], 16 * (n // RING + 1))


def sems(nc, ctx, names, tag=""):
    made = {n: nc.alloc_semaphore(name=n + tag) for n in names.split()}

    def clear():
        for handle in made.values():
            nc.gpsimd.sem_clear(handle)
            nc.release_semaphore(handle)
    ctx.callback(clear)
    return made


class Buffers:
    pass


def linker(eng, sem):
    count = [0]

    def link(ins):
        count[0] += 1
        ins.then_inc(sem, 1)
        eng.wait_ge(sem, count[0])
    return link


def norm_transposed(nc, K, tag, x, g, xn, hT, x_src=None, load_upto=0):
    with ExitStack() as ctx:
        S = sems(nc, ctx, "x_in g_in squared var_ok root_ok rec_ok xn_ok turned emptied", tag)
        sq = ctx.enter_context(nc.sbuf_tensor("sq" + tag, [P, D], F32))
        ss = ctx.enter_context(nc.sbuf_tensor("ss" + tag, [P, 4 * NT], F32))
        gc = ctx.enter_context(nc.sbuf_tensor("gc" + tag, [P, KD], F32))
        block = ctx.enter_context(nc.Block())

        @block.sync
        def _(sp):
            if x_src is not None:
                for t in range(NT):
                    sp.dma_start(x[:, t, :], x_src[t * P:(t + 1) * P, :]).then_inc(S["x_in"], 16)
            with nc.allow_non_contiguous_dma(reason="one gain per partition"):
                sp.dma_start(gc[:, :], g.rearrange("(k p) -> p k", p=P)).then_inc(S["g_in"], 16)
            K.ring.load(sp, load_upto)
            sp.wait_ge(S["g_in"], 16)

        @block.scalar
        def _(act):
            if x_src is not None:
                act.wait_ge(S["x_in"], 16 * NT)
            for t in range(NT):
                if t:
                    act.wait_ge(S["squared"], t)
                nc.scalar.activation(sq[:, :], x[:, t, :], ACT.Square, accum_out=ss[:, t:t + 1]).then_inc(S["squared"], 1)
            act.wait_ge(S["var_ok"], 1)
            nc.scalar.activation(ss[:, 2 * NT:3 * NT], ss[:, NT:2 * NT], ACT.Sqrt).then_inc(S["root_ok"], 1)
            act.wait_ge(S["rec_ok"], 1)
            for t in range(NT):
                nc.scalar.activation(xn[:, t, :], x[:, t, :], ACT.Copy, scale=ss[:, 3 * NT + t:3 * NT + t + 1]).then_inc(S["xn_ok"], 1)

        @block.vector
        def _(dve):
            dve.wait_ge(S["squared"], NT)
            dve.tensor_scalar(ss[:, NT:2 * NT], ss[:, 0:NT], 1.0 / D, EPS, ALU.mult, ALU.add).then_inc(S["var_ok"], 1)
            dve.wait_ge(S["root_ok"], 1)
            dve.reciprocal(ss[:, 3 * NT:4 * NT], ss[:, 2 * NT:3 * NT]).then_inc(S["rec_ok"], 1)
            dve.wait_ge(S["g_in"], 16)
            for b in range(NT * 2):
                t, half = b // 2, b % 2
                dve.wait_ge(S["turned"], b + 1)
                for c in range(4):
                    k = half * 4 + c
                    last = dve.tensor_scalar(hT[:, k, t * P:(t + 1) * P], K.ps[b % 4][:, c * P:(c + 1) * P],
                                             gc[:, k:k + 1], None, ALU.mult)
                last.then_inc(S["emptied"], 1)

        @block.tensor
        def _(pe):
            for b in range(NT * 2):
                t, half = b // 2, b % 2
                pe.wait_ge(S["xn_ok"], t + 1)
                if b >= 4:
                    pe.wait_ge(S["emptied"], b - 3)
                for c in range(4):
                    k = half * 4 + c
                    last = pe.transpose(K.ps[b % 4][:, c * P:(c + 1) * P], xn[:, t, k * P:(k + 1) * P], K.ident[:, :])
                last.then_inc(S["turned"], 1)


def mm_feature(pe, ps, w, cols, hT, nk, k0=0):
    for k in range(nk):
        last = pe.matmul(ps, w[:, k, cols], hT[:, k0 + k, :], start=(k == 0), stop=(k == nk - 1))
    return last


def attention(nc, K, tag, items, out, width, outT, flips=None):
    with ExitStack() as ctx:
        S = sems(nc, ctx, "scored biased maxed exped turned copied pved y_done chain o_turned o_copied flip_in0 flip_in1 flipped unflipped", tag)
        scored, biased, maxed, exped, turned = S["scored"], S["biased"], S["maxed"], S["exped"], S["turned"]
        copied, pved, y_done, chain, o_turned = S["copied"], S["pved"], S["y_done"], S["chain"], S["o_turned"]
        sbt = lambda n, s: ctx.enter_context(nc.sbuf_tensor(n + tag, s, F32))
        SB = 3 if flips is None else 2
        Sb = sbt("Sb", [P, SB, width])
        PT = sbt("PT", [P, 2, width])
        N = len(items)
        nm, mx, den, rd, esk = (sbt(n, [P, N]) for n in ("anm", "amx", "aden", "ard", "aesk"))
        seg0, bank0 = [0], [0]
        for it in items:
            seg0.append(seg0[-1] + len(it["segs"]))
            bank0.append(bank0[-1] + -(-len(it["values"]) // 4))
        ps_s, ps_f, ps_t, ps_v = K.ps[0:3], K.ps[3], K.ps[4:6], K.ps[6:8]
        flip_segs = ((0, 256), (256, 512), (768, 512))
        block = ctx.enter_context(nc.Block())
        nout = out.shape[2] // P

        def key_blocks(i, b):
            return range(4 * b, min(4 * b + 4, len(items[i]["values"])))

        @block.sync
        def _(sp):
            if flips is None:
                return
            for h in range(G2_HEADS):
                if h >= 2:
                    sp.wait_ge(biased, seg0[NT * (h - 1)])
                for g, (c0, w) in enumerate(flip_segs):
                    base = K.R_dram[g, h:h + 1, 512 - w:512]
                    src = bass.AP(tensor=base.tensor, offset=base.offset, ap=[[1, P], [1, w]])
                    sp.dma_start(flips[:, h % 2, c0:c0 + w], src).then_inc((S["flip_in0"], S["flip_in1"])[h % 2], 16)

        @block.tensor
        def _(pe):
            def flip(h, g):
                pe.wait_ge((S["flip_in0"], S["flip_in1"])[h % 2], 48 * (h // 2 + 1))
                if h or g:
                    pe.wait_ge(S["unflipped"], 3 * h + g)
                c0, w = flip_segs[g]
                pe.matmul(ps_f[:, 0:w], K.flip[:, :], flips[:, h % 2, c0:c0 + w], start=True, stop=True).then_inc(S["flipped"], 1)

            if flips is not None:
                for g in range(3):
                    flip(0, g)
            for i in range(N + 2):
                if i < N:
                    for j, (q, k, w, _, _) in enumerate(items[i]["segs"]):
                        g = seg0[i] + j
                        if g >= 3:
                            pe.wait_ge(biased, g - 2)
                        pe.matmul(ps_s[g % 3][:, 0:w], q, k, start=True, stop=True).then_inc(scored, 1)
                if flips is not None and i % NT and i // NT + 1 < G2_HEADS:
                    flip(i // NT + 1, i % NT - 1)
                if 1 <= i <= N:
                    pe.wait_ge(exped, i)
                    for b in range(bank0[i] - bank0[i - 1]):
                        g = bank0[i - 1] + b
                        if g >= 2:
                            pe.wait_ge(copied, g - 1)
                        for n, kb in enumerate(key_blocks(i - 1, b)):
                            last = pe.transpose(ps_t[g % 2][:, n * P:(n + 1) * P],
                                                Sb[:, (i - 1) % SB, kb * P:(kb + 1) * P], K.ident[:, :])
                        last.then_inc(turned, 1)
                if i >= 2:
                    j = i - 2
                    pe.wait_ge(copied, bank0[j + 1])
                    if j >= 2:
                        pe.wait_ge(y_done, j - 1)
                    vs = items[j]["values"]
                    for kb, v in enumerate(vs):
                        last = pe.matmul(ps_v[j % 2][:, 0:64], PT[:, j % 2, kb * P:(kb + 1) * P], v,
                                         start=(kb == 0), stop=(kb == len(vs) - 1))
                    last.then_inc(pved, 1)
            pe.wait_ge(y_done, N)
            for c in range(nout):
                if c >= 3:
                    pe.wait_ge(S["o_copied"], c - 2)
                for t in range(NT):
                    last = pe.transpose(ps_s[c % 3][:, t * P:(t + 1) * P], out[:, t, c * P:(c + 1) * P], K.ident[:, :])
                last.then_inc(o_turned, 1)

        @block.scalar
        def _(act):
            def unflip(h, g):
                act.wait_ge(S["flipped"], 3 * h + g + 1)
                c0, w = flip_segs[g]
                nc.scalar.activation(flips[:, h % 2, c0:c0 + w], ps_f[:, 0:w], ACT.Copy).then_inc(S["unflipped"], 1)

            if flips is not None:
                for g in range(3):
                    unflip(0, g)
            for i in range(N + 1):
                if flips is not None and i % NT and i // NT + 1 < G2_HEADS:
                    unflip(i // NT + 1, i % NT - 1)
                if i < N:
                    w = sum(s[2] for s in items[i]["segs"])
                    act.wait_ge(maxed, i + 1)
                    last = nc.scalar.activation(Sb[:, i % SB, 0:w], Sb[:, i % SB, 0:w], ACT.Exp,
                                                bias=nm[:, i:i + 1], accum_out=den[:, i:i + 1])
                    if items[i]["sink"] is not None:
                        last = nc.scalar.activation(esk[:, i:i + 1], nm[:, i:i + 1], ACT.Exp, bias=items[i]["sink"])
                    last.then_inc(exped, 1)
                if i >= 1:
                    j = i - 1
                    if j >= 2:
                        act.wait_ge(pved, j - 1)
                    for b in range(bank0[j + 1] - bank0[j]):
                        g = bank0[j] + b
                        act.wait_ge(turned, g + 1)
                        kb = key_blocks(j, b)
                        nc.scalar.activation(PT[:, j % 2, kb[0] * P:(kb[-1] + 1) * P],
                                             ps_t[g % 2][:, 0:len(kb) * P], ACT.Copy).then_inc(copied, 1)
            for c in range(nout):
                act.wait_ge(o_turned, c + 1)
                nc.scalar.activation(outT[:, c, :], ps_s[c % 3][:, :], ACT.Copy).then_inc(S["o_copied"], 1)

        @block.vector
        def _(dve):
            link = linker(dve, chain)
            for i in range(N + 2):
                if i < N:
                    if flips is not None:
                        dve.wait_ge(S["unflipped"], 3 * (i // NT + 1))
                    if i >= SB:
                        dve.wait_ge(turned, bank0[i - SB + 1])
                    c0 = 0
                    for j, (q, k, w, bias, scale) in enumerate(items[i]["segs"]):
                        g = seg0[i] + j
                        dve.wait_ge(scored, g + 1)
                        o = Sb[:, i % SB, c0:c0 + w]
                        dve.scalar_tensor_tensor(out=o, in0=bias, scalar=scale, in1=ps_s[g % 3][:, 0:w],
                                                 op0=ALU.mult, op1=ALU.add).then_inc(biased, 1)
                        c0 += w
                    dve.wait_ge(biased, seg0[i + 1])
                    if items[i]["sink"] is not None:
                        link(dve.tensor_reduce(mx[:, i:i + 1], Sb[:, i % SB, 0:c0], AX, ALU.max))
                        dve.tensor_scalar(nm[:, i:i + 1], mx[:, i:i + 1], items[i]["sink"], -1.0,
                                          ALU.max, ALU.mult).then_inc(maxed, 1)
                    else:
                        dve.tensor_reduce(nm[:, i:i + 1], Sb[:, i % SB, 0:c0], AX, ALU.max, negate=True).then_inc(maxed, 1)
                if i >= 2:
                    j = i - 2
                    dve.wait_ge(exped, j + 1)
                    d = den[:, j:j + 1]
                    if items[j]["sink"] is not None:
                        link(dve.tensor_tensor(esk[:, j:j + 1], esk[:, j:j + 1], d, ALU.add))
                        d = esk[:, j:j + 1]
                    link(dve.reciprocal(rd[:, j:j + 1], d))
                    dve.wait_ge(pved, j + 1)
                    dve.tensor_scalar(items[j]["at"], ps_v[j % 2][:, 0:64], rd[:, j:j + 1], None,
                                      ALU.mult).then_inc(y_done, 1)


def first_projection(nc, K, first):
    I = K.I
    nch = 21
    with ExitStack() as ctx:
        S = sems(nc, ctx, "bmm bmu bc0 bscaled bprev bevac")
        mu = ctx.enter_context(nc.sbuf_tensor("mu", [P, 3, RC], F32))
        K.ring.used = {first + i: (S["bmm"], min(4 * i + 4, nch)) for i in range(6)}
        block = ctx.enter_context(nc.Block())

        @block.sync
        def _(sp):
            with nc.allow_non_contiguous_dma(reason="one mixing weight per partition"):
                sp.dma_start(mu[:, 0, :], I["mu_prev"][0].rearrange("(c p) -> p c", p=P)).then_inc(S["bmu"], 16)
                sp.dma_start(mu[:, 1, :], I["mu_next"][0].rearrange("(c p) -> p c", p=P)).then_inc(S["bmu"], 16)
                sp.dma_start(K.sink[:, :], I["attn_sink"].to_broadcast([P, A_HEADS])).then_inc(S["bmu"], 16)
            K.ring.load(sp, first + 6 + RING)
            sp.wait_ge(S["bmu"], 48)

        @block.tensor
        def _(pe):
            for c in range(nch):
                n = first + c // 4
                if c % 4 == 0:
                    K.ring.wait(pe, n)
                if c >= 4:
                    pe.wait_ge(S["bevac"] if c - 4 < RC else S["bscaled"], c - 3)
                w = K.ring.tile(n)
                ps = K.ps[c % 4]
                cw = (c % 4) * P
                if c < 19:
                    last = mm_feature(pe, ps[:, :], w, slice(cw, cw + P), K.hT, KD)
                elif c == 19:
                    ps = K.ps[4:6]
                    for g in range(2):
                        for half in range(2):
                            last = mm_feature(pe, ps[g][64 * half:64 * half + 64, :], w,
                                              slice(cw + 64 * g, cw + 64 * g + 64), K.hT, KD)
                else:
                    for t in range(NT):
                        for k in range(KD):
                            last = pe.matmul(ps[:, t * P:(t + 1) * P], K.hT[:, k, t * P:(t + 1) * P], w[:, k, 0:P],
                                             start=(k == 0), stop=(k == KD - 1))
                last.then_inc(S["bmm"], 1)

        @block.scalar
        def _(act):
            act.wait_ge(S["bc0"], 2)
            for c in range(nch):
                act.wait_ge(S["bmm"], c + 1)
                ps = K.ps[c % 4]
                if c < RC:
                    nc.scalar.activation(K.u[:, c, :], ps[:, :], ACT.Copy, scale=mu[:, 2, c:c + 1]).then_inc(S["bscaled"], 1)
                elif c < 19:
                    nc.scalar.activation(K.qT[:, c - RC, :], ps[:, :], ACT.Copy, scale=A_DH ** -0.5).then_inc(S["bscaled"], 1)
                elif c == 19:
                    nc.scalar.activation(K.kT[:, 0, :], K.ps[4][:, :], ACT.Copy)
                    nc.scalar.activation(K.kT[:, 1, :], K.ps[5][:, :], ACT.Copy).then_inc(S["bscaled"], 1)
                else:
                    nc.scalar.activation(K.va[:, :, :], ps[:, :].rearrange("p (t d) -> p t d", t=NT), ACT.Copy).then_inc(S["bscaled"], 1)

        @block.vector
        def _(dve):
            dve.wait_ge(S["bmu"], 48)
            dve.tensor_tensor(mu[:, 2, :], mu[:, 0, :], mu[:, 1, :], ALU.add).then_inc(S["bc0"], 1)
            dve.wait_ge(S["bc0"], 1)
            dve.tensor_scalar(mu[:, 2, :], mu[:, 2, :], -1.0, 1.0, ALU.mult, ALU.add).then_inc(S["bc0"], 1)
            for c in range(RC):
                dve.wait_ge(S["bscaled"], c + 1)
                u, ps = K.u[:, c, :], K.ps[c % 4]
                dve.scalar_tensor_tensor(out=u[:, 1:T], in0=ps[:, 0:T - 1], scalar=mu[:, 0, c:c + 1], in1=u[:, 1:T],
                                         op0=ALU.mult, op1=ALU.add).then_inc(S["bprev"], 1)
                dve.wait_ge(S["bprev"], c + 1)
                dve.scalar_tensor_tensor(out=u[:, 0:T - 1], in0=ps[:, 1:T], scalar=mu[:, 1, c:c + 1],
                                         in1=u[:, 0:T - 1], op0=ALU.mult, op1=ALU.add).then_inc(S["bevac"], 1)


def rwkv_setup(nc, K):
    I = K.I
    with ExitStack() as ctx:
        S = sems(nc, ctx, "rpar rth")
        block = ctx.enter_context(nc.Block())
        cols = "w0_f w0_b a0_f a0_b k_k k_a k_a r_k ln_x_w ln_x_b".split()

        @block.sync
        def _(sp):
            n = 0
            with nc.allow_non_contiguous_dma(reason="one parameter per partition"):
                for j, name in enumerate(cols):
                    src = I[name][0] if name != "r_k" else I[name][0].rearrange("h n -> (h n)")
                    sp.dma_start(K.par[:, j, :], src.rearrange("(c p) -> p c", p=P)).then_inc(S["rpar"], 16)
            for dst, src in ((K.wup[0:64, :], I["w_up_f"][0]), (K.wup[64:128, :], I["w_up_b"][0]),
                             (K.aup[0:64, :], I["a_up_f"][0]), (K.aup[64:128, :], I["a_up_b"][0]),
                             (K.gup[:, :], I["g_up"][0]), (K.masks[:, :, :, :], I["c_masks"]),
                             (K.masks_t[:, :, :], I["c_masks_t"]), (K.heads1[:, :], I["c_heads1"]),
                             (K.chunk0[:, :], I["c_chunk0"])):
                sp.dma_start(dst, src).then_inc(S["rpar"], 16)
            sp.wait_ge(S["rpar"], 16 * (len(cols) + 9))

        @block.scalar
        def _(act):
            nc.scalar.activation(K.u[:, 13, :], K.u[:, 13, :], ACT.Tanh)
            nc.scalar.activation(K.u[:, 12, :], K.u[:, 12, :], ACT.Sigmoid)

        @block.vector
        def _(dve):
            dve.wait_ge(S["rpar"], 16 * (len(cols) + 9))
            dve.tensor_scalar(K.par[:, 6, :], K.par[:, 5, :], -1.0, 1.0, ALU.mult, ALU.add)


W0, A0, GAIN_KK, GAIN_KA, GAIN_K1, GAIN_RK, LN_W, LN_B = 0, 2, 4, 5, 6, 7, 8, 9


def rwkv_keys(nc, K, hf):
    tag = f"k{hf}"
    with ExitStack() as ctx:
        S = sems(nc, ctx, "scaled squared summed rooted turned kl", tag)
        block = ctx.enter_context(nc.Block())
        raw, sq = K.tmp[0], K.tmp[1]
        uf = K.u[:, :, :].rearrange("p c t -> p (c t)")

        @block.vector
        def _(dve):
            for c in range(2):
                cp = 2 * hf + c
                dve.tensor_scalar(raw[:, c, :], K.u[:, 4 + cp, :], K.par[:, GAIN_KK, cp:cp + 1], None, ALU.mult).then_inc(S["scaled"], 1)
            link = linker(dve, S["kl"])
            for c in range(2):
                dve.wait_ge(S["rooted"], c + 1)
                link(dve.tensor_scalar(sq[:, c, :], sq[:, c, :], 1e-12, None, ALU.max))
                link(dve.reciprocal(sq[:, c, :], sq[:, c, :]))
                dve.tensor_tensor(K.kk[:, c, :], raw[:, c, :], sq[:, c, :], ALU.mult)

        @block.scalar
        def _(act):
            for c in range(2):
                act.wait_ge(S["scaled"], c + 1)
                nc.scalar.activation(sq[:, c, :], raw[:, c, :], ACT.Square).then_inc(S["squared"], 1)
            for c in range(2):
                act.wait_ge(S["summed"], c + 1)
                nc.scalar.activation(sq[:, c, :], K.ps[c][:, :], ACT.Sqrt).then_inc(S["rooted"], 1)
            for b in range(6):
                c, q = b // 3, 4 * (b % 3)
                act.wait_ge(S["turned"], b + 1)
                ps = K.ps[2 + b].rearrange("p (w f) -> p w f", f=P)
                if q < NCH:
                    nc.scalar.activation(K.SV[64:128, q:q + 4, c, 0, :], ps[64:128, :, 0:64], ACT.Copy)
                lo, hi = max(q, 1), min(q + 4, NCH + 1)
                nc.scalar.activation(K.SV[0:64, lo - 1:hi - 1, c, 1, :], ps[0:64, lo - q:hi - q, 64:128], ACT.Copy)

        @block.tensor
        def _(pe):
            for b in range(6):
                c, q = b // 3, 4 * (b % 3)
                for w in range(q, min(q + 4, NCH + 1)):
                    t0 = (8 + 2 * hf + c) * T + 64 * w - 64
                    last = pe.transpose(K.ps[2 + b][:, (w - q) * P:(w - q + 1) * P], uf[:, t0:t0 + P], K.ident[:, :])
                last.then_inc(S["turned"], 1)
            for c in range(2):
                pe.wait_ge(S["squared"], c + 1)
                pe.matmul(K.ps[c][:, :], K.heads1[:, :], sq[:, c, :], start=True, stop=True).then_inc(S["summed"], 1)


def rwkv_decays(nc, K, hf, d):
    tag = f"d{hf}{d}"
    with ExitStack() as ctx:
        S = sems(nc, ctx, "lora gated sums expd dl", tag)
        block = ctx.enter_context(nc.Block())
        sg, cs, a, e1 = K.tmp
        rows = slice(64 * d, 64 * d + 64)
        v4 = lambda t: t[:, :, :].rearrange("p c (n s) -> p c n s", s=CHUNK)
        first = lambda t: K.AR[:, :, :, t, :]
        r, k = K.u[:, 2 * hf:2 * hf + 2, :], K.u[:, 4 + 2 * hf:6 + 2 * hf, :]

        @block.tensor
        def _(pe):
            for c in range(2):
                f = slice((2 * hf + c) * P, (2 * hf + c + 1) * P)
                pe.matmul(K.ps[c][:, :], K.wup[rows, f], K.u[rows, 13, :], start=True, stop=True).then_inc(S["lora"], 1)
                pe.matmul(K.ps[2 + c][:, :], K.aup[rows, f], K.u[rows, 14, :], start=True, stop=True).then_inc(S["lora"], 1)

        @block.scalar
        def _(act):
            for c in range(2):
                cp = 2 * hf + c
                act.wait_ge(S["lora"], 2 * c + 2)
                nc.scalar.activation(sg[:, c, :], K.ps[c][:, :], ACT.Sigmoid, bias=K.par[:, W0 + d, cp:cp + 1]).then_inc(S["gated"], 1)
                nc.scalar.activation(a[:, c, :], K.ps[2 + c][:, :], ACT.Sigmoid, bias=K.par[:, A0 + d, cp:cp + 1]).then_inc(S["gated"], 1)
            act.wait_ge(S["sums"], 1)
            e2 = cs if d == 0 else sg
            last = CHUNK - 1 if d == 0 else 0
            for c in range(2):
                nc.scalar.activation(K.AR[:, c, :, 0, :], v4(e1)[:, c], ACT.Exp, scale=-DECAY)
                nc.scalar.activation(K.AR[:, c, :, 1, :], v4(e2)[:, c], ACT.Exp, scale=-DECAY)
                nc.scalar.activation(K.BK[:, c, :, 0, :], v4(e2)[:, c], ACT.Exp, scale=DECAY)
                nc.scalar.activation(K.BK[:, c, :, 1, :], v4(e2)[:, c], ACT.Exp, scale=DECAY).then_inc(S["expd"], 1)
                nc.scalar.activation(K.DC[:, c, :], v4(e2)[:, c, :, last], ACT.Exp, scale=-DECAY)

        @block.vector
        def _(dve):
            link = linker(dve, S["dl"])
            for c in range(2):
                dve.wait_ge(S["gated"], 2 * c + 1)
                link(dve.tensor_tensor_scan(cs[:, c, :], K.chunk0[:, :], sg[:, c, :], 0.0, ALU.mult, ALU.add))
            if d == 0:
                dve.tensor_tensor(e1[:, :, :], cs[:, :, :], sg[:, :, :], ALU.subtract).then_inc(S["sums"], 1)
            else:
                for c in range(2):
                    link(dve.tensor_tensor(v4(e1)[:, c], v4(cs)[:, c, :, CHUNK - 1:CHUNK].to_broadcast([P, NCH, CHUNK]),
                                           v4(cs)[:, c], ALU.subtract))
                dve.tensor_tensor(sg[:, :, :], e1[:, :, :], sg[:, :, :], ALU.add).then_inc(S["sums"], 1)
            dve.wait_ge(S["gated"], 4)
            dve.wait_ge(S["sums"], 1)
            ak = cs if d == 1 else sg
            link(dve.tensor_tensor(ak[:, :, :], a[:, :, :], K.kk[:, :, :], ALU.mult))
            for c in range(2):
                cp = 2 * hf + c
                link(dve.tensor_scalar(a[:, c, :], a[:, c, :], K.par[:, GAIN_KA, cp:cp + 1], K.par[:, GAIN_K1, cp:cp + 1],
                                       ALU.mult, ALU.add))
            link(dve.tensor_tensor(a[:, :, :], a[:, :, :], k, ALU.mult))
            if d == 0:
                link(dve.tensor_copy(K.ksum[:, :, :], a[:, :, :]))
            else:
                link(dve.tensor_tensor(K.ksum[:, :, :], K.ksum[:, :, :], a[:, :, :], ALU.add))
            for c in range(2):
                dve.wait_ge(S["expd"], c + 1)
                v3 = lambda t: t.rearrange("p (n s) -> p n s", s=CHUNK)
                dve.tensor_tensor(K.AR[:, c, :, 0, :], K.AR[:, c, :, 0, :], v4(K.kk)[:, c], ALU.mult)
                dve.tensor_tensor(K.AR[:, c, :, 1, :], K.AR[:, c, :, 1, :], v3(r[:, c, :]), ALU.mult)
                for par in range(2):
                    rows = slice(64 * par, 64 * par + 64)
                    for j, factor in ((par, ak), (1 - par, a)):
                        o = K.BK[rows, c, :, j, :]
                        dve.tensor_tensor(o, o, v4(factor)[rows, c], ALU.mult)


def rwkv_chunks(nc, K, hf, d):
    tag = f"c{hf}{d}"
    names = ("products masked bk_turned powered0 powered1 p_copied0 p_copied1 x_added0 x_added1 r_ready r_copied n_ready "
             "n_copied state_mm state_ok y_copied cl")
    ROUNDS = 6
    with ExitStack() as ctx:
        S = sems(nc, ctx, names, tag)
        powered, p_copied, x_added = ([S[n + "0"], S[n + "1"]] for n in ("powered", "p_copied", "x_added"))
        sbt = lambda n, s: ctx.enter_context(nc.sbuf_tensor(n + tag, s, F32))
        M = sbt("M", [P, 2, 2, 2, P])
        PB, PT = sbt("PB", [P, 2, 2, P]), sbt("PT", [P, 2, 2, P])
        X = sbt("X", [P, 2, 2, 64])
        XF = sbt("XF", [P, 2, 2, P])
        BKT = sbt("BKT", [P, 2, 2, P])
        RH = sbt("RH", [P, 2, 64])
        ST = sbt("ST", [P, 2, 64])
        block = ctx.enter_context(nc.Block())
        psM, psP, psQ, psC, psN = K.ps[0:2], K.ps[2:4], K.ps[4:6], K.ps[6], K.ps[7]
        MT, BT, R_, Y_, U_ = 256, 256, 0, 128, 256
        chunk = lambda s: s if d == 0 else NCH - 1 - s
        pair = lambda t, w: t.rearrange("p (c w) -> p c w", w=w)
        halves = ((0, slice(0, 64)), (1, slice(64, 128)))

        @block.tensor
        def _(pe):
            def products(s):
                ch, q = chunk(s), s % 2
                if s:
                    pe.wait_ge(S["masked"], s)
                if s >= 2:
                    pe.wait_ge(p_copied[q], 5 * (s // 2))
                for c in range(2):
                    for par, rows in halves:
                        pe.matmul(psM[par][:, c * P:(c + 1) * P], K.BK[rows, c, ch, :, :], K.AR[rows, c, ch, :, :],
                                  start=True, stop=True)
                for c in range(2):
                    for par, rows in halves:
                        pe.matmul(psM[par][rows, MT + c * 64:MT + c * 64 + 64], K.AR[rows, c, ch, 0, :],
                                  K.BK[rows, c, ch, par, :], start=True, stop=True)
                for c in range(2):
                    last = pe.transpose(psQ[q][:, BT + c * P:BT + (c + 1) * P], K.BK[:, c, ch, :, :], K.ident[:, :])
                last.then_inc(S["products"], 1)

            def power(s, r):
                q, n = s % 2, s // 2
                if r == 0:
                    pe.wait_ge(S["masked"], s + 1)
                    pe.wait_ge(S["bk_turned"], s + 1)
                if n or r:
                    pe.wait_ge(p_copied[q], 5 * n + r)
                    pe.wait_ge(x_added[q], 6 * n + r)
                for c in range(2):
                    o = psP[q][:, c * 192:c * 192 + 192]
                    if r < ROUNDS - 1:
                        last = pe.matmul(o[:, 0:P], PT[:, q, c, :], PB[:, q, c, :], start=True, stop=True)
                        last = pe.matmul(psQ[q][:, c * P:(c + 1) * P], PB[:, q, c, :], PT[:, q, c, :], start=True, stop=True)
                    if r:
                        last = pe.matmul(o[:, P:192], PT[:, q, c, :], X[:, q, c, :], start=True, stop=True)
                last.then_inc(powered[q], 1)

            def solve_in(s):
                ch, q = chunk(s), s % 2
                pe.wait_ge(S["masked"], s + 1)
                pe.wait_ge(S["state_ok"], s + 1)
                if s:
                    pe.wait_ge(S["y_copied"], s)
                for c in range(2):
                    for par, rows in halves:
                        o = psC[rows, R_ + c * 64:R_ + c * 64 + 64]
                        pe.matmul(o, M[:, q, c, par, 0:64], K.SV[:, ch, c, par, :], start=True, stop=False)
                        last = pe.matmul(o, K.AR[rows, c, ch, 0, :], ST[rows, c, :], start=False, stop=True)
                last.then_inc(S["r_ready"], 1)

            def solve(s):
                q = s % 2
                pe.wait_ge(S["r_copied"], s + 1)
                pe.wait_ge(x_added[q], 6 * (s // 2 + 1))
                for c in range(2):
                    last = pe.matmul(psN[:, c * 64:c * 64 + 64], XF[:, q, c, :], RH[:, c, :], start=True, stop=True)
                last.then_inc(S["n_ready"], 1)

            def finish(s):
                ch, q = chunk(s), s % 2
                pe.wait_ge(S["n_copied"], s + 1)
                for c in range(2):
                    for par, rows in halves:
                        o = psC[rows, Y_ + c * 64:Y_ + c * 64 + 64]
                        pe.matmul(o, M[:, q, c, par, 64:128], K.SV[:, ch, c, par, :], start=True, stop=False)
                        pe.matmul(o, K.AR[rows, c, ch, 1, :], ST[rows, c, :], start=False, stop=True)
                for c in range(2):
                    for par, rows in halves:
                        last = pe.matmul(psC[rows, U_ + c * 64:U_ + c * 64 + 64], BKT[:, q, c, rows],
                                         K.SV[:, ch, c, par, :], start=True, stop=True)
                last.then_inc(S["state_mm"], 1)

            products(0)
            products(1)
            for r in range(ROUNDS):
                power(0, r)
                power(1, r)
            for s in range(0, NCH, 2):
                more = s + 2 < NCH
                solve_in(s)
                solve(s)
                finish(s)
                if more:
                    products(s + 2)
                    power(s + 2, 0)
                solve_in(s + 1)
                if more:
                    power(s + 2, 1)
                solve(s + 1)
                if more:
                    power(s + 2, 2)
                finish(s + 1)
                if more:
                    products(s + 3)
                    for r in range(ROUNDS):
                        if r + 3 < ROUNDS:
                            power(s + 2, r + 3)
                        power(s + 3, r)

        @block.scalar
        def _(act):
            def turn(s):
                act.wait_ge(S["products"], s + 1)
                if s >= 2:
                    act.wait_ge(S["state_mm"], s - 1)
                nc.scalar.activation(BKT[:, s % 2, :, :], pair(psQ[s % 2][:, BT:BT + 256], P), ACT.Copy).then_inc(S["bk_turned"], 1)

            def copy_transposes(s, r):
                q = s % 2
                act.wait_ge(powered[q], 6 * (s // 2) + r + 1)
                nc.scalar.activation(PT[:, q, :, :], pair(psQ[q][:, 0:256], P), ACT.Copy).then_inc(p_copied[q], 1)

            def negate(s):
                act.wait_ge(S["r_ready"], s + 1)
                nc.scalar.activation(RH[:, :, :], pair(psC[:, R_:R_ + 128], 64), ACT.Copy, scale=-1.0).then_inc(S["r_copied"], 1)

            turn(0)
            turn(1)
            for r in range(ROUNDS - 1):
                copy_transposes(0, r)
                copy_transposes(1, r)
            for s in range(0, NCH, 2):
                more = s + 2 < NCH
                negate(s)
                if more:
                    turn(s + 2)
                    copy_transposes(s + 2, 0)
                negate(s + 1)
                if more:
                    copy_transposes(s + 2, 1)
                    copy_transposes(s + 2, 2)
                    turn(s + 3)
                    for r in range(ROUNDS - 1):
                        if r + 3 < ROUNDS - 1:
                            copy_transposes(s + 2, r + 3)
                        copy_transposes(s + 3, r)

        @block.vector
        def _(dve):
            link = linker(dve, S["cl"])
            dve.memset(PT[:, :, :, :], 0.0)
            dve.memset(PB[:, :, :, :], 0.0)
            dve.memset(XF[:, :, :, :], 0.0)
            for par, rows in halves:
                last = dve.memset(K.SV[rows, :, :, par, :], 0.0)
            link(last)
            dve.memset(ST[:, :, :], 0.0).then_inc(S["state_ok"], 1)

            def mask(s):
                q = s % 2
                dve.wait_ge(S["products"], s + 1)
                if s >= 2:
                    dve.wait_ge(S["state_mm"], s - 1)
                    dve.wait_ge(x_added[q], 6 * (s // 2))
                for par, rows in halves:
                    dve.tensor_tensor(PT[rows, q, :, rows], pair(psM[par][rows, MT:MT + 128], 64),
                                      K.masks_t[rows, d, :].unsqueeze(1).to_broadcast([64, 2, 64]), ALU.mult)
                    last = dve.tensor_tensor(M[:, q, :, par, :], pair(psM[par][:, 0:256], P),
                                             K.masks[:, par, d, :].unsqueeze(1).to_broadcast([P, 2, P]), ALU.mult)
                link(last)
                for par, rows in halves:
                    dve.tensor_copy(PB[rows, q, :, rows], M[rows, q, :, par, 0:64])
                    last = dve.tensor_tensor(X[rows, q, :, :], M[rows, q, :, par, 0:64],
                                             K.ident[rows, rows].unsqueeze(1).to_broadcast([64, 2, 64]), ALU.add)
                last.then_inc(S["masked"], 1)

            def add_x(s, r):
                q = s % 2
                dve.wait_ge(powered[q], 6 * (s // 2) + r + 1)
                if r == ROUNDS - 1 and s >= 2:
                    dve.wait_ge(S["n_ready"], s - 1)
                if s >= 2 or r:
                    dve.wait_ge(x_added[q], 6 * (s // 2) + r)
                prod = pair(psP[q][:, 0:384], 192)
                if r == ROUNDS - 1:
                    for par, rows in halves:
                        last = dve.tensor_tensor(XF[rows, q, :, rows], X[rows, q, :, :], prod[rows, :, P:192], ALU.add)
                else:
                    if r < ROUNDS - 2:
                        last = dve.tensor_copy(PB[:, q, :, :], prod[:, :, 0:P])
                    if r:
                        last = dve.tensor_tensor(X[:, q, :, :], X[:, q, :, :], prod[:, :, P:192], ALU.add)
                last.then_inc(x_added[q], 1)

            def take_n(s):
                dve.wait_ge(S["n_ready"], s + 1)
                for par, rows in halves:
                    last = dve.tensor_copy(K.SV[rows, chunk(s), :, par, :], pair(psN[rows, 0:128], 64))
                last.then_inc(S["n_copied"], 1)

            def take_state(s):
                dve.wait_ge(S["state_mm"], s + 1)
                link(dve.tensor_tensor(ST[:, :, :], ST[:, :, :], pair(psC[:, U_:U_ + 128], 64), ALU.add))
                dve.tensor_tensor(ST[:, :, :], ST[:, :, :], K.DC[:, :, chunk(s):chunk(s) + 1].to_broadcast([P, 2, 64]),
                                  ALU.mult).then_inc(S["state_ok"], 1)
                y, prod = K.Y[:, chunk(s), :, :], pair(psC[:, Y_:Y_ + 128], 64)
                last = dve.tensor_copy(y, prod) if d == 0 else dve.tensor_tensor(y, y, prod, ALU.add)
                last.then_inc(S["y_copied"], 1)

            mask(0)
            mask(1)
            for r in range(ROUNDS):
                add_x(0, r)
                add_x(1, r)
            for s in range(0, NCH, 2):
                more = s + 2 < NCH
                take_n(s)
                take_state(s)
                if more:
                    mask(s + 2)
                    add_x(s + 2, 0)
                    add_x(s + 2, 1)
                take_n(s + 1)
                if more:
                    add_x(s + 2, 2)
                take_state(s + 1)
                if more:
                    mask(s + 3)
                    for r in range(ROUNDS):
                        if r + 3 < ROUNDS:
                            add_x(s + 2, r + 3)
                        add_x(s + 3, r)


def rwkv_output(nc, K, hf):
    tag = f"o{hf}"
    with ExitStack() as ctx:
        S = sems(nc, ctx, "centred sqd vard rooted normed turned bonus gate ol", tag)
        Y = K.Y[:, :, :, :].rearrange("p n c f -> p (n c) f")
        NG = 2 * NCH
        block = ctx.enter_context(nc.Block())
        sq = K.AR[:, 0, :, :, :].rearrange("p a b c -> p (a b) c")
        st = K.BK[:, 0, 0, 0, :]
        mean, rstd = st[:, 0:NG], st[:, NG:2 * NG]
        tb = K.tmp[0]
        z = K.tmp[1]

        @block.vector
        def _(dve):
            link = linker(dve, S["ol"])
            link(dve.tensor_reduce(mean, Y, AX, ALU.add))
            link(dve.tensor_scalar(mean, mean, 1.0 / 64, None, ALU.mult))
            link(dve.tensor_tensor(Y, Y, mean.unsqueeze(2).to_broadcast([P, NG, 64]), ALU.subtract))
            link(dve.tensor_tensor(sq, Y, Y, ALU.mult))
            link(dve.tensor_reduce(rstd, sq, AX, ALU.add))
            dve.tensor_scalar(rstd, rstd, 1.0 / 64, LNX_EPS, ALU.mult, ALU.add).then_inc(S["vard"], 1)
            for c in range(2):
                cp = 2 * hf + c
                dve.scalar_tensor_tensor(out=tb[:, c, :], in0=K.u[:, cp, :], scalar=K.par[:, GAIN_RK, cp:cp + 1],
                                         in1=K.ksum[:, c, :], op0=ALU.mult, op1=ALU.mult).then_inc(S["bonus"], 1)
            dve.wait_ge(S["rooted"], 1)
            link(dve.reciprocal(rstd, rstd))
            dve.tensor_tensor(Y, Y, rstd.unsqueeze(2).to_broadcast([P, NG, 64]), ALU.mult).then_inc(S["normed"], 1)
            for c in range(2):
                cp = 2 * hf + c
                dve.wait_ge(S["gate"], 2 * c + 2)
                bo = tb[:, c, :]
                link(dve.tensor_tensor(bo, K.u[:, 8 + cp, :], K.ps[2 + c][:, :], ALU.mult))
                dve.wait_ge(S["turned"], c + 1)
                link(dve.tensor_scalar(z[:, c, :], K.ps[c][:, :], K.par[:, LN_W, cp:cp + 1], K.par[:, LN_B, cp:cp + 1],
                                       ALU.mult, ALU.add))
                link(dve.tensor_tensor(z[:, c, :], z[:, c, :], bo, ALU.add))
                dve.tensor_tensor(K.u[:, cp, :], z[:, c, :], K.ps[4 + c][:, :], ALU.mult)

        @block.scalar
        def _(act):
            act.wait_ge(S["vard"], 1)
            nc.scalar.activation(rstd, rstd, ACT.Sqrt).then_inc(S["rooted"], 1)

        @block.tensor
        def _(pe):
            for c in range(2):
                cp = 2 * hf + c
                pe.wait_ge(S["bonus"], c + 1)
                pe.matmul(K.ps[2 + c][:, :], K.heads1[:, :], tb[:, c, :], start=True, stop=True).then_inc(S["gate"], 1)
                pe.matmul(K.ps[4 + c][:, :], K.gup[:, cp * P:(cp + 1) * P], K.u[:, 12, :], start=True, stop=True).then_inc(S["gate"], 1)
            pe.wait_ge(S["normed"], 1)
            for c in range(2):
                for ch in range(NCH):
                    for b in (0, 64):
                        last = pe.matmul(K.ps[c][b:b + 64, ch * 64:ch * 64 + 64], K.Y[b:b + 64, ch, c, :],
                                         K.ident[b:b + 64, b:b + 64], start=True, stop=True)
                last.then_inc(S["turned"], 1)


def merge_branches(nc, K, tag, gates, proj, w_out, parts, load_upto):
    with ExitStack() as ctx:
        names = "emm egate eprod esum eadd"
        S = sems(nc, ctx, names, tag)
        G = ctx.enter_context(nc.sbuf_tensor("G" + tag, [P, 2 * KD, T], F32))
        tmp = ctx.enter_context(nc.sbuf_tensor("gt" + tag, [P, 2, T], F32))
        groups = [(b, ch) for b in range(2) for ch in range(KD)]
        for i, n in enumerate(gates):
            K.ring.used[n] = (S["emm"], 4 * i + 4)
        for b, (_, _, loads) in enumerate(proj):
            per = KD // len(loads)
            for i, n in enumerate(loads):
                K.ring.used[n] = (S["emm"], 16 + 8 * b + per * (i + 1))
        for i, n in enumerate(w_out):
            K.ring.used[n] = (S["emm"], 32 + 4 * i + 4)
        block = ctx.enter_context(nc.Block())

        @block.sync
        def _(sp):
            K.ring.load(sp, load_upto)

        @block.tensor
        def _(pe):
            for c in range(16):
                n = gates[c // 4]
                if c % 4 == 0:
                    K.ring.wait(pe, n)
                if c >= 4:
                    pe.wait_ge(S["egate"], c - 3)
                mm_feature(pe, K.ps[c % 4][:, :], K.ring.tile(n), slice((c % 4) * P, (c % 4) * P + P), K.hT, KD).then_inc(S["emm"], 1)
            for i, (b, ch) in enumerate(groups):
                yT, nk, loads = proj[b]
                per = KD // len(loads)
                n = loads[ch // per]
                if ch % per == 0:
                    K.ring.wait(pe, n)
                if i >= 4:
                    pe.wait_ge(S["eprod"], i - 3)
                f = ch % per
                mm_feature(pe, K.ps[4 + i % 4][:, :], K.ring.tile(n), slice(f * P, f * P + P), yT, nk).then_inc(S["emm"], 1)
            pe.wait_ge(S["esum"], KD)
            for half in range(2):
                n = w_out[half]
                K.ring.wait(pe, n)
                w = K.ring.tile(n)
                for t in range(NT):
                    j = half * NT + t
                    if j >= 4:
                        pe.wait_ge(S["eadd"], j - 3)
                    for k in range(KD):
                        last = pe.matmul(K.ps[j % 4][:, :], G[:, k, t * P:(t + 1) * P], w[:, k, :], start=(k == 0), stop=(k == KD - 1))
                    last.then_inc(S["emm"], 1)

        @block.scalar
        def _(act):
            for c in range(16):
                act.wait_ge(S["emm"], c + 1)
                nc.scalar.activation(G[:, c, :], K.ps[c % 4][:, :], ACT.Sigmoid).then_inc(S["egate"], 1)

        @block.vector
        def _(dve):
            for i, (b, ch) in enumerate(groups):
                dve.wait_ge(S["emm"], 16 + i + 1)
                dve.wait_ge(S["egate"], 16)
                ps = K.ps[4 + i % 4][:, :]
                if b == 0:
                    dve.tensor_tensor(G[:, ch, :], G[:, ch, :], ps, ALU.mult).then_inc(S["eprod"], 1)
                else:
                    if ch >= 2:
                        dve.wait_ge(S["esum"], ch - 1)
                    dve.tensor_tensor(tmp[:, ch % 2, :], G[:, KD + ch, :], ps, ALU.mult).then_inc(S["eprod"], 1)
                    dve.wait_ge(S["eprod"], i + 1)
                    dve.tensor_tensor(G[:, ch, :], G[:, ch, :], tmp[:, ch % 2, :], ALU.add).then_inc(S["esum"], 1)
            for half in range(2):
                for t in range(NT):
                    j = half * NT + t
                    dve.wait_ge(S["emm"], 32 + j + 1)
                    o = K.x[:, t, half * 512:(half + 1) * 512]
                    dve.tensor_tensor(o, o, K.ps[j % 4][:, :], ALU.add).then_inc(S["eadd"], 1)


def route(nc, K):
    I = K.I
    with ExitStack() as ctx:
        names = "win lmm neg ex rec aff_t aff topped bmm bcop rl"
        S = sems(nc, ctx, names, "r")
        sbt = lambda n, s, dt=F32: ctx.enter_context(nc.sbuf_tensor(n, s, dt))
        wr, L, st = sbt("wr", [P, KD, N_EXP]), sbt("L", [P, NT, N_EXP]), sbt("rst", [P, 3, NT])
        aff, tv = sbt("aff", [N_EXP, T]), sbt("tv", [N_EXP, 4, CAP])
        ti = sbt("ti", [N_EXP, CAP], U32)
        sel = sbt("sel", [N_EXP, N_EXP, P])
        block = ctx.enter_context(nc.Block())

        @block.sync
        def _(sp):
            sp.dma_start(wr[:, :, :], I["w_router"][0].rearrange("(k p) e -> p k e", p=P)).then_inc(S["win"], 16)
            sp.dma_start(sel[:, :, :], I["c_sel"]).then_inc(S["win"], 16)
            sp.dma_start(K.tok[:, :], I["c_tok"]).then_inc(S["win"], 16)
            with nc.allow_non_contiguous_dma(reason="one gain per partition"):
                sp.dma_start(K.gf[:, :], I["norm_ffn_g"][0].rearrange("(k p) -> p k", p=P)).then_inc(S["win"], 16)
            sp.wait_ge(S["win"], 64)

        @block.tensor
        def _(pe):
            pe.wait_ge(S["win"], 64)
            for t in range(NT):
                for k in range(KD):
                    last = pe.matmul(K.ps[0][:, t * N_EXP:(t + 1) * N_EXP], K.hT[:, k, t * P:(t + 1) * P], wr[:, k, :],
                                     start=(k == 0), stop=(k == KD - 1))
            last.then_inc(S["lmm"], 1)
            pe.wait_ge(S["aff_t"], 1)
            for t in range(NT):
                last = pe.transpose(K.ps[1][0:N_EXP, t * P:(t + 1) * P], L[:, t, :], K.ident[:, :])
            last.then_inc(S["aff"], 1)
            pe.wait_ge(S["topped"], 1)
            for e in range(N_EXP):
                if e >= 2 * 4 and e % 2 == 0:
                    pe.wait_ge(S["bcop"], e // 2 - 3)
                last = pe.matmul(K.ps[2 + (e // 2) % 4][:, (e % 2) * 256:(e % 2) * 256 + 256], sel[:, e, :], tv[:, :, :],
                                 start=True, stop=True)
                if e % 2:
                    last.then_inc(S["bmm"], 1)

        @block.scalar
        def _(act):
            act.wait_ge(S["neg"], 1)
            for t in range(NT):
                last = nc.scalar.activation(L[:, t, :], K.ps[0][:, t * N_EXP:(t + 1) * N_EXP], ACT.Exp, bias=st[:, 0, t:t + 1],
                                            accum_out=st[:, 1, t:t + 1])
            last.then_inc(S["ex"], 1)
            for b in range(N_EXP // 2):
                act.wait_ge(S["bmm"], b + 1)
                nc.scalar.activation(K.IB[:, 2 * b:2 * b + 2, :], K.ps[2 + b % 4][:, :].rearrange("p (e c) -> p e c", e=2),
                                     ACT.Copy).then_inc(S["bcop"], 1)

        @block.vector
        def _(dve):
            link = linker(dve, S["rl"])
            dve.wait_ge(S["lmm"], 1)
            logits = K.ps[0][:, 0:NT * N_EXP].rearrange("p (t e) -> p t e", t=NT)
            dve.tensor_reduce(st[:, 0, :], logits, AX, ALU.max, negate=True).then_inc(S["neg"], 1)
            dve.wait_ge(S["ex"], 1)
            link(dve.reciprocal(st[:, 2, :], st[:, 1, :]))
            dve.tensor_tensor(L[:, :, :], L[:, :, :], st[:, 2, :].unsqueeze(2).to_broadcast([P, NT, N_EXP]), ALU.mult).then_inc(S["aff_t"], 1)
            dve.wait_ge(S["aff"], 1)
            link(dve.tensor_copy(aff[:, :], K.ps[1][0:N_EXP, :]))
            for r in range(CAP // 8):
                best = tv[:, 2, 8 * r:8 * r + 8]
                link(dve.max(best, aff[:, :]))
                link(dve.max_index(ti[:, 8 * r:8 * r + 8], best, aff[:, :]))
                if r + 1 < CAP // 8:
                    link(dve.match_replace(aff[:, :], best, aff[:, :], -1.0))
            dve.tensor_copy(tv[:, 3, :], tv[:, 2, :])
            dve.tensor_copy(tv[:, 0, :], ti[:, :])
            dve.tensor_copy(tv[:, 1, :], ti[:, :]).then_inc(S["topped"], 1)


def experts(nc, K, n0, load_upto):
    I = K.I
    H = 512
    names = ("w_used oh_ready gathered xs_copied xs_turned xsT_ready gate_sig gated hid_ready hid_turned hidT_ready "
             "ys_ready oht_turned oht_ready combined x_added")
    with ExitStack() as ctx:
        S = sems(nc, ctx, names, "m")
        sbt = lambda n, s: ctx.enter_context(nc.sbuf_tensor(n, s, F32))
        OH, OHV = sbt("OH", [P, NT, CAP]), sbt("OHV", [P, NT, P])
        XS = sbt("XS", [P, H])
        xsT = sbt("xsT", [P, 2, 4, 2, CAP])
        HS, hidT, ys = sbt("HS", [P, H]), sbt("hidT", [P, 4, 2, CAP]), sbt("ys", [P, H])
        OHT = sbt("OHT", [P, 2, NT, P])
        psO, psX, psT, psG, psU, psD = K.ps[0:6]
        psC = K.ps[6:8]
        srcs = (I["exp_w_gate"], I["exp_w_up"], I["exp_w_down"])
        slot = lambda j: K.ring.buf[:, (n0 + j) % RING, :].rearrange("p (k w) -> p k w", k=4)
        block = ctx.enter_context(nc.Block())
        LOOPS = N_EXP // 2 - 1

        def wait(eng, sem, value):
            if not isinstance(value, int) or value > 0:
                eng.wait_ge(sem, value)

        def load(sp, e, part, j):
            src = srcs[part // 2][0, bass.ds(e, 1), (part % 2) * H:(part % 2) * H + H, :]
            sp.dma_start(slot(j), src.rearrange("e (k p) w -> p (e k) w", p=P)).then_inc(K.ring.full[(n0 + j) % RING], 16)

        @block.sync
        def _(sp):
            if K.ring.issued < n0 + 4:
                for j in range(K.ring.issued - n0, 4):
                    load(sp, 0, j, j)
            with sp.Fori(0, LOOPS) as i:
                for j in range(12):
                    m = 4 + j
                    sp.wait_ge(S["w_used"], i * 12 + (j + 1))
                    load(sp, i * 2 + m // 6, m % 6, m)
            for j in range(12 * LOOPS + 4, 96):
                sp.wait_ge(S["w_used"], j - 3)
                load(sp, j // 6, j % 6, j)
            K.ring.issued = n0 + 96
            K.ring.used = {n0 + j: (S["w_used"], j + 1) for j in range(92, 96)}
            K.ring.load(sp, load_upto)

        def each(eng, steps):
            steps(0, 0, False)
            steps(1, 1, False)
            with eng.Fori(1, LOOPS) as i:
                for u in range(2):
                    steps(i * 2 + u, u, False)
            steps(N_EXP - 2, 0, False)
            steps(N_EXP - 1, 1, True)

        @block.tensor
        def _(pe):
            def gather(e):
                pe.wait_ge(S["oh_ready"], e + 1)
                wait(pe, S["xs_copied"], e)
                for t in range(NT):
                    for half in range(2):
                        last = pe.matmul(psX[64 * half:64 * half + 64, :], OH[:, t, :], K.xn[:, t, half * H:(half + 1) * H],
                                         start=(t == 0), stop=(t == NT - 1))
                last.then_inc(S["gathered"], 1)

            def turn_xs(e):
                pe.wait_ge(S["xs_copied"], e + 1)
                wait(pe, S["hidT_ready"], e)
                for c in range(4):
                    last = pe.transpose(psT[:, c * P:(c + 1) * P], XS[:, c * P:(c + 1) * P], K.ident[:, :])
                last.then_inc(S["xs_turned"], 1)

            def turn_oh(e):
                pe.wait_ge(S["oh_ready"], e + 1)
                wait(pe, S["oht_ready"], e)
                for t in range(NT):
                    last = pe.transpose(psO[:, t * P:(t + 1) * P], OHV[:, t, :], K.ident[:, :])
                last.then_inc(S["oht_turned"], 1)

            def halves(e, u, out, lhs, part):
                for ld in range(2):
                    j = 6 * u + 2 * part + ld
                    s = (n0 + j) % RING
                    pe.wait_ge(K.ring.full[s], (e - u) * 24 + 16 * ((n0 + j) // RING + 1))
                    for kk in range(4):
                        k = 4 * ld + kk
                        for half in range(2):
                            last = pe.matmul(out[64 * half:64 * half + 64, :], lhs[:, k % 4, k // 4, :],
                                             slot(j)[:, kk, half * H:(half + 1) * H], start=(k == 0), stop=(k == KD - 1))
                    last.then_inc(S["w_used"], 1)

            def steps(e, u, final):
                pe.wait_ge(S["xsT_ready"], e + 1)
                wait(pe, S["hid_ready"], e)
                halves(e, u, psG, xsT[:, u], 0)
                halves(e, u, psU, xsT[:, u], 1)
                if not final:
                    gather(e + 1)
                pe.wait_ge(S["hid_ready"], e + 1)
                for c in range(4):
                    last = pe.transpose(psT[:, c * P:(c + 1) * P], HS[:, c * P:(c + 1) * P], K.ident[:, :])
                last.then_inc(S["hid_turned"], 1)
                pe.wait_ge(S["hidT_ready"], e + 1)
                wait(pe, S["ys_ready"], e)
                halves(e, u, psD, hidT, 2)
                if not final:
                    turn_xs(e + 1)
                    turn_oh(e + 1)
                pe.wait_ge(S["ys_ready"], e + 1)
                pe.wait_ge(S["oht_ready"], e + 1)
                for j in range(8):
                    t, half = j // 2, j % 2
                    if j >= 2:
                        wait(pe, S["x_added"], e * 8 + (j - 1))
                    else:
                        wait(pe, S["x_added"], e * 8)
                    rows = slice(64 * half, 64 * half + 64)
                    pe.matmul(psC[half][:, :], OHT[rows, u, t, :], ys[rows, :], start=True, stop=True).then_inc(S["combined"], 1)

            gather(0)
            turn_xs(0)
            turn_oh(0)
            each(pe, steps)

        @block.scalar
        def _(act):
            def copy_xs(e):
                act.wait_ge(S["gathered"], e + 1)
                wait(act, S["xs_turned"], e)
                nc.scalar.activation(XS[:, :], psX[:, :], ACT.Copy).then_inc(S["xs_copied"], 1)

            def copy_oh(e, u):
                act.wait_ge(S["oht_turned"], e + 1)
                nc.scalar.activation(OHT[:, u, :, :], psO[:, :].rearrange("p (t c) -> p t c", t=NT), ACT.Copy).then_inc(S["oht_ready"], 1)

            def steps(e, u, final):
                act.wait_ge(S["w_used"], e * 6 + 2)
                wait(act, S["hid_turned"], e)
                nc.scalar.activation(HS[:, :], psG[:, :], ACT.Sigmoid).then_inc(S["gate_sig"], 1)
                if not final:
                    copy_xs(e + 1)
                act.wait_ge(S["hid_turned"], e + 1)
                nc.scalar.activation(hidT[:, :, :, :], psT[:, :].rearrange("p (c h s) -> p c h s", c=4, h=2), ACT.Copy).then_inc(S["hidT_ready"], 1)
                act.wait_ge(S["w_used"], e * 6 + 6)
                wait(act, S["combined"], e * 8)
                nc.scalar.activation(ys[:, :], psD[:, :], ACT.Copy).then_inc(S["ys_ready"], 1)
                if not final:
                    copy_oh(e + 1, 1 - u)

            copy_xs(0)
            copy_oh(0, 0)
            each(act, steps)

        @block.vector
        def _(dve):
            def one_hots(e):
                wait(dve, S["gathered"], e)
                wait(dve, S["oht_turned"], e)
                for t in range(NT):
                    dve.tensor_scalar(OH[:, t, :], K.IB[:, bass.ds(e, 1), 0:CAP].rearrange("p a c -> p (a c)"),
                                      K.tok[:, t:t + 1], None, ALU.is_equal)
                    last = dve.scalar_tensor_tensor(
                        out=OHV[:, t, :], in0=K.IB[:, bass.ds(e, 1), 0:P].rearrange("p a c -> p (a c)"), scalar=K.tok[:, t:t + 1],
                        in1=K.IB[:, bass.ds(e, 1), P:2 * P].rearrange("p a c -> p (a c)"), op0=ALU.is_equal, op1=ALU.mult)
                last.then_inc(S["oh_ready"], 1)

            def scale_xs(e, u):
                dve.wait_ge(S["xs_turned"], e + 1)
                dve.tensor_tensor(xsT[:, u, :, :, :], psT[:, :].rearrange("p (c h s) -> p c h s", c=4, h=2),
                                  K.gf[:, :].rearrange("p (h c) -> p c h", h=2).unsqueeze(3).to_broadcast([P, 4, 2, CAP]), ALU.mult).then_inc(S["xsT_ready"], 1)

            def steps(e, u, final):
                if not final:
                    one_hots(e + 1)
                dve.wait_ge(S["gate_sig"], e + 1)
                dve.tensor_tensor(HS[:, :], HS[:, :], psG[:, :], ALU.mult).then_inc(S["gated"], 1)
                dve.wait_ge(S["gated"], e + 1)
                dve.wait_ge(S["w_used"], e * 6 + 4)
                dve.tensor_tensor(HS[:, :], HS[:, :], psU[:, :], ALU.mult).then_inc(S["hid_ready"], 1)
                if not final:
                    scale_xs(e + 1, 1 - u)
                for j in range(8):
                    t, half = j // 2, j % 2
                    dve.wait_ge(S["combined"], e * 8 + (j + 1))
                    o = K.x[:, t, half * H:(half + 1) * H]
                    dve.tensor_tensor(o, o, psC[half][:, :], ALU.add).then_inc(S["x_added"], 1)

            one_hots(0)
            scale_xs(0, 0)
            each(dve, steps)


def gain_norm(nc, K, tag, g, out_dram=None, keep_dram=None):
    dst = out_dram if out_dram is not None else keep_dram
    with ExitStack() as ctx:
        S = sems(nc, ctx, "g_in squared var_ok root_ok rec_ok scaled gained stored", tag)
        gb = ctx.enter_context(nc.sbuf_tensor("gb" + tag, [P, D], F32))
        sq = ctx.enter_context(nc.sbuf_tensor("sqg" + tag, [P, 2, D], F32))
        ss = ctx.enter_context(nc.sbuf_tensor("ssg" + tag, [P, 4, NT], F32))
        block = ctx.enter_context(nc.Block())

        @block.sync
        def _(sp):
            sp.dma_start(gb[:, :], g.rearrange("(a d) -> a d", a=1).to_broadcast([P, D])).then_inc(S["g_in"], 16)
            for t in range(NT):
                sp.wait_ge(S["gained"], t + 1)
                sp.dma_start(dst[t * P:(t + 1) * P, :], K.x[:, t, :]).then_inc(S["stored"], 16)
            sp.wait_ge(S["stored"], 16 * NT)

        @block.scalar
        def _(act):
            for t in range(NT):
                if t >= 2:
                    act.wait_ge(S["squared"], t - 1)
                nc.scalar.activation(sq[:, t % 2, :], K.x[:, t, :], ACT.Square, accum_out=ss[:, 0, t:t + 1]).then_inc(S["squared"], 1)
            act.wait_ge(S["var_ok"], 1)
            nc.scalar.activation(ss[:, 2, :], ss[:, 1, :], ACT.Sqrt).then_inc(S["root_ok"], 1)

        @block.vector
        def _(dve):
            dve.wait_ge(S["squared"], NT)
            dve.tensor_scalar(ss[:, 1, :], ss[:, 0, :], 1.0 / D, EPS, ALU.mult, ALU.add).then_inc(S["var_ok"], 1)
            dve.wait_ge(S["root_ok"], 1)
            dve.reciprocal(ss[:, 3, :], ss[:, 2, :]).then_inc(S["rec_ok"], 1)
            dve.wait_ge(S["rec_ok"], 1)
            dve.wait_ge(S["g_in"], 16)
            for t in range(NT):
                dve.scalar_tensor_tensor(out=K.x[:, t, :], in0=K.x[:, t, :], scalar=ss[:, 3, t:t + 1], in1=gb[:, :],
                                         op0=ALU.mult, op1=ALU.mult).then_inc(S["gained"], 1)


def mlstm_inputs(nc, K, n0, load_upto):
    I = K.I
    NC2 = 2 * D // P
    with ExitStack() as ctx:
        S = sems(nc, ctx, "mm par first tap sig act vcop gmm gcop rows e1 e2 e3 bmm bcop cmm xl al", "I")
        sbt = lambda n, s: ctx.enter_context(nc.sbuf_tensor(n, s, F32))
        cw, cb = sbt("cw", [P, 5, NC2]), None
        acc = sbt("acc", [P, 2, T])
        sgb = sbt("sgb", [P, 2, T])
        wif = sbt("wif", [P, KD, 8])
        bif = sbt("bif", [M_HEADS, 2])
        rows = sbt("rows", [M_HEADS, 6, T])
        mrow = sbt("mrow", [M_HEADS, 4, NT + 1])
        reset = sbt("reset", [M_HEADS, 2, T])
        K.ring.used = {n0 + i: (S["mm"], 4 * i + 4) for i in range(6)}
        block = ctx.enter_context(nc.Block())
        ig, lf, b, M, ex, wk = (rows[:, j, :] for j in range(6))

        @block.sync
        def _(sp):
            with nc.allow_non_contiguous_dma(reason="one tap per partition"):
                for j in range(4):
                    sp.dma_start(cw[:, j, :], I["conv_w_2"][0][j].rearrange("(c p) -> p c", p=P)).then_inc(S["par"], 16)
                sp.dma_start(cw[:, 4, :], I["conv_b_2"][0].rearrange("(c p) -> p c", p=P)).then_inc(S["par"], 16)
                sp.dma_start(wif[:, :, :], I["w_in_2"][0][:, IF_M:IF_M + 8].rearrange("(k p) w -> p k w", p=P)).then_inc(S["par"], 16)
                sp.dma_start(bif[:, :], I["b_gate_if_2"][0].rearrange("(j h) -> h j", j=2)).then_inc(S["par"], 16)
            sp.dma_start(reset[:, :, :], I["c_reset"]).then_inc(S["par"], 16)
            sp.dma_start(K.sel4[:, :, :], I["c_sel4"]).then_inc(S["par"], 16)
            sp.dma_start(K.causal[:, :], I["c_causal"]).then_inc(S["par"], 16)
            K.ring.load(sp, load_upto)
            sp.wait_ge(S["par"], 160)

        @block.tensor
        def _(pe):
            pe.wait_ge(S["par"], 160)
            for j in range(2):
                for k in range(KD):
                    last = pe.matmul(K.ps[4 + j][0:M_HEADS, :], wif[:, k, 4 * j:4 * j + 4], K.hT[:, k, :], start=(k == 0), stop=(k == KD - 1))
            last.then_inc(S["gmm"], 1)
            for c in range(NC2):
                if c % 4 == 0:
                    K.ring.wait(pe, n0 + c // 4)
                if c >= 4:
                    pe.wait_ge(S["tap"], c - 3)
                mm_feature(pe, K.ps[c % 4][:, :], K.ring.tile(n0 + c // 4), slice((c % 4) * P, (c % 4) * P + P), K.hT, KD).then_inc(S["mm"], 1)
            for half in range(2):
                n = n0 + 4 + half
                K.ring.wait(pe, n)
                w = K.ring.tile(n)
                for t in range(NT):
                    j = half * NT + t
                    if j < 4:
                        pe.wait_ge(S["tap"], 13 + j)
                    else:
                        pe.wait_ge(S["vcop"], j - 3)
                    for k in range(KD):
                        last = pe.matmul(K.ps[j % 4][:, :], K.hT[:, k, t * P:(t + 1) * P], w[:, k, :], start=(k == 0), stop=(k == KD - 1))
                    last.then_inc(S["mm"], 1)
            pe.wait_ge(S["e2"], 1)
            for j, row in enumerate((M, ex)):
                for h in range(M_HEADS):
                    i = j * 4 + h
                    if i >= 2:
                        pe.wait_ge(S["bcop"], i - 1)
                    pe.matmul(K.ps[4 + i % 2][:, :], K.sel4[:, h, :], row, start=True, stop=True).then_inc(S["bmm"], 1)
            for q, row in enumerate((b, ig, wk)):
                for c in range(NT):
                    pe.transpose(K.ps[6][:, (q * NT + c) * 4:(q * NT + c) * 4 + 4], row[:, c * P:(c + 1) * P], K.ident[0:4, 0:4])
            for h in range(M_HEADS):
                last = pe.matmul(K.ps[6][:, 64 + 4 * h:68 + 4 * h], K.sel4[:, h, :], mrow[:, 2, 0:NT], start=True, stop=True)
            last.then_inc(S["cmm"], 1)

        @block.scalar
        def _(act):
            act.wait_ge(S["par"], 160)
            link = linker(act, S["al"])
            act.wait_ge(S["gcop"], 2)
            link(nc.scalar.activation(M, lf, ACT.Abs))
            link(nc.scalar.activation(M, M, ACT.Exp, scale=-1.0))
            nc.scalar.activation(M, M, ACT.Ln, bias=1.0).then_inc(S["e1"], 1)
            for c in range(NC2):
                dst = K.qmT[:, c, :] if c < 8 else K.kmT[:, c - 8, :]
                act.wait_ge(S["mm"], c + 1)
                if c >= 2:
                    act.wait_ge(S["act"], c - 1)
                nc.scalar.activation(acc[:, c % 2, :], K.ps[c % 4][:, :], ACT.Identity, scale=cw[:, 3, c:c + 1],
                                     bias=cw[:, 4, c:c + 1]).then_inc(S["first"], 1)
                act.wait_ge(S["tap"], c + 1)
                nc.scalar.activation(sgb[:, c % 2, :], acc[:, c % 2, :], ACT.Sigmoid).then_inc(S["sig"], 1)
            for j in range(8):
                t, half = j % 4, j // 4
                act.wait_ge(S["mm"], NC2 + j + 1)
                nc.scalar.activation(K.vm[:, t, 2 * half:2 * half + 2, 0:M_DH], K.ps[j % 4][:, :].rearrange("p (h d) -> p h d", h=2),
                                     ACT.Copy).then_inc(S["vcop"], 1)
            act.wait_ge(S["rows"], 1)
            nc.scalar.activation(ex, ex, ACT.Exp)
            nc.scalar.activation(mrow[:, 2, 0:NT], mrow[:, 2, 0:NT], ACT.Exp)
            nc.scalar.activation(wk, wk, ACT.Exp)
            nc.scalar.activation(b, b, ACT.Exp).then_inc(S["e2"], 1)
            for i in range(8):
                act.wait_ge(S["bmm"], i + 1)
                dst = K.MB if i < 4 else K.WI
                nc.scalar.activation(dst[:, i % 4, :], K.ps[4 + i % 2][:, :], ACT.Copy).then_inc(S["bcop"], 1)
            act.wait_ge(S["cmm"], 1)
            nc.scalar.activation(K.cols[:, :, :], K.ps[6][:, 0:48].rearrange("p (q c h) -> p q (c h)", q=3, c=NT), ACT.Copy)
            nc.scalar.activation(K.dec[:, :], K.ps[6][:, 64:80], ACT.Copy)

        @block.vector
        def _(dve):
            dve.wait_ge(S["par"], 160)
            dve.wait_ge(S["gmm"], 1)
            dve.tensor_scalar(ig, K.ps[4][0:M_HEADS, :], bif[:, 0:1], None, ALU.add).then_inc(S["gcop"], 1)
            dve.tensor_scalar(lf, K.ps[5][0:M_HEADS, :], bif[:, 1:2], None, ALU.add).then_inc(S["gcop"], 1)
            link = linker(dve, S["xl"])
            dve.wait_ge(S["e1"], 1)
            link(dve.tensor_scalar(lf, lf, 0.0, None, ALU.min))
            link(dve.tensor_tensor(lf, lf, M, ALU.subtract))
            link(dve.tensor_tensor_scan(b, reset[:, 0, :], lf, 0.0, ALU.mult, ALU.add))
            link(dve.tensor_tensor(ig, ig, b, ALU.subtract))
            link(dve.memset(mrow[:, :, :], 0.0))
            for c in range(NT):
                cc = slice(c * P, (c + 1) * P)
                last = (c + 1) * P - 1
                link(dve.tensor_tensor_scan(M[:, cc], reset[:, 1, cc], ig[:, cc], mrow[:, 0, c:c + 1], ALU.add, ALU.max))
                link(dve.tensor_tensor(mrow[:, 0, c + 1:c + 2], M[:, last:last + 1], b[:, last:last + 1], ALU.add))
                dve.tensor_scalar(ex[:, cc], M[:, cc], -1.0, mrow[:, 0, c:c + 1], ALU.mult, ALU.add)
                dve.tensor_tensor(mrow[:, 2, c:c + 1], mrow[:, 0, c:c + 1], M[:, last:last + 1], ALU.subtract)
                link(dve.tensor_scalar(wk[:, cc], ig[:, cc], M[:, last:last + 1], None, ALU.subtract))
            dve.scalar_tensor_tensor(out=b, in0=b, scalar=-1.0, in1=M, op0=ALU.mult, op1=ALU.subtract).then_inc(S["rows"], 1)
            dve.memset(K.vm[:, :, :, M_DH:M_DH + 1], 1.0)
            for c in range(NC2):
                dst = K.qmT[:, c, :] if c < 8 else K.kmT[:, c - 8, :]
                a, ps = acc[:, c % 2, :], K.ps[c % 4]
                dve.wait_ge(S["first"], c + 1)
                for j in (2, 1, 0):
                    d = 3 - j
                    ins = dve.scalar_tensor_tensor(out=a[:, d:T], in0=ps[:, 0:T - d], scalar=cw[:, j, c:c + 1], in1=a[:, d:T],
                                                   op0=ALU.mult, op1=ALU.add)
                    if j:
                        link(ins)
                    else:
                        ins.then_inc(S["tap"], 1)
                dve.wait_ge(S["sig"], c + 1)
                dve.scalar_tensor_tensor(out=dst, in0=a, scalar=M_DH ** -0.5 if c < 8 else 1.0, in1=sgb[:, c % 2, :],
                                         op0=ALU.mult, op1=ALU.mult).then_inc(S["act"], 1)


def mlstm_cell(nc, K):
    W1 = M_DH + 1
    N = NT * M_HEADS
    with ExitStack() as ctx:
        S = sems(nc, ctx, "sc kt num cup d1 w0 w wq kw den h c stat var root l", "L")
        sbt = lambda n, s: ctx.enter_context(nc.sbuf_tensor(n, s, F32))
        W, D1 = sbt("W", [P, 2, P]), sbt("D1", [P, 2, P])
        qI, kw = sbt("qI", [P, 2, 2, P]), sbt("kw", [P, 2, M_DH])
        C = sbt("C", [P, M_HEADS, 2, W1])
        den = sbt("den", [P, 2, N])
        bs, ba = sbt("bs", [P, N, 6]), sbt("ba", [P, N, 2])
        rs = sbt("rs", [P, N])
        block = ctx.enter_context(nc.Block())
        units = [(c, h) for c in range(NT) for h in range(M_HEADS)]
        psS, psK, psN, psC = K.ps[0:2], K.ps[2:4], K.ps[4:6], K.ps[6:8]
        G_, E_, K_ = 1, 0, 2

        @block.tensor
        def _(pe):
            def scores(i):
                c, h = units[i]
                cc = slice(c * P, (c + 1) * P)
                if i >= 2:
                    pe.wait_ge(S["w"], i - 1)
                    pe.wait_ge(S["kw"], i - 1)
                for j in range(2):
                    last = pe.matmul(psS[i % 2][:, 0:P], K.kmT[:, 2 * h + j, cc], K.qmT[:, 2 * h + j, cc], start=(j == 0), stop=(j == 1))
                last.then_inc(S["sc"], 1)
                for j in range(2):
                    last = pe.transpose(psK[i % 2][:, j * P:(j + 1) * P], K.kmT[:, 2 * h + j, cc], K.ident[:, :])
                last.then_inc(S["kt"], 1)

            scores(0)
            for i, (c, h) in enumerate(units):
                if i + 1 < N:
                    scores(i + 1)
                pe.wait_ge(S["w"], i + 1)
                if c:
                    pe.wait_ge(S["wq"], i - 3)
                    pe.wait_ge(S["c"], i - 3)
                if i >= 2:
                    pe.wait_ge(S["h"], i - 1)
                v = K.vm[:, c, h, :]
                last = pe.matmul(psN[i % 2][:, 0:W1], W[:, i % 2, :], v, start=True, stop=(c == 0))
                if c:
                    for j in range(2):
                        last = pe.matmul(psN[i % 2][:, 0:W1], qI[:, i % 2, j, :], C[:, h, j, :], start=False, stop=(j == 1))
                last.then_inc(S["num"], 1)
                if c < NT - 1:
                    pe.wait_ge(S["kw"], i + 1)
                    if i:
                        pe.wait_ge(S["c"], i)
                    for j in range(2):
                        last = pe.matmul(psC[j][:, 0:W1], kw[:, i % 2, j * P:(j + 1) * P], v, start=True, stop=True)
                    last.then_inc(S["cup"], 1)

        @block.scalar
        def _(act):
            for i, (c, h) in enumerate(units):
                act.wait_ge(S["d1"], i + 1)
                nc.scalar.activation(D1[:, i % 2, :], D1[:, i % 2, :], ACT.Exp, scale=-1.0).then_inc(S["w0"], 1)
                act.wait_ge(S["kt"], i + 1)
                if i >= 2:
                    act.wait_ge(S["cup"], min(i - 1, 12))
                nc.scalar.activation(kw[:, i % 2, :], psK[i % 2][:, 0:2 * P], ACT.Copy, scale=K.cols[:, K_, i:i + 1]).then_inc(S["kw"], 1)
            act.wait_ge(S["var"], 1)
            nc.scalar.activation(rs[:, :], rs[:, :], ACT.Sqrt).then_inc(S["root"], 1)

        @block.vector
        def _(dve):
            link = linker(dve, S["l"])

            def weights(i):
                c, h = units[i]
                cc = slice(c * P, (c + 1) * P)
                if i >= 2:
                    dve.wait_ge(S["num"], i - 1)
                    dve.wait_ge(S["w"], i - 1)
                dve.tensor_scalar(D1[:, i % 2, :], K.MB[:, h, cc], K.cols[:, G_, i:i + 1], 0.0, ALU.subtract, ALU.max).then_inc(S["d1"], 1)
                if c:
                    dve.tensor_tensor(qI[:, i % 2, :, :], K.qmT[:, 2 * h:2 * h + 2, cc],
                                      K.WI[:, h, cc].unsqueeze(1).to_broadcast([P, 2, P]), ALU.mult).then_inc(S["wq"], 1)
                dve.wait_ge(S["w0"], i + 1)
                link(dve.tensor_tensor(D1[:, i % 2, :], D1[:, i % 2, :], K.causal[:, :], ALU.mult))
                dve.wait_ge(S["sc"], i + 1)
                dve.tensor_tensor(W[:, i % 2, :], D1[:, i % 2, :], psS[i % 2][:, 0:P], ALU.mult).then_inc(S["w"], 1)

            weights(0)
            for i, (c, h) in enumerate(units):
                if i + 1 < N:
                    weights(i + 1)
                dve.wait_ge(S["num"], i + 1)
                a, r = den[:, 0, i:i + 1], den[:, 1, i:i + 1]
                dot = psN[i % 2][:, M_DH:W1]
                link(dve.tensor_scalar(a, dot, -1.0, K.cols[:, E_, i:i + 1], ALU.mult, ALU.max))
                link(dve.tensor_tensor(a, a, dot, ALU.max))
                link(dve.reciprocal(r, a))
                hm = K.hm[:, c, h, :]
                dve.tensor_scalar(hm, psN[i % 2][:, 0:M_DH], r, None, ALU.mult).then_inc(S["h"], 1)
                if c < NT - 1:
                    dve.wait_ge(S["cup"], i + 1)
                    for j in range(2):
                        if c == 0:
                            last = dve.tensor_copy(C[:, h, j, :], psC[j][:, 0:W1])
                        else:
                            last = dve.scalar_tensor_tensor(out=C[:, h, j, :], in0=C[:, h, j, :], scalar=K.dec[:, 4 * h + c:4 * h + c + 1],
                                                            in1=psC[j][:, 0:W1], op0=ALU.mult, op1=ALU.add)
                    last.then_inc(S["c"], 1)
                dve.wait_ge(S["h"], i + 1)
                link(dve.bn_stats(bs[:, i, :], hm))
                link(dve.bn_aggr(ba[:, i, :], bs[:, i, :]))
            dve.tensor_scalar(rs[:, :], ba[:, :, 1], EPS, None, ALU.add).then_inc(S["var"], 1)
            dve.wait_ge(S["root"], 1)
            link(dve.reciprocal(rs[:, :], rs[:, :]))
            for i, (c, h) in enumerate(units):
                hm = K.hm[:, c, h, :]
                dve.tensor_scalar(hm, hm, ba[:, i, 0:1], rs[:, i:i + 1], ALU.subtract, ALU.mult)


def mlstm_output(nc, K, n0, load_upto):
    I = K.I
    with ExitStack() as ctx:
        S = sems(nc, ctx, "mm sig tr out par", "O")
        so = ctx.enter_context(nc.sbuf_tensor("so", [P, 2, T], F32))
        gm = ctx.enter_context(nc.sbuf_tensor("gm", [P, KD], F32))
        K.ring.used = {n0 + i: (S["mm"], 4 * i + 4) for i in range(2)}
        block = ctx.enter_context(nc.Block())

        @block.sync
        def _(sp):
            with nc.allow_non_contiguous_dma(reason="one gain per partition"):
                sp.dma_start(gm[:, :], I["mlstm_norm_g_2"][0].rearrange("(c p) -> p c", p=P)).then_inc(S["par"], 16)
            K.ring.load(sp, load_upto)
            sp.wait_ge(S["par"], 16)

        @block.tensor
        def _(pe):
            for c in range(KD):
                if c % 4 == 0:
                    K.ring.wait(pe, n0 + c // 4)
                if c >= 2:
                    pe.wait_ge(S["sig"], c - 1)
                mm_feature(pe, K.ps[c % 2][:, :], K.ring.tile(n0 + c // 4), slice((c % 4) * P, (c % 4) * P + P), K.hT, KD).then_inc(S["mm"], 1)
                if c >= 2:
                    pe.wait_ge(S["out"], c - 1)
                for t in range(NT):
                    last = pe.transpose(K.ps[2 + c % 2][:, t * P:(t + 1) * P], K.hm[:, t, c // 2, (c % 2) * P:(c % 2) * P + P], K.ident[:, :])
                last.then_inc(S["tr"], 1)

        @block.scalar
        def _(act):
            for c in range(KD):
                act.wait_ge(S["mm"], c + 1)
                if c >= 2:
                    act.wait_ge(S["out"], c - 1)
                nc.scalar.activation(so[:, c % 2, :], K.ps[c % 2][:, :], ACT.Sigmoid).then_inc(S["sig"], 1)

        @block.vector
        def _(dve):
            dve.wait_ge(S["par"], 16)
            for c in range(KD):
                dve.wait_ge(S["tr"], c + 1)
                dve.wait_ge(S["sig"], c + 1)
                dve.scalar_tensor_tensor(out=K.ymT[:, c, :], in0=K.ps[2 + c % 2][:, :], scalar=gm[:, c:c + 1], in1=so[:, c % 2, :],
                                         op0=ALU.mult, op1=ALU.mult).then_inc(S["out"], 1)


def second_attention_inputs(nc, K, n0, load_upto):
    I = K.I
    with ExitStack() as ctx:
        S = sems(nc, ctx, "mm cop par one bmm bcop st", "Q")
        rb = ctx.enter_context(nc.sbuf_tensor("rb", [33, 24], F32))
        dist = ctx.enter_context(nc.sbuf_tensor("dist", [33, 640], F32))
        R = ctx.enter_context(nc.sbuf_tensor("R", [8, 640], F32))
        K.ring.used = {n0 + i: (S["mm"], 4 * i + 4) for i in range(9)}
        block = ctx.enter_context(nc.Block())

        @block.sync
        def _(sp):
            sp.wait_ge(S["one"], 1)
            sp.dma_start(rb[0:32, :], I["rel_bias_2"]).then_inc(S["par"], 16)
            sp.dma_start(K.flip[:, :], I["c_flip"]).then_inc(S["par"], 16)
            sp.dma_start(dist[:, :], I["c_dist"][:, 0, :]).then_inc(S["par"], 16)
            K.ring.load(sp, n0 + 2 + RING, more=True)
            for g in range(3):
                if g:
                    sp.wait_ge(S["bmm"], g)
                    sp.dma_start(dist[:, :], I["c_dist"][:, g, :]).then_inc(S["par"], 16)
                sp.wait_ge(S["bcop"], g + 1)
                sp.dma_start(K.R_dram[g, :, :], R[:, :]).then_inc(S["st"], 16)
            sp.wait_ge(S["st"], 48)
            K.ring.load(sp, load_upto)

        @block.tensor
        def _(pe):
            for c in range(24):
                n = n0 + c // 4
                if c % 4 == 0:
                    K.ring.wait(pe, n)
                if c >= 4:
                    pe.wait_ge(S["cop"], c - 3)
                mm_feature(pe, K.ps[c % 4][:, :], K.ring.tile(n), slice((c % 4) * P, (c % 4) * P + P), K.hT, KD).then_inc(S["mm"], 1)
                if c in (4, 8, 12):
                    g = c // 4 - 1
                    pe.wait_ge(S["par"], 48 + 16 * g)
                    if g:
                        pe.wait_ge(S["bcop"], g)
                    pe.matmul(K.ps[4][0:8, :], rb[:, 8 * g:8 * g + 8], dist[:, 0:512], start=True, stop=True)
                    pe.matmul(K.ps[5][0:8, 0:128], rb[:, 8 * g:8 * g + 8], dist[:, 512:640], start=True, stop=True).then_inc(S["bmm"], 1)
            for j in range(12):
                s, t = j // NT, j % NT
                n = n0 + 6 + s
                if t == 0:
                    K.ring.wait(pe, n)
                pe.wait_ge(S["cop"], 24 + j - 3)
                for k in range(KD):
                    last = pe.matmul(K.ps[j % 4][:, :], K.hT[:, k, t * P:(t + 1) * P], K.ring.tile(n)[:, k, :], start=(k == 0), stop=(k == KD - 1))
                last.then_inc(S["mm"], 1)

        @block.scalar
        def _(act):
            for c in range(36):
                act.wait_ge(S["mm"], c + 1)
                ps = K.ps[c % 4][:, :]
                if c < 12:
                    ins = nc.scalar.activation(K.qa[:, c, :], ps, ACT.Copy, scale=0.125)
                elif c < 24:
                    ins = nc.scalar.activation(K.ka[:, c - 12, :], ps, ACT.Copy)
                else:
                    s, t = (c - 24) // NT, (c - 24) % NT
                    ins = nc.scalar.activation(K.va2[:, t, s * 512:(s + 1) * 512], ps, ACT.Copy)
                ins.then_inc(S["cop"], 1)

        @block.vector
        def _(dve):
            dve.memset(rb[:, :], 1.0).then_inc(S["one"], 1)
            for g in range(3):
                dve.wait_ge(S["bmm"], g + 1)
                if g:
                    dve.wait_ge(S["st"], 16 * g)
                dve.tensor_copy(R[:, 0:512], K.ps[4][0:8, :])
                dve.tensor_copy(R[:, 512:640], K.ps[5][0:8, 0:128]).then_inc(S["bcop"], 1)


def feed_forward(nc, K, n0, load_upto):
    NF = FF2 // P
    with ExitStack() as ctx:
        S = sems(nc, ctx, "mm sig gated hid down", "F")
        hid = ctx.enter_context(nc.sbuf_tensor("hid", [P, NF, T], F32))
        ups = list(range(n0, n0 + 12))
        for i in range(12):
            last = min(4 * (i // 2) + 4, NF)
            K.ring.used[n0 + i] = (S["mm"], 2 * last - (1 if i % 2 == 0 else 0))
        for i in range(6):
            K.ring.used[n0 + 12 + i] = (S["down"], i + 1)
        block = ctx.enter_context(nc.Block())

        @block.sync
        def _(sp):
            K.ring.load(sp, load_upto)

        @block.tensor
        def _(pe):
            for c in range(NF):
                cols = slice((c % 4) * P, (c % 4) * P + P)
                for j in range(2):
                    n = n0 + 2 * (c // 4) + j
                    if c % 4 == 0:
                        K.ring.wait(pe, n)
                    if c >= 4:
                        pe.wait_ge(S["hid"], c - 3)
                    mm_feature(pe, K.ps[(c % 4) * 2 + j][:, :], K.ring.tile(n), cols, K.hT, KD).then_inc(S["mm"], 1)
            pe.wait_ge(S["hid"], NF)
            for f in range(NF):
                n = n0 + 12 + f // 4
                if f % 4 == 0:
                    K.ring.wait(pe, n)
                for t in range(NT):
                    for half in range(2):
                        last = pe.matmul(K.ps[2 * t + half][:, :], hid[:, f, t * P:(t + 1) * P],
                                         K.ring.tile(n)[:, f % 4, half * 512:(half + 1) * 512], start=(f == 0), stop=(f == NF - 1))
                if f % 4 == 3 or f == NF - 1:
                    last.then_inc(S["down"], 1)

        @block.scalar
        def _(act):
            for c in range(NF):
                act.wait_ge(S["mm"], 2 * c + 1)
                nc.scalar.activation(hid[:, c, :], K.ps[(c % 4) * 2][:, :], ACT.Sigmoid).then_inc(S["sig"], 1)

        @block.vector
        def _(dve):
            for c in range(NF):
                dve.wait_ge(S["sig"], c + 1)
                dve.tensor_tensor(hid[:, c, :], hid[:, c, :], K.ps[(c % 4) * 2][:, :], ALU.mult).then_inc(S["gated"], 1)
                dve.wait_ge(S["gated"], c + 1)
                dve.wait_ge(S["mm"], 2 * c + 2)
                dve.tensor_tensor(hid[:, c, :], hid[:, c, :], K.ps[(c % 4) * 2 + 1][:, :], ALU.mult).then_inc(S["hid"], 1)
            dve.wait_ge(S["down"], 6)
            for t in range(NT):
                for half in range(2):
                    o = K.x[:, t, half * 512:(half + 1) * 512]
                    dve.tensor_tensor(o, o, K.ps[2 * t + half][:, :], ALU.add)


def build(nc, I, out):
    ctx = ExitStack()
    with ctx:
        sb = lambda n, s, dt=F32: ctx.enter_context(nc.sbuf_tensor(n, s, dt))
        K = Buffers()
        K.I = I
        K.ps = [ctx.enter_context(nc.psum_tensor(f"ps{i}", [P, 512], F32)) for i in range(8)]
        K.ring = R = Ring(nc, ctx)
        K.ident = sb("ident", [P, P])
        w_in = I["w_in"][0]
        b_first = [R.plan(w_in[:, c:min(c + 512, 2688)], KD, min(512, 2688 - c)) for c in range(0, 2688, 512)][0]
        e_first = len(R.loads)
        for c in range(0, 2 * D, 512):
            R.plan(w_in[:, 2688 + c:2688 + c + 512], KD, 512)
        R.plan(I["w_proj_rwkv"][0], 4, D)
        R.plan(I["w_proj_attn"][0], 4, D)
        for c in range(0, D, 512):
            R.plan(I["w_out"][0][:, c:c + 512], KD, 512)
        moe_first = len(R.loads)
        for e in range(N_EXP):
            for w in ("exp_w_gate", "exp_w_up", "exp_w_down"):
                for half in range(2):
                    R.plan(I[w][0, e, half * 512:half * 512 + 512, :], 4, D)
        second = len(R.loads)
        w2 = I["w_in_2"][0]
        for c0, cols in ((Q_M, 1024), (K_M, 1024), (V_M, 1024), (O_M, 1024), (Q_A, 1536), (K_A, 1536), (V_A, 1536), (G_A, 2048)):
            for c in range(c0, c0 + cols, 512):
                R.plan(w2[:, c:c + 512], KD, 512)
        for c in range(0, D, 512):
            R.plan(I["w_proj_a_2"][0][:, c:c + 512], KD, 512)
        R.plan(I["w_proj_b_2"][0], 4, D)
        for c in range(0, D, 512):
            R.plan(I["w_out_2"][0][:, c:c + 512], KD, 512)
        ffn = len(R.loads)
        for c in range(0, FF2, 512):
            w = min(512, FF2 - c)
            for name in ("w_gate_2", "w_up_2"):
                R.plan(I[name][0][:, c:c + w], KD, w)
        for f in range(0, FF2, 512):
            w = min(512, FF2 - f)
            R.plan(I["w_down_2"][0][f:f + w, :], w // P, D)
        K.x = sb("x", [P, NT, D])
        xs = I["x"][0]
        S0 = sems(nc, ctx, "consts moved")
        with ExitStack() as one:
            sb1 = lambda n, s: one.enter_context(nc.sbuf_tensor(n, s, F32))
            with nc.Block() as block:
                @block.sync
                def _(sp):
                    sp.dma_start(K.ident[:, :], I["c_ident"]).then_inc(S0["consts"], 16)
                    sp.wait_ge(S0["consts"], 16)
            K.hT = sb1("hT", [P, KD, T])
            K.yaT = sb1("yaT", [P, 4, T])
            K.u = sb1("u", [P, RC, T])
            with ExitStack() as att:
                norm_transposed(nc, K, "1", K.x, I["norm_mix_g"][0], K.x, K.hT, xs, RING)
                sb2 = lambda n, s: att.enter_context(nc.sbuf_tensor(n, s, F32))
                K.qT, K.kT, K.va = sb2("qT", [P, 4, T]), sb2("kT", [P, 2, T]), sb2("va", [P, NT, P])
                K.sink = sb2("sink", [P, A_HEADS])
                first_projection(nc, K, b_first)
                K.absrel = sb2("absrel", [P, 3 * P])
                ya = sb2("ya", [P, NT, 512])
                with nc.Block() as block:
                    @block.sync
                    def _(sp):
                        sp.dma_start(K.absrel[:, :], I["c_absrel"]).then_inc(S0["consts"], 16)
                        sp.wait_ge(S0["consts"], 32)
                items = []
                for n in range(NT):
                    lo, hi = max(n - 1, 0), min(n + 1, NT - 1)
                    for h in range(A_HEADS):
                        b, g = 64 * (h % 2), h // 4
                        w = (hi - lo + 1) * P
                        r0 = (lo - (n - 1)) * P
                        items.append(dict(
                            segs=[(K.qT[b:b + 64, h // 2, n * P:(n + 1) * P], K.kT[b:b + 64, g, lo * P:(hi + 1) * P], w,
                                   K.absrel[:, r0:r0 + w], -(2.0 ** (-8.0 * (h + 1) / A_HEADS)))],
                            values=[K.va[:, kb, 64 * g:64 * g + 64] for kb in range(lo, hi + 1)],
                            sink=K.sink[:, h:h + 1], at=ya[:, n, 64 * h:64 * h + 64]))
                attention(nc, K, "A", items, ya, 3 * P, K.yaT)
            with ExitStack() as rw:
                sb2 = lambda n, s: rw.enter_context(nc.sbuf_tensor(n, s, F32))
                K.par = sb2("par", [P, 10, 4])
                K.wup, K.aup, K.gup = sb2("wup", [P, RW]), sb2("aup", [P, RW]), sb2("gup", [P, RW])
                K.masks, K.masks_t = sb2("masks", [P, 2, 2, P]), sb2("masks_t", [P, 2, 64])
                K.heads1, K.chunk0 = sb2("heads1", [P, P]), sb2("chunk0", [P, T])
                K.kk, K.ksum = sb2("kk", [P, 2, T]), sb2("ksum", [P, 2, T])
                K.SV = sb2("SV", [P, NCH, 2, 2, 64])
                K.Y = sb2("Y", [P, NCH, 2, 64])
                K.AR, K.BK = sb2("AR", [P, 2, NCH, 2, CHUNK]), sb2("BK", [P, 2, NCH, 2, CHUNK])
                K.DC = sb2("DC", [P, 2, NCH])
                K.tmp = [K.x[:, i, :].rearrange("p (c t) -> p c t", c=2) for i in range(4)]
                rwkv_setup(nc, K)
                for hf in range(2):
                    rwkv_keys(nc, K, hf)
                    for d in range(2):
                        rwkv_decays(nc, K, hf, d)
                        rwkv_chunks(nc, K, hf, d)
                    rwkv_output(nc, K, hf)
            K.yrT = K.u[:, 0:4, :]
            with nc.Block() as block:
                @block.sync
                def _(sp):
                    for t in range(NT):
                        sp.dma_start(K.x[:, t, :], xs[t * P:(t + 1) * P, :]).then_inc(S0["consts"], 16)
                    sp.wait_ge(S0["consts"], 32 + 16 * NT)
            merge_branches(nc, K, "E", [e_first + i for i in range(4)],
                           [(K.yrT, 4, [e_first + 4]), (K.yaT, 4, [e_first + 5])], [e_first + 6, e_first + 7], None, moe_first + RING)
            K.x1 = K.x
        with ExitStack() as moe:
            sb1 = lambda n, s: moe.enter_context(nc.sbuf_tensor(n, s, F32))
            K.xn = sb1("xn", [P, NT, D])
            K.IB = sb1("IB", [P, N_EXP, 256])
            K.tok, K.gf = sb1("tok", [P, NT]), sb1("gf", [P, KD])
            with nc.sbuf_tensor("hT2", [P, KD, T], F32) as K.hT:
                norm_transposed(nc, K, "2", K.x, I["norm_ffn_g"][0], K.xn, K.hT)
                route(nc, K)
            experts(nc, K, moe_first, second + RING)
            K.x2 = K.x
        x3 = nc.dram_tensor("x3_dram", (T, D), F32, kind="Internal").ap()
        K.R_dram = nc.dram_tensor("bias_dram", (3, G2_HEADS, 640), F32, kind="Internal").ap()
        gain_norm(nc, K, "G1", I["norm_final_g"], keep_dram=x3)
        with ExitStack() as two:
            sb1 = lambda n, s: two.enter_context(nc.sbuf_tensor(n, s, F32))
            K.hT = sb1("hT3", [P, KD, T])
            norm_transposed(nc, K, "3", K.x, I["norm_mix_g_2"][0], K.x, K.hT)
            K.hm = K.x[:, :, :].rearrange("p t (h d) -> p t h d", h=M_HEADS)
            with ExitStack() as ml:
                sb2 = lambda n, s: ml.enter_context(nc.sbuf_tensor(n, s, F32))
                K.qmT, K.kmT = sb2("qmT", [P, KD, T]), sb2("kmT", [P, KD, T])
                K.vm = sb2("vm", [P, NT, M_HEADS, M_DH + 1])
                K.MB, K.WI = sb2("MB", [P, M_HEADS, T]), sb2("WI", [P, M_HEADS, T])
                K.cols, K.dec = sb2("cols", [P, 3, 16]), sb2("dec", [P, 16])
                K.sel4, K.causal = sb2("sel4", [4, 4, P]), sb2("causal", [P, P])
                mlstm_inputs(nc, K, second, second + 6 + RING)
                mlstm_cell(nc, K)
                K.ymT = K.qmT
                mlstm_output(nc, K, second + 6, second + 8 + RING)
                with nc.Block() as block:
                    @block.vector
                    def _(dve):
                        dve.tensor_copy(K.x[:, :, :].rearrange("p t (a b) -> p (t a) b", a=2), K.ymT[:, :, :])
            K.ymT = K.x[:, :, :].rearrange("p t (a b) -> p (t a) b", a=2)
            BT = sb1("BT", [P, 2, 1280])
            K.ybT = BT[:, :, :].rearrange("p a b -> p (a b)")[:, 0:4 * T].rearrange("p (c t) -> p c t", c=4)
            with ExitStack() as at:
                sb2 = lambda n, s: at.enter_context(nc.sbuf_tensor(n, s, F32))
                K.qa, K.ka, K.va2 = sb2("qa", [P, 12, T]), sb2("ka", [P, 12, T]), sb2("va2", [P, NT, 1536])
                K.flip = sb2("flip", [P, P])
                second_attention_inputs(nc, K, second + 8, second + 17 + RING)
                yb = sb2("yb", [P, NT, 512])
                items = []
                for h in range(G2_HEADS):
                    for n in range(NT):
                        segs, vals = [], []
                        for g, (lo, c0, w0) in enumerate(((max(n - 1, 0), 0, 256), (0, 256, 512), (0, 768, 512))):
                            ch, b = 4 * g + h // 2, 64 * (h % 2)
                            w = (n + 1 - lo) * P
                            segs.append((K.qa[b:b + 64, ch, n * P:(n + 1) * P], K.ka[b:b + 64, ch, lo * P:(n + 1) * P], w,
                                         BT[:, h % 2, c0 + w0 - w:c0 + w0], 1.0))
                            vals += [K.va2[:, kb, 512 * g + 64 * h:512 * g + 64 * h + 64] for kb in range(lo, n + 1)]
                        items.append(dict(segs=segs, values=vals, sink=None, at=yb[:, n, 64 * h:64 * h + 64]))
                attention(nc, K, "B", items, yb, 1280, K.ybT, flips=BT)
            K.yaT2 = K.ymT
            with ExitStack() as mg:
                ym = mg.enter_context(nc.sbuf_tensor("ym2", [P, KD, T], F32))
                with nc.Block() as block:
                    @block.vector
                    def _(dve):
                        dve.tensor_copy(ym[:, :, :], K.ymT).then_inc(S0["moved"], 1)
                    @block.sync
                    def _(sp):
                        sp.wait_ge(S0["moved"], 1)
                        for t in range(NT):
                            sp.dma_start(K.x[:, t, :], x3[t * P:(t + 1) * P, :]).then_inc(S0["consts"], 16)
                        sp.wait_ge(S0["consts"], 32 + 32 * NT)
                merge_branches(nc, K, "H", [second + 17 + i for i in range(4)],
                               [(ym, KD, [second + 21, second + 22]), (K.ybT, 4, [second + 23])],
                               [second + 24, second + 25], None, ffn + RING)
            K.x4 = K.x
            with nc.sbuf_tensor("xn4", [P, NT, D], F32) as xn4:
                norm_transposed(nc, K, "4", K.x, I["norm_ffn_g_2"][0], xn4, K.hT)
            feed_forward(nc, K, ffn, 10 ** 6)
        gain_norm(nc, K, "G2", I["norm_final_g_2"], out_dram=out)


def constants():
    rel = np.arange(3 * P)[None, :] - P - np.arange(P)[:, None]
    absrel = np.where(np.abs(rel) <= P, np.abs(rel), 1e33).astype(np.float32)
    s, t = np.arange(CHUNK)[:, None], np.arange(CHUNK)[None, :]
    masks, masks_t = np.zeros((P, 2, 2, P), np.float32), np.zeros((P, 2, CHUNK), np.float32)
    for d, (before, through) in enumerate(((s < t, s <= t), (s > t, s >= t))):
        for odd in range(2):
            b, k = slice(CHUNK * odd, CHUNK * odd + CHUNK), slice(CHUNK - CHUNK * odd, P - CHUNK * odd)
            masks[b, odd, d] = np.concatenate([-1.0 * before, 1.0 * through], 1)
            masks[k, odd, d] = np.concatenate([1.0 * before, 1.0 * through], 1)
            masks_t[b, d] = -1.0 * before.T
    heads1 = (np.arange(P)[:, None] // 64 == np.arange(P)[None, :] // 64).astype(np.float32)
    chunk0 = np.broadcast_to((np.arange(T) % CHUNK != 0).astype(np.float32), (P, T))
    reset = np.zeros((M_HEADS, 2, T), np.float32)
    reset[:, 0] = np.arange(T) % P != 0
    causal = (np.arange(P)[:, None] <= np.arange(P)[None, :]).astype(np.float32)
    dist = np.zeros((33, 3, 640), np.float32)
    for g, (window, dilation) in enumerate(WINDOWS):
        for r in range(640):
            n = 511 - r
            if n < 0 or n > window or n % dilation:
                dist[32, g, r] = -1e30
            else:
                large = 16 + int(np.float32(np.log(max(n, 16) / 16)) / np.float32(np.log(2048 / 16)) * np.float32(16))
                dist[n if n < 16 else min(large, 31), g, r] = 1.0
    return {"c_reset": reset, "c_causal": causal, "c_dist": dist, "c_flip": np.ascontiguousarray(np.eye(P, dtype=np.float32)[::-1]),
            "c_sel4": np.repeat(np.eye(M_HEADS, dtype=np.float32)[:, :, None], P, 2),
            "c_ident": np.eye(P, dtype=np.float32), "c_absrel": absrel, "c_masks": masks, "c_masks_t": masks_t,
            "c_sel": np.repeat(np.eye(N_EXP, dtype=np.float32)[:, :, None], P, 2),
            "c_tok": (np.arange(P)[:, None] + P * np.arange(NT)[None, :]).astype(np.float32),
            "c_heads1": heads1, "c_chunk0": chunk0}


_INS = ["x", "norm_mix_g", "w_in", "mu_prev", "mu_next", "w0_f", "w_up_f", "w0_b", "w_up_b", "a0_f", "a_up_f", "a0_b",
        "a_up_b", "g_up", "k_k", "k_a", "r_k", "ln_x_w", "ln_x_b", "attn_sink", "w_proj_rwkv", "w_proj_attn", "w_out",
        "norm_ffn_g", "w_router", "exp_w_gate", "exp_w_up", "exp_w_down", "norm_final_g", "norm_mix_g_2", "w_in_2",
        "b_gate_if_2", "conv_w_2", "conv_b_2", "mlstm_norm_g_2", "w_proj_a_2", "w_proj_b_2", "w_out_2",
        "norm_ffn_g_2", "w_gate_2", "w_up_2", "w_down_2", "rel_bias_2", "norm_final_g_2"]


def kernel(**inputs):
    import numpy as _np
    import concourse.bacc as _bacc
    from concourse.bass_utils import run_bass_kernel_spmd as _run

    nc = _bacc.Bacc("TRN2", target_bir_lowering=False, num_devices=1)
    arrays, aps = {}, {}
    for name, a in [(n, inputs[n]) for n in _INS] + list(constants().items()):
        a = _np.ascontiguousarray(a)
        arrays["in_" + name] = a
        aps[name] = nc.dram_tensor("in_" + name, a.shape, F32, kind="ExternalInput").ap()
    out = nc.dram_tensor("out_0", (1, T, D), F32, kind="ExternalOutput").ap()
    build(nc, aps, out[0])
    return _run(nc, [arrays], core_ids=[0]).results[0]["out_0"]
```

```python
import numpy as np
from contextlib import ExitStack

import concourse.bass as bass
from concourse import mybir

F32 = mybir.dt.float32
U32 = mybir.dt.uint32
I32 = mybir.dt.int32
F32R = mybir.dt.float32r
ALU = mybir.AluOpType
ACT = mybir.ActivationFunctionType
AX = mybir.AxisListType.X

P = 128
T = 512
D = 1024
NT = T // P
KD = D // P
EPS = 1e-6

R_HEADS, R_N = 8, 64
RW = R_HEADS * R_N
RWKV_COLS = 3 * RW + 128 + 4 * 64
RC = RWKV_COLS // P
CHUNK = 64
NCH = T // CHUNK
DECAY = float(np.exp(-0.5))
LNX_EPS = 64e-5
A_HEADS, A_DH = 8, 64
N_EXP, CAP, FF1 = 16, 64, 1024

M_HEADS, M_DH = 4, 256
G2_HEADS = 8
WINDOWS = ((128, 1), (512, 4), (2048, 16))
Q_M, K_M, V_M, IF_M = 0, 1024, 2048, 3072
O_M = IF_M + 2 * M_HEADS
Q_A = O_M + 1024
K_A = Q_A + 1536
V_A = K_A + 1536
G_A = V_A + 1536
FF2 = 2816

RING = 4
PAIR = 2
SLOT = KD * 512



def twins(nc, ctx, name, shape):
    at = -(-nc.sbuf_base // 32) * 32
    whole = ctx.enter_context(nc.sbuf_tensor(name, shape, F32))
    return whole, nc.alloc_sbuf_tensor_at(name + "_parts", shape, F32R, offset=at)


def high(dve, out, x):
    return dve.tensor_copy(out, x)


def low(dve, out, x, hi):
    return dve.tensor_tensor(out, x, hi.bitcast(F32), ALU.subtract)


def product(pe, ps, w, h, start, stop):
    (wh, wl), (hh, hl) = w, h
    pe.matmul(ps, wh, hh, start=start, stop=False)
    pe.matmul(ps, wh, hl, start=False, stop=False)
    return pe.matmul(ps, wl, hh, start=False, stop=stop)


class Ring:

    def __init__(self, nc, ctx):
        self.buf, self.parts = twins(nc, ctx, "ring", [P, RING, SLOT])
        self.full = [ctx.enter_context(nc.semaphore(f"ring_full{i}")) for i in range(RING)]
        self.ready = ctx.enter_context(nc.semaphore("ring_ready"))
        self.rounded = ctx.enter_context(nc.semaphore("ring_rounded"))
        self.loads, self.slots, self.landed, self.pieces = [], [], [], []
        self.count = [0] * RING
        self.total = 0
        self.issued = 0
        self.used = {}

    def place(self, src, k, w, slot):
        self.count[slot] += 16
        self.loads.append((src, k, w))
        self.slots.append(slot)
        self.landed.append(self.count[slot])
        return len(self.loads) - 1

    def plan(self, src, k, w, rows=False):
        n = self.place(src, k, w, len(self.loads) % PAIR)
        num = min(4, k) if rows else min(4, w // P)
        step = (k if rows else w) // num
        cut = [(slice(i * step, (i + 1) * step), slice(0, w)) if rows else (slice(0, k), slice(i * step, (i + 1) * step))
               for i in range(num)]
        self.pieces.append((self.total, cut))
        self.total += num
        return n

    def plan_whole(self, src, k, w, j):
        self.pieces.append(None)
        return self.place(src, k, w, j % RING)

    def view(self, n, buf, slot):
        _, k, w = self.loads[n]
        return buf[:, slot, 0:k * w].rearrange("p (k w) -> p k w", k=k)

    def cut(self, n, k, cols):
        s = self.slots[n]
        return self.view(n, self.parts, PAIR + s)[:, k, cols], self.view(n, self.parts, s)[:, k, cols]

    def load(self, eng, upto):
        for n in range(self.issued, min(upto, len(self.loads))):
            last = n - PAIR if self.pieces[n] or self.pieces[n - PAIR] else n - 2 * PAIR
            if last in self.used:
                eng.wait_ge(*self.used[last])
            src, k, w = self.loads[n]
            eng.dma_start(self.view(n, self.buf, self.slots[n]), src.rearrange("(k p) w -> p k w", p=P)).then_inc(self.full[self.slots[n]], 16)
            self.issued = n + 1

    def split(self, dve, n):
        s = self.slots[n]
        first, cut = self.pieces[n]
        dve.wait_ge(self.full[s], self.landed[n])
        if n - PAIR in self.used:
            dve.wait_ge(*self.used[n - PAIR])
        whole, hi, lo = self.view(n, self.buf, s), self.view(n, self.parts, PAIR + s), self.view(n, self.parts, s)
        for i in range(len(cut) + 1):
            if i < len(cut):
                k, w = cut[i]
                high(dve, hi[:, k, w], whole[:, k, w]).then_inc(self.rounded, 1)
            if i:
                k, w = cut[i - 1]
                dve.wait_ge(self.rounded, first + i)
                low(dve, lo[:, k, w], whole[:, k, w], hi[:, k, w]).then_inc(self.ready, 1)

    def wait(self, pe, n, piece=None):
        first, cut = self.pieces[n]
        pe.wait_ge(self.ready, first + (len(cut) if piece is None else piece + 1))


def sems(nc, ctx, names, tag=""):
    made = {n: nc.alloc_semaphore(name=n + tag) for n in names.split()}

    def clear():
        for handle in made.values():
            nc.gpsimd.sem_clear(handle)
            nc.release_semaphore(handle)
    ctx.callback(clear)
    return made


class Buffers:
    pass


def linker(eng, sem):
    count = [0]

    def link(ins):
        count[0] += 1
        ins.then_inc(sem, 1)
        eng.wait_ge(sem, count[0])
    return link


def norm_transposed(nc, K, tag, x, g, xn, hT, x_src=None, load_upto=0, parts=None):
    K.ring.used = {}
    with ExitStack() as ctx:
        S = sems(nc, ctx, "x_in g_in squared var_ok root_ok rec_ok xn_ok turned emptied highs", tag)
        sq = ctx.enter_context(nc.sbuf_tensor("sq" + tag, [P, D], F32))
        ss = ctx.enter_context(nc.sbuf_tensor("ss" + tag, [P, 4 * NT], F32))
        gc = ctx.enter_context(nc.sbuf_tensor("gc" + tag, [P, KD], F32))
        block = ctx.enter_context(nc.Block())

        def empty(eng, b):
            t, half = b // 2, b % 2
            eng.wait_ge(S["turned"], b + 1)
            for c in range(4):
                k = half * 4 + c
                o, ps = hT[:, k, t * P:(t + 1) * P], K.ps[b % 4][:, c * P:(c + 1) * P]
                if parts:
                    last = nc.scalar.activation(o, ps, ACT.Copy, scale=gc[:, k:k + 1])
                else:
                    last = eng.tensor_scalar(o, ps, gc[:, k:k + 1], None, ALU.mult)
            last.then_inc(S["emptied"], 1)

        @block.sync
        def _(sp):
            if x_src is not None:
                for t in range(NT):
                    sp.dma_start(x[:, t, :], x_src[t * P:(t + 1) * P, :]).then_inc(S["x_in"], 16)
            with nc.allow_non_contiguous_dma(reason="one gain per partition"):
                sp.dma_start(gc[:, :], g.rearrange("(k p) -> p k", p=P)).then_inc(S["g_in"], 16)
            K.ring.load(sp, load_upto)
            sp.wait_ge(S["g_in"], 16)

        @block.scalar
        def _(act):
            if x_src is not None:
                act.wait_ge(S["x_in"], 16 * NT)
            for t in range(NT):
                if t:
                    act.wait_ge(S["squared"], t)
                nc.scalar.activation(sq[:, :], x[:, t, :], ACT.Square, accum_out=ss[:, t:t + 1]).then_inc(S["squared"], 1)
            act.wait_ge(S["var_ok"], 1)
            nc.scalar.activation(ss[:, 2 * NT:3 * NT], ss[:, NT:2 * NT], ACT.Sqrt).then_inc(S["root_ok"], 1)
            act.wait_ge(S["rec_ok"], 1)
            for t in range(NT):
                nc.scalar.activation(xn[:, t, :], x[:, t, :], ACT.Copy, scale=ss[:, 3 * NT + t:3 * NT + t + 1]).then_inc(S["xn_ok"], 1)
            if parts:
                act.wait_ge(S["g_in"], 16)
                for b in range(NT * 2):
                    empty(act, b)

        @block.vector
        def _(dve):
            dve.wait_ge(S["squared"], NT)
            dve.tensor_scalar(ss[:, NT:2 * NT], ss[:, 0:NT], 1.0 / D, EPS, ALU.mult, ALU.add).then_inc(S["var_ok"], 1)
            dve.wait_ge(S["root_ok"], 1)
            dve.reciprocal(ss[:, 3 * NT:4 * NT], ss[:, 2 * NT:3 * NT]).then_inc(S["rec_ok"], 1)
            if not parts:
                dve.wait_ge(S["g_in"], 16)
                for b in range(NT * 2):
                    empty(dve, b)
            else:
                hi, lo = parts
                for b in range(NT * 2):
                    t, half = b // 2, b % 2
                    at = (slice(None), slice(4 * half, 4 * half + 4), slice(t * P, (t + 1) * P))
                    dve.wait_ge(S["emptied"], b + 1)
                    high(dve, hi[at], hT[at]).then_inc(S["highs"], 1)
                    dve.wait_ge(S["highs"], b + 1)
                    low(dve, lo[at], hT[at], hi[at])

        @block.tensor
        def _(pe):
            for b in range(NT * 2):
                t, half = b // 2, b % 2
                pe.wait_ge(S["xn_ok"], t + 1)
                if b >= 4:
                    pe.wait_ge(S["emptied"], b - 3)
                for c in range(4):
                    k = half * 4 + c
                    last = pe.transpose(K.ps[b % 4][:, c * P:(c + 1) * P], xn[:, t, k * P:(k + 1) * P], K.ident[:, :])
                last.then_inc(S["turned"], 1)


def mm_feature(pe, ps, w, cols, hT, nk):
    ring, n = w
    for k in range(nk):
        last = product(pe, ps, ring.cut(n, k, cols), [t[:, k, :] for t in hT], k == 0, k == nk - 1)
    return last


def mm_tokens(pe, ps, w, cols, hT, nk, t):
    ring, n = w
    for k in range(nk):
        if t == 0:
            ring.wait(pe, n, k * len(ring.pieces[n][1]) // nk)
        last = product(pe, ps, [x[:, k, t * P:(t + 1) * P] for x in hT], ring.cut(n, k, cols), k == 0, k == nk - 1)
    return last


def attention(nc, K, tag, items, out, width, outT, flips=None):
    with ExitStack() as ctx:
        S = sems(nc, ctx, "scored biased maxed exped turned copied pved y_done chain o_turned o_copied flip_in0 flip_in1 flipped unflipped", tag)
        scored, biased, maxed, exped, turned = S["scored"], S["biased"], S["maxed"], S["exped"], S["turned"]
        copied, pved, y_done, chain, o_turned = S["copied"], S["pved"], S["y_done"], S["chain"], S["o_turned"]
        sbt = lambda n, s: ctx.enter_context(nc.sbuf_tensor(n + tag, s, F32))
        SB = 3
        if flips is None:
            Sb, PT = sbt("Sb", [P, SB, width]), sbt("PT", [P, 2, width])
        else:
            Sb, PT = (K.ring.buf[:, PAIR + i, 0:n * width].rearrange("p (s w) -> p s w", s=n) for i, n in ((0, SB), (1, 2)))
        N = len(items)
        nm, mx, den, rd, esk = (sbt(n, [P, N]) for n in ("anm", "amx", "aden", "ard", "aesk"))
        seg0, bank0 = [0], [0]
        for it in items:
            seg0.append(seg0[-1] + len(it["segs"]))
            bank0.append(bank0[-1] + -(-len(it["values"]) // 4))
        ps_s, ps_f, ps_t, ps_v = K.ps[0:3], K.ps[3], K.ps[4:6], K.ps[6:8]
        flip_segs = ((0, 256), (256, 512), (768, 512))
        block = ctx.enter_context(nc.Block())
        nout = out.shape[2] // P

        def key_blocks(i, b):
            return range(4 * b, min(4 * b + 4, len(items[i]["values"])))

        @block.sync
        def _(sp):
            if flips is None:
                return
            for h in range(G2_HEADS):
                if h >= 2:
                    sp.wait_ge(biased, seg0[NT * (h - 1)])
                for g, (c0, w) in enumerate(flip_segs):
                    base = K.R_dram[g, h:h + 1, 512 - w:512]
                    src = bass.AP(tensor=base.tensor, offset=base.offset, ap=[[1, P], [1, w]])
                    sp.dma_start(flips[:, h % 2, c0:c0 + w], src).then_inc((S["flip_in0"], S["flip_in1"])[h % 2], 16)

        @block.tensor
        def _(pe):
            def flip(h, g):
                pe.wait_ge((S["flip_in0"], S["flip_in1"])[h % 2], 48 * (h // 2 + 1))
                if h or g:
                    pe.wait_ge(S["unflipped"], 3 * h + g)
                c0, w = flip_segs[g]
                pe.matmul(ps_f[:, 0:w], K.flip[:, :], flips[:, h % 2, c0:c0 + w], start=True, stop=True).then_inc(S["flipped"], 1)

            if flips is not None:
                for g in range(3):
                    flip(0, g)
            for i in range(N + 2):
                if i < N:
                    for j, (q, k, w, _, _) in enumerate(items[i]["segs"]):
                        g = seg0[i] + j
                        if g >= 3:
                            pe.wait_ge(biased, g - 2)
                        pe.matmul(ps_s[g % 3][:, 0:w], q, k, start=True, stop=True).then_inc(scored, 1)
                if flips is not None and i % NT and i // NT + 1 < G2_HEADS:
                    flip(i // NT + 1, i % NT - 1)
                if 1 <= i <= N:
                    pe.wait_ge(exped, i)
                    for b in range(bank0[i] - bank0[i - 1]):
                        g = bank0[i - 1] + b
                        if g >= 2:
                            pe.wait_ge(copied, g - 1)
                        for n, kb in enumerate(key_blocks(i - 1, b)):
                            last = pe.transpose(ps_t[g % 2][:, n * P:(n + 1) * P],
                                                Sb[:, (i - 1) % SB, kb * P:(kb + 1) * P], K.ident[:, :])
                        last.then_inc(turned, 1)
                if i >= 2:
                    j = i - 2
                    pe.wait_ge(copied, bank0[j + 1])
                    if j >= 2:
                        pe.wait_ge(y_done, j - 1)
                    vs = items[j]["values"]
                    for kb, v in enumerate(vs):
                        last = pe.matmul(ps_v[j % 2][:, 0:64], PT[:, j % 2, kb * P:(kb + 1) * P], v,
                                         start=(kb == 0), stop=(kb == len(vs) - 1))
                    last.then_inc(pved, 1)
            pe.wait_ge(y_done, N)
            for c in range(nout):
                if c >= 3:
                    pe.wait_ge(S["o_copied"], c - 2)
                for t in range(NT):
                    last = pe.transpose(ps_s[c % 3][:, t * P:(t + 1) * P], out[:, t, c * P:(c + 1) * P], K.ident[:, :])
                last.then_inc(o_turned, 1)

        @block.scalar
        def _(act):
            def unflip(h, g):
                act.wait_ge(S["flipped"], 3 * h + g + 1)
                c0, w = flip_segs[g]
                nc.scalar.activation(flips[:, h % 2, c0:c0 + w], ps_f[:, 0:w], ACT.Copy).then_inc(S["unflipped"], 1)

            if flips is not None:
                for g in range(3):
                    unflip(0, g)
            for i in range(N + 1):
                if flips is not None and i % NT and i // NT + 1 < G2_HEADS:
                    unflip(i // NT + 1, i % NT - 1)
                if i < N:
                    w = sum(s[2] for s in items[i]["segs"])
                    act.wait_ge(maxed, i + 1)
                    last = nc.scalar.activation(Sb[:, i % SB, 0:w], Sb[:, i % SB, 0:w], ACT.Exp,
                                                bias=nm[:, i:i + 1], accum_out=den[:, i:i + 1])
                    if items[i]["sink"] is not None:
                        last = nc.scalar.activation(esk[:, i:i + 1], nm[:, i:i + 1], ACT.Exp, bias=items[i]["sink"])
                    last.then_inc(exped, 1)
                if i >= 1:
                    j = i - 1
                    if j >= 2:
                        act.wait_ge(pved, j - 1)
                    for b in range(bank0[j + 1] - bank0[j]):
                        g = bank0[j] + b
                        act.wait_ge(turned, g + 1)
                        kb = key_blocks(j, b)
                        nc.scalar.activation(PT[:, j % 2, kb[0] * P:(kb[-1] + 1) * P],
                                             ps_t[g % 2][:, 0:len(kb) * P], ACT.Copy).then_inc(copied, 1)
            for c in range(nout):
                act.wait_ge(o_turned, c + 1)
                nc.scalar.activation(outT[:, c, :], ps_s[c % 3][:, :], ACT.Copy).then_inc(S["o_copied"], 1)

        @block.vector
        def _(dve):
            link = linker(dve, chain)
            for i in range(N + 2):
                if i < N:
                    if flips is not None:
                        dve.wait_ge(S["unflipped"], 3 * (i // NT + 1))
                    if i >= SB:
                        dve.wait_ge(turned, bank0[i - SB + 1])
                    c0 = 0
                    for j, (q, k, w, bias, scale) in enumerate(items[i]["segs"]):
                        g = seg0[i] + j
                        dve.wait_ge(scored, g + 1)
                        o = Sb[:, i % SB, c0:c0 + w]
                        dve.scalar_tensor_tensor(out=o, in0=bias, scalar=scale, in1=ps_s[g % 3][:, 0:w],
                                                 op0=ALU.mult, op1=ALU.add).then_inc(biased, 1)
                        c0 += w
                    dve.wait_ge(biased, seg0[i + 1])
                    if items[i]["sink"] is not None:
                        link(dve.tensor_reduce(mx[:, i:i + 1], Sb[:, i % SB, 0:c0], AX, ALU.max))
                        dve.tensor_scalar(nm[:, i:i + 1], mx[:, i:i + 1], items[i]["sink"], -1.0,
                                          ALU.max, ALU.mult).then_inc(maxed, 1)
                    else:
                        dve.tensor_reduce(nm[:, i:i + 1], Sb[:, i % SB, 0:c0], AX, ALU.max, negate=True).then_inc(maxed, 1)
                if i >= 2:
                    j = i - 2
                    dve.wait_ge(exped, j + 1)
                    d = den[:, j:j + 1]
                    if items[j]["sink"] is not None:
                        link(dve.tensor_tensor(esk[:, j:j + 1], esk[:, j:j + 1], d, ALU.add))
                        d = esk[:, j:j + 1]
                    link(dve.reciprocal(rd[:, j:j + 1], d))
                    dve.wait_ge(pved, j + 1)
                    dve.tensor_scalar(items[j]["at"], ps_v[j % 2][:, 0:64], rd[:, j:j + 1], None,
                                      ALU.mult).then_inc(y_done, 1)


def first_projection(nc, K, first):
    I = K.I
    nch = 21
    with ExitStack() as ctx:
        S = sems(nc, ctx, "bmm bmu bc0 bscaled bprev bevac")
        mu = ctx.enter_context(nc.sbuf_tensor("mu", [P, 3, RC], F32))
        K.ring.used = {first + i: (S["bmm"], min(4 * i + 4, nch)) for i in range(6)}
        block = ctx.enter_context(nc.Block())

        @block.sync
        def _(sp):
            with nc.allow_non_contiguous_dma(reason="one mixing weight per partition"):
                sp.dma_start(mu[:, 0, :], I["mu_prev"][0].rearrange("(c p) -> p c", p=P)).then_inc(S["bmu"], 16)
                sp.dma_start(mu[:, 1, :], I["mu_next"][0].rearrange("(c p) -> p c", p=P)).then_inc(S["bmu"], 16)
                sp.dma_start(K.sink[:, :], I["attn_sink"].to_broadcast([P, A_HEADS])).then_inc(S["bmu"], 16)
            K.ring.load(sp, first + 5 + PAIR)
            sp.wait_ge(S["bscaled"], 20)
            sp.dma_start(K.kT[64:128, 0, :], K.kT[0:64, 0, :]).then_inc(S["bmu"], 16)
            sp.dma_start(K.kT[0:64, 1, :], K.kT[64:128, 1, :]).then_inc(S["bmu"], 16)
            K.ring.load(sp, first + 6 + PAIR)
            sp.wait_ge(S["bmu"], 80)

        @block.tensor
        def _(pe):
            for c in range(nch):
                n = first + c // 4
                K.ring.wait(pe, n, c % 4)
                if c >= 4:
                    pe.wait_ge(S["bevac"] if c - 4 < RC else S["bscaled"], c - 3)
                w = K.ring, n
                ps = K.ps[c % 4]
                cw = (c % 4) * P
                if c < 20:
                    last = mm_feature(pe, ps[:, :], w, slice(cw, cw + P), K.hp, KD)
                else:
                    for t in range(NT):
                        last = mm_tokens(pe, ps[:, t * P:(t + 1) * P], w, slice(0, P), K.hp, KD, t)
                last.then_inc(S["bmm"], 1)

        @block.scalar
        def _(act):
            act.wait_ge(S["bc0"], 2)
            for c in range(nch):
                act.wait_ge(S["bmm"], c + 1)
                ps = K.ps[c % 4]
                if c < RC:
                    nc.scalar.activation(K.u[:, c, :], ps[:, :], ACT.Copy, scale=mu[:, 2, c:c + 1]).then_inc(S["bscaled"], 1)
                elif c < 19:
                    nc.scalar.activation(K.qT[:, c - RC, :], ps[:, :], ACT.Copy, scale=A_DH ** -0.5).then_inc(S["bscaled"], 1)
                elif c == 19:
                    nc.scalar.activation(K.kT[0:64, 0, :], ps[0:64, :], ACT.Copy)
                    nc.scalar.activation(K.kT[64:128, 1, :], ps[64:128, :], ACT.Copy).then_inc(S["bscaled"], 1)
                else:
                    nc.scalar.activation(K.va[:, :, :], ps[:, :].rearrange("p (t d) -> p t d", t=NT), ACT.Copy).then_inc(S["bscaled"], 1)

        @block.vector
        def _(dve):
            K.ring.split(dve, first)
            dve.wait_ge(S["bmu"], 48)
            dve.tensor_tensor(mu[:, 2, :], mu[:, 0, :], mu[:, 1, :], ALU.add).then_inc(S["bc0"], 1)
            dve.wait_ge(S["bc0"], 1)
            dve.tensor_scalar(mu[:, 2, :], mu[:, 2, :], -1.0, 1.0, ALU.mult, ALU.add).then_inc(S["bc0"], 1)
            K.ring.split(dve, first + 1)
            for c in range(nch):
                if c % 4 == 1 and 4 < c:
                    K.ring.split(dve, first + c // 4 + 1)
                if c >= RC:
                    continue
                dve.wait_ge(S["bscaled"], c + 1)
                u, ps = K.u[:, c, :], K.ps[c % 4]
                dve.scalar_tensor_tensor(out=u[:, 1:T], in0=ps[:, 0:T - 1], scalar=mu[:, 0, c:c + 1], in1=u[:, 1:T],
                                         op0=ALU.mult, op1=ALU.add).then_inc(S["bprev"], 1)
                dve.wait_ge(S["bprev"], c + 1)
                dve.scalar_tensor_tensor(out=u[:, 0:T - 1], in0=ps[:, 1:T], scalar=mu[:, 1, c:c + 1],
                                         in1=u[:, 0:T - 1], op0=ALU.mult, op1=ALU.add).then_inc(S["bevac"], 1)


def rwkv_setup(nc, K):
    I = K.I
    with ExitStack() as ctx:
        S = sems(nc, ctx, "rpar rth")
        block = ctx.enter_context(nc.Block())
        cols = "w0_f w0_b a0_f a0_b k_k k_a k_a r_k ln_x_w ln_x_b".split()

        @block.sync
        def _(sp):
            n = 0
            with nc.allow_non_contiguous_dma(reason="one parameter per partition"):
                for j, name in enumerate(cols):
                    src = I[name][0] if name != "r_k" else I[name][0].rearrange("h n -> (h n)")
                    sp.dma_start(K.par[:, j, :], src.rearrange("(c p) -> p c", p=P)).then_inc(S["rpar"], 16)
            for dst, src in ((K.wup[0:64, :], I["w_up_f"][0]), (K.wup[64:128, :], I["w_up_b"][0]),
                             (K.aup[0:64, :], I["a_up_f"][0]), (K.aup[64:128, :], I["a_up_b"][0]),
                             (K.gup[:, :], I["g_up"][0]), (K.masks[:, :, :, :], I["c_masks"]),
                             (K.masks_t[:, :, :], I["c_masks_t"]), (K.heads1[:, :], I["c_heads1"]),
                             (K.chunk0[:, :], I["c_chunk0"])):
                sp.dma_start(dst, src).then_inc(S["rpar"], 16)
            sp.wait_ge(S["rpar"], 16 * (len(cols) + 9))

        @block.scalar
        def _(act):
            nc.scalar.activation(K.u[:, 13, :], K.u[:, 13, :], ACT.Tanh)
            nc.scalar.activation(K.u[:, 12, :], K.u[:, 12, :], ACT.Sigmoid)

        @block.vector
        def _(dve):
            dve.wait_ge(S["rpar"], 16 * (len(cols) + 9))
            dve.tensor_scalar(K.par[:, 6, :], K.par[:, 5, :], -1.0, 1.0, ALU.mult, ALU.add)


W0, A0, GAIN_KK, GAIN_KA, GAIN_K1, GAIN_RK, LN_W, LN_B = 0, 2, 4, 5, 6, 7, 8, 9


def rwkv_keys(nc, K, hf):
    tag = f"k{hf}"
    with ExitStack() as ctx:
        S = sems(nc, ctx, "scaled squared summed rooted turned kl", tag)
        block = ctx.enter_context(nc.Block())
        raw, sq = K.tmp[0], K.tmp[1]
        uf = K.u[:, :, :].rearrange("p c t -> p (c t)")

        @block.vector
        def _(dve):
            for c in range(2):
                cp = 2 * hf + c
                dve.tensor_scalar(raw[:, c, :], K.u[:, 4 + cp, :], K.par[:, GAIN_KK, cp:cp + 1], None, ALU.mult).then_inc(S["scaled"], 1)
            link = linker(dve, S["kl"])
            for c in range(2):
                dve.wait_ge(S["rooted"], c + 1)
                link(dve.tensor_scalar(sq[:, c, :], sq[:, c, :], 1e-12, None, ALU.max))
                link(dve.reciprocal(sq[:, c, :], sq[:, c, :]))
                dve.tensor_tensor(K.kk[:, c, :], raw[:, c, :], sq[:, c, :], ALU.mult)

        @block.scalar
        def _(act):
            for c in range(2):
                act.wait_ge(S["scaled"], c + 1)
                nc.scalar.activation(sq[:, c, :], raw[:, c, :], ACT.Square).then_inc(S["squared"], 1)
            for c in range(2):
                act.wait_ge(S["summed"], c + 1)
                nc.scalar.activation(sq[:, c, :], K.ps[c][:, :], ACT.Sqrt).then_inc(S["rooted"], 1)
            for b in range(6):
                c, q = b // 3, 4 * (b % 3)
                act.wait_ge(S["turned"], b + 1)
                ps = K.ps[2 + b].rearrange("p (w f) -> p w f", f=P)
                if q < NCH:
                    nc.scalar.activation(K.SV[64:128, q:q + 4, c, 0, :], ps[64:128, :, 0:64], ACT.Copy)
                lo, hi = max(q, 1), min(q + 4, NCH + 1)
                nc.scalar.activation(K.SV[0:64, lo - 1:hi - 1, c, 1, :], ps[0:64, lo - q:hi - q, 64:128], ACT.Copy)

        @block.tensor
        def _(pe):
            for b in range(6):
                c, q = b // 3, 4 * (b % 3)
                for w in range(q, min(q + 4, NCH + 1)):
                    t0 = (8 + 2 * hf + c) * T + 64 * w - 64
                    last = pe.transpose(K.ps[2 + b][:, (w - q) * P:(w - q + 1) * P], uf[:, t0:t0 + P], K.ident[:, :])
                last.then_inc(S["turned"], 1)
            for c in range(2):
                pe.wait_ge(S["squared"], c + 1)
                pe.matmul(K.ps[c][:, :], K.heads1[:, :], sq[:, c, :], start=True, stop=True).then_inc(S["summed"], 1)


def rwkv_decays(nc, K, hf, d):
    tag = f"d{hf}{d}"
    with ExitStack() as ctx:
        S = sems(nc, ctx, "lora gated sums expd dl", tag)
        block = ctx.enter_context(nc.Block())
        sg, cs, a, e1 = K.tmp
        rows = slice(64 * d, 64 * d + 64)
        v4 = lambda t: t[:, :, :].rearrange("p c (n s) -> p c n s", s=CHUNK)
        first = lambda t: K.AR[:, :, :, t, :]
        r, k = K.u[:, 2 * hf:2 * hf + 2, :], K.u[:, 4 + 2 * hf:6 + 2 * hf, :]

        @block.tensor
        def _(pe):
            for c in range(2):
                f = slice((2 * hf + c) * P, (2 * hf + c + 1) * P)
                pe.matmul(K.ps[c][:, :], K.wup[rows, f], K.u[rows, 13, :], start=True, stop=True).then_inc(S["lora"], 1)
                pe.matmul(K.ps[2 + c][:, :], K.aup[rows, f], K.u[rows, 14, :], start=True, stop=True).then_inc(S["lora"], 1)

        @block.scalar
        def _(act):
            for c in range(2):
                cp = 2 * hf + c
                act.wait_ge(S["lora"], 2 * c + 2)
                nc.scalar.activation(sg[:, c, :], K.ps[c][:, :], ACT.Sigmoid, bias=K.par[:, W0 + d, cp:cp + 1]).then_inc(S["gated"], 1)
                nc.scalar.activation(a[:, c, :], K.ps[2 + c][:, :], ACT.Sigmoid, bias=K.par[:, A0 + d, cp:cp + 1]).then_inc(S["gated"], 1)
            act.wait_ge(S["sums"], 1)
            e2 = cs if d == 0 else sg
            last = CHUNK - 1 if d == 0 else 0
            for c in range(2):
                nc.scalar.activation(K.AR[:, c, :, 0, :], v4(e1)[:, c], ACT.Exp, scale=-DECAY)
                nc.scalar.activation(K.AR[:, c, :, 1, :], v4(e2)[:, c], ACT.Exp, scale=-DECAY)
                nc.scalar.activation(K.BK[:, c, :, 0, :], v4(e2)[:, c], ACT.Exp, scale=DECAY)
                nc.scalar.activation(K.BK[:, c, :, 1, :], v4(e2)[:, c], ACT.Exp, scale=DECAY).then_inc(S["expd"], 1)
                nc.scalar.activation(K.DC[:, c, :], v4(e2)[:, c, :, last], ACT.Exp, scale=-DECAY)

        @block.vector
        def _(dve):
            link = linker(dve, S["dl"])
            for c in range(2):
                dve.wait_ge(S["gated"], 2 * c + 1)
                link(dve.tensor_tensor_scan(cs[:, c, :], K.chunk0[:, :], sg[:, c, :], 0.0, ALU.mult, ALU.add))
            if d == 0:
                dve.tensor_tensor(e1[:, :, :], cs[:, :, :], sg[:, :, :], ALU.subtract).then_inc(S["sums"], 1)
            else:
                for c in range(2):
                    link(dve.tensor_tensor(v4(e1)[:, c], v4(cs)[:, c, :, CHUNK - 1:CHUNK].to_broadcast([P, NCH, CHUNK]),
                                           v4(cs)[:, c], ALU.subtract))
                dve.tensor_tensor(sg[:, :, :], e1[:, :, :], sg[:, :, :], ALU.add).then_inc(S["sums"], 1)
            dve.wait_ge(S["gated"], 4)
            dve.wait_ge(S["sums"], 1)
            ak = cs if d == 1 else sg
            link(dve.tensor_tensor(ak[:, :, :], a[:, :, :], K.kk[:, :, :], ALU.mult))
            for c in range(2):
                cp = 2 * hf + c
                link(dve.tensor_scalar(a[:, c, :], a[:, c, :], K.par[:, GAIN_KA, cp:cp + 1], K.par[:, GAIN_K1, cp:cp + 1],
                                       ALU.mult, ALU.add))
            link(dve.tensor_tensor(a[:, :, :], a[:, :, :], k, ALU.mult))
            if d == 0:
                link(dve.tensor_copy(K.ksum[:, :, :], a[:, :, :]))
            else:
                link(dve.tensor_tensor(K.ksum[:, :, :], K.ksum[:, :, :], a[:, :, :], ALU.add))
            for c in range(2):
                dve.wait_ge(S["expd"], c + 1)
                v3 = lambda t: t.rearrange("p (n s) -> p n s", s=CHUNK)
                dve.tensor_tensor(K.AR[:, c, :, 0, :], K.AR[:, c, :, 0, :], v4(K.kk)[:, c], ALU.mult)
                dve.tensor_tensor(K.AR[:, c, :, 1, :], K.AR[:, c, :, 1, :], v3(r[:, c, :]), ALU.mult)
                for par in range(2):
                    rows = slice(64 * par, 64 * par + 64)
                    for j, factor in ((par, ak), (1 - par, a)):
                        o = K.BK[rows, c, :, j, :]
                        dve.tensor_tensor(o, o, v4(factor)[rows, c], ALU.mult)


def rwkv_chunks(nc, K, hf, d):
    tag = f"c{hf}{d}"
    names = ("products masked bk_turned powered0 powered1 p_copied0 p_copied1 x_added0 x_added1 r_ready r_copied n_ready "
             "n_copied state_mm state_ok y_copied cl")
    ROUNDS = 6
    with ExitStack() as ctx:
        S = sems(nc, ctx, names, tag)
        powered, p_copied, x_added = ([S[n + "0"], S[n + "1"]] for n in ("powered", "p_copied", "x_added"))
        sbt = lambda n, s: ctx.enter_context(nc.sbuf_tensor(n + tag, s, F32))
        M = sbt("M", [P, 2, 2, 2, P])
        PB, PT = sbt("PB", [P, 2, 2, P]), sbt("PT", [P, 2, 2, P])
        X = sbt("X", [P, 2, 2, 64])
        XF = sbt("XF", [P, 2, 2, P])
        BKT = sbt("BKT", [P, 2, 2, P])
        RH = sbt("RH", [P, 2, 64])
        ST = sbt("ST", [P, 2, 64])
        block = ctx.enter_context(nc.Block())
        psM, psP, psQ, psC, psN = K.ps[0:2], K.ps[2:4], K.ps[4:6], K.ps[6], K.ps[7]
        MT, BT, R_, Y_, U_ = 256, 256, 0, 128, 256
        chunk = lambda s: s if d == 0 else NCH - 1 - s
        pair = lambda t, w: t.rearrange("p (c w) -> p c w", w=w)
        halves = ((0, slice(0, 64)), (1, slice(64, 128)))

        @block.tensor
        def _(pe):
            def products(s):
                ch, q = chunk(s), s % 2
                if s:
                    pe.wait_ge(S["masked"], s)
                if s >= 2:
                    pe.wait_ge(p_copied[q], 5 * (s // 2))
                for c in range(2):
                    for par, rows in halves:
                        pe.matmul(psM[par][:, c * P:(c + 1) * P], K.BK[rows, c, ch, :, :], K.AR[rows, c, ch, :, :],
                                  start=True, stop=True)
                for c in range(2):
                    for par, rows in halves:
                        pe.matmul(psM[par][rows, MT + c * 64:MT + c * 64 + 64], K.AR[rows, c, ch, 0, :],
                                  K.BK[rows, c, ch, par, :], start=True, stop=True)
                for c in range(2):
                    last = pe.transpose(psQ[q][:, BT + c * P:BT + (c + 1) * P], K.BK[:, c, ch, :, :], K.ident[:, :])
                last.then_inc(S["products"], 1)

            def power(s, r):
                q, n = s % 2, s // 2
                if r == 0:
                    pe.wait_ge(S["masked"], s + 1)
                    pe.wait_ge(S["bk_turned"], s + 1)
                if n or r:
                    pe.wait_ge(p_copied[q], 5 * n + r)
                    pe.wait_ge(x_added[q], 6 * n + r)
                for c in range(2):
                    o = psP[q][:, c * 192:c * 192 + 192]
                    if r < ROUNDS - 1:
                        last = pe.matmul(o[:, 0:P], PT[:, q, c, :], PB[:, q, c, :], start=True, stop=True)
                        last = pe.matmul(psQ[q][:, c * P:(c + 1) * P], PB[:, q, c, :], PT[:, q, c, :], start=True, stop=True)
                    if r:
                        last = pe.matmul(o[:, P:192], PT[:, q, c, :], X[:, q, c, :], start=True, stop=True)
                last.then_inc(powered[q], 1)

            def solve_in(s):
                ch, q = chunk(s), s % 2
                pe.wait_ge(S["masked"], s + 1)
                pe.wait_ge(S["state_ok"], s + 1)
                if s:
                    pe.wait_ge(S["y_copied"], s)
                for c in range(2):
                    for par, rows in halves:
                        o = psC[rows, R_ + c * 64:R_ + c * 64 + 64]
                        pe.matmul(o, M[:, q, c, par, 0:64], K.SV[:, ch, c, par, :], start=True, stop=False)
                        last = pe.matmul(o, K.AR[rows, c, ch, 0, :], ST[rows, c, :], start=False, stop=True)
                last.then_inc(S["r_ready"], 1)

            def solve(s):
                q = s % 2
                pe.wait_ge(S["r_copied"], s + 1)
                pe.wait_ge(x_added[q], 6 * (s // 2 + 1))
                for c in range(2):
                    last = pe.matmul(psN[:, c * 64:c * 64 + 64], XF[:, q, c, :], RH[:, c, :], start=True, stop=True)
                last.then_inc(S["n_ready"], 1)

            def finish(s):
                ch, q = chunk(s), s % 2
                pe.wait_ge(S["n_copied"], s + 1)
                for c in range(2):
                    for par, rows in halves:
                        o = psC[rows, Y_ + c * 64:Y_ + c * 64 + 64]
                        pe.matmul(o, M[:, q, c, par, 64:128], K.SV[:, ch, c, par, :], start=True, stop=False)
                        pe.matmul(o, K.AR[rows, c, ch, 1, :], ST[rows, c, :], start=False, stop=True)
                for c in range(2):
                    for par, rows in halves:
                        last = pe.matmul(psC[rows, U_ + c * 64:U_ + c * 64 + 64], BKT[:, q, c, rows],
                                         K.SV[:, ch, c, par, :], start=True, stop=True)
                last.then_inc(S["state_mm"], 1)

            products(0)
            products(1)
            for r in range(ROUNDS):
                power(0, r)
                power(1, r)
            for s in range(0, NCH, 2):
                more = s + 2 < NCH
                solve_in(s)
                solve(s)
                finish(s)
                if more:
                    products(s + 2)
                    power(s + 2, 0)
                solve_in(s + 1)
                if more:
                    power(s + 2, 1)
                solve(s + 1)
                if more:
                    power(s + 2, 2)
                finish(s + 1)
                if more:
                    products(s + 3)
                    for r in range(ROUNDS):
                        if r + 3 < ROUNDS:
                            power(s + 2, r + 3)
                        power(s + 3, r)

        @block.scalar
        def _(act):
            def turn(s):
                act.wait_ge(S["products"], s + 1)
                if s >= 2:
                    act.wait_ge(S["state_mm"], s - 1)
                nc.scalar.activation(BKT[:, s % 2, :, :], pair(psQ[s % 2][:, BT:BT + 256], P), ACT.Copy).then_inc(S["bk_turned"], 1)

            def copy_transposes(s, r):
                q = s % 2
                act.wait_ge(powered[q], 6 * (s // 2) + r + 1)
                nc.scalar.activation(PT[:, q, :, :], pair(psQ[q][:, 0:256], P), ACT.Copy).then_inc(p_copied[q], 1)

            def negate(s):
                act.wait_ge(S["r_ready"], s + 1)
                nc.scalar.activation(RH[:, :, :], pair(psC[:, R_:R_ + 128], 64), ACT.Copy, scale=-1.0).then_inc(S["r_copied"], 1)

            turn(0)
            turn(1)
            for r in range(ROUNDS - 1):
                copy_transposes(0, r)
                copy_transposes(1, r)
            for s in range(0, NCH, 2):
                more = s + 2 < NCH
                negate(s)
                if more:
                    turn(s + 2)
                    copy_transposes(s + 2, 0)
                negate(s + 1)
                if more:
                    copy_transposes(s + 2, 1)
                    copy_transposes(s + 2, 2)
                    turn(s + 3)
                    for r in range(ROUNDS - 1):
                        if r + 3 < ROUNDS - 1:
                            copy_transposes(s + 2, r + 3)
                        copy_transposes(s + 3, r)

        @block.vector
        def _(dve):
            link = linker(dve, S["cl"])
            dve.memset(PT[:, :, :, :], 0.0)
            dve.memset(PB[:, :, :, :], 0.0)
            dve.memset(XF[:, :, :, :], 0.0)
            for par, rows in halves:
                last = dve.memset(K.SV[rows, :, :, par, :], 0.0)
            link(last)
            dve.memset(ST[:, :, :], 0.0).then_inc(S["state_ok"], 1)

            def mask(s):
                q = s % 2
                dve.wait_ge(S["products"], s + 1)
                if s >= 2:
                    dve.wait_ge(S["state_mm"], s - 1)
                    dve.wait_ge(x_added[q], 6 * (s // 2))
                for par, rows in halves:
                    dve.tensor_tensor(PT[rows, q, :, rows], pair(psM[par][rows, MT:MT + 128], 64),
                                      K.masks_t[rows, d, :].unsqueeze(1).to_broadcast([64, 2, 64]), ALU.mult)
                    last = dve.tensor_tensor(M[:, q, :, par, :], pair(psM[par][:, 0:256], P),
                                             K.masks[:, par, d, :].unsqueeze(1).to_broadcast([P, 2, P]), ALU.mult)
                link(last)
                for par, rows in halves:
                    dve.tensor_copy(PB[rows, q, :, rows], M[rows, q, :, par, 0:64])
                    last = dve.tensor_tensor(X[rows, q, :, :], M[rows, q, :, par, 0:64],
                                             K.ident[rows, rows].unsqueeze(1).to_broadcast([64, 2, 64]), ALU.add)
                last.then_inc(S["masked"], 1)

            def add_x(s, r):
                q = s % 2
                dve.wait_ge(powered[q], 6 * (s // 2) + r + 1)
                if r == ROUNDS - 1 and s >= 2:
                    dve.wait_ge(S["n_ready"], s - 1)
                if s >= 2 or r:
                    dve.wait_ge(x_added[q], 6 * (s // 2) + r)
                prod = pair(psP[q][:, 0:384], 192)
                if r == ROUNDS - 1:
                    for par, rows in halves:
                        last = dve.tensor_tensor(XF[rows, q, :, rows], X[rows, q, :, :], prod[rows, :, P:192], ALU.add)
                else:
                    if r < ROUNDS - 2:
                        last = dve.tensor_copy(PB[:, q, :, :], prod[:, :, 0:P])
                    if r:
                        last = dve.tensor_tensor(X[:, q, :, :], X[:, q, :, :], prod[:, :, P:192], ALU.add)
                last.then_inc(x_added[q], 1)

            def take_n(s):
                dve.wait_ge(S["n_ready"], s + 1)
                for par, rows in halves:
                    last = dve.tensor_copy(K.SV[rows, chunk(s), :, par, :], pair(psN[rows, 0:128], 64))
                last.then_inc(S["n_copied"], 1)

            def take_state(s):
                dve.wait_ge(S["state_mm"], s + 1)
                link(dve.tensor_tensor(ST[:, :, :], ST[:, :, :], pair(psC[:, U_:U_ + 128], 64), ALU.add))
                dve.tensor_tensor(ST[:, :, :], ST[:, :, :], K.DC[:, :, chunk(s):chunk(s) + 1].to_broadcast([P, 2, 64]),
                                  ALU.mult).then_inc(S["state_ok"], 1)
                y, prod = K.Y[:, chunk(s), :, :], pair(psC[:, Y_:Y_ + 128], 64)
                last = dve.tensor_copy(y, prod) if d == 0 else dve.tensor_tensor(y, y, prod, ALU.add)
                last.then_inc(S["y_copied"], 1)

            mask(0)
            mask(1)
            for r in range(ROUNDS):
                add_x(0, r)
                add_x(1, r)
            for s in range(0, NCH, 2):
                more = s + 2 < NCH
                take_n(s)
                take_state(s)
                if more:
                    mask(s + 2)
                    add_x(s + 2, 0)
                    add_x(s + 2, 1)
                take_n(s + 1)
                if more:
                    add_x(s + 2, 2)
                take_state(s + 1)
                if more:
                    mask(s + 3)
                    for r in range(ROUNDS):
                        if r + 3 < ROUNDS:
                            add_x(s + 2, r + 3)
                        add_x(s + 3, r)


def rwkv_output(nc, K, hf):
    tag = f"o{hf}"
    with ExitStack() as ctx:
        S = sems(nc, ctx, "centred sqd vard rooted normed turned bonus gate ol", tag)
        Y = K.Y[:, :, :, :].rearrange("p n c f -> p (n c) f")
        NG = 2 * NCH
        block = ctx.enter_context(nc.Block())
        sq = K.AR[:, 0, :, :, :].rearrange("p a b c -> p (a b) c")
        st = K.BK[:, 0, 0, 0, :]
        mean, rstd = st[:, 0:NG], st[:, NG:2 * NG]
        tb = K.tmp[0]
        z = K.tmp[1]

        @block.vector
        def _(dve):
            link = linker(dve, S["ol"])
            link(dve.tensor_reduce(mean, Y, AX, ALU.add))
            link(dve.tensor_scalar(mean, mean, 1.0 / 64, None, ALU.mult))
            link(dve.tensor_tensor(Y, Y, mean.unsqueeze(2).to_broadcast([P, NG, 64]), ALU.subtract))
            link(dve.tensor_tensor(sq, Y, Y, ALU.mult))
            link(dve.tensor_reduce(rstd, sq, AX, ALU.add))
            dve.tensor_scalar(rstd, rstd, 1.0 / 64, LNX_EPS, ALU.mult, ALU.add).then_inc(S["vard"], 1)
            for c in range(2):
                cp = 2 * hf + c
                dve.scalar_tensor_tensor(out=tb[:, c, :], in0=K.u[:, cp, :], scalar=K.par[:, GAIN_RK, cp:cp + 1],
                                         in1=K.ksum[:, c, :], op0=ALU.mult, op1=ALU.mult).then_inc(S["bonus"], 1)
            dve.wait_ge(S["rooted"], 1)
            link(dve.reciprocal(rstd, rstd))
            dve.tensor_tensor(Y, Y, rstd.unsqueeze(2).to_broadcast([P, NG, 64]), ALU.mult).then_inc(S["normed"], 1)
            for c in range(2):
                cp = 2 * hf + c
                dve.wait_ge(S["gate"], 2 * c + 2)
                bo = tb[:, c, :]
                link(dve.tensor_tensor(bo, K.u[:, 8 + cp, :], K.ps[2 + c][:, :], ALU.mult))
                dve.wait_ge(S["turned"], c + 1)
                link(dve.tensor_scalar(z[:, c, :], K.ps[c][:, :], K.par[:, LN_W, cp:cp + 1], K.par[:, LN_B, cp:cp + 1],
                                       ALU.mult, ALU.add))
                link(dve.tensor_tensor(z[:, c, :], z[:, c, :], bo, ALU.add))
                dve.tensor_tensor(K.u[:, cp, :], z[:, c, :], K.ps[4 + c][:, :], ALU.mult)

        @block.scalar
        def _(act):
            act.wait_ge(S["vard"], 1)
            nc.scalar.activation(rstd, rstd, ACT.Sqrt).then_inc(S["rooted"], 1)

        @block.tensor
        def _(pe):
            for c in range(2):
                cp = 2 * hf + c
                pe.wait_ge(S["bonus"], c + 1)
                pe.matmul(K.ps[2 + c][:, :], K.heads1[:, :], tb[:, c, :], start=True, stop=True).then_inc(S["gate"], 1)
                pe.matmul(K.ps[4 + c][:, :], K.gup[:, cp * P:(cp + 1) * P], K.u[:, 12, :], start=True, stop=True).then_inc(S["gate"], 1)
            pe.wait_ge(S["normed"], 1)
            for c in range(2):
                for ch in range(NCH):
                    for b in (0, 64):
                        last = pe.matmul(K.ps[c][b:b + 64, ch * 64:ch * 64 + 64], K.Y[b:b + 64, ch, c, :],
                                         K.ident[b:b + 64, b:b + 64], start=True, stop=True)
                last.then_inc(S["turned"], 1)


def merge_branches(nc, K, tag, gates, proj, w_out, load_upto):
    with ExitStack() as ctx:
        names = "emm egate eypart eprod esum eadd el"
        S = sems(nc, ctx, names, tag)
        G, Gp = twins(nc, ctx, "G" + tag, [P, 2 * KD, T])
        tmp = ctx.enter_context(nc.sbuf_tensor("gt" + tag, [P, 2, T], F32))
        groups = [(b, ch) for b in range(2) for ch in range(KD)]
        starts = {}
        K.ring.used = {n: (S["emm"], 4 * i + 4) for i, n in enumerate(gates)}
        for b, (_, _, _, loads) in enumerate(proj):
            per = KD // len(loads)
            for i, n in enumerate(loads):
                starts[8 * b + per * i] = n
                K.ring.used[n] = (S["emm"], 16 + 8 * b + per * (i + 1))
        for i, n in enumerate(w_out):
            starts[16 + 4 * i] = n
            K.ring.used[n] = (S["emm"], 32 + 4 * i + 4)
        block = ctx.enter_context(nc.Block())

        @block.sync
        def _(sp):
            K.ring.load(sp, load_upto)

        @block.tensor
        def _(pe):
            for c in range(16):
                n = gates[c // 4]
                K.ring.wait(pe, n, c % 4)
                if c >= 4:
                    pe.wait_ge(S["egate"], c - 3)
                mm_feature(pe, K.ps[c % 4][:, :], (K.ring, n), slice((c % 4) * P, (c % 4) * P + P), K.hp, KD).then_inc(S["emm"], 1)
            for i, (b, ch) in enumerate(groups):
                _, parts, nk, loads = proj[b]
                per = KD // len(loads)
                n, f = loads[ch // per], ch % per
                K.ring.wait(pe, n, f * 4 // per)
                if ch == 0:
                    pe.wait_ge(S["eypart"], b + 1)
                if i >= 4:
                    pe.wait_ge(S["eprod"], i - 3)
                mm_feature(pe, K.ps[4 + i % 4][:, :], (K.ring, n), slice(f * P, f * P + P), parts, nk).then_inc(S["emm"], 1)
            pe.wait_ge(S["esum"], KD)
            for half in range(2):
                for t in range(NT):
                    j = half * NT + t
                    if j >= 4:
                        pe.wait_ge(S["eadd"], j - 3)
                    mm_tokens(pe, K.ps[j % 4][:, :], (K.ring, w_out[half]), slice(0, 512), (Gp[:, KD:2 * KD, :], Gp[:, 0:KD, :]),
                              KD, t).then_inc(S["emm"], 1)

        @block.scalar
        def _(act):
            for c in range(16):
                act.wait_ge(S["emm"], c + 1)
                nc.scalar.activation(G[:, c, :], K.ps[c % 4][:, :], ACT.Sigmoid).then_inc(S["egate"], 1)

        @block.vector
        def _(dve):
            link = linker(dve, S["el"])
            K.ring.split(dve, gates[0])
            K.ring.split(dve, gates[1])
            for yT, (hi, lo), _, _ in proj:
                link(high(dve, hi, yT))
                low(dve, lo, yT, hi).then_inc(S["eypart"], 1)
            for n in range(gates[2], gates[3] + 2):
                K.ring.split(dve, n)
            for i, (b, ch) in enumerate(groups):
                if i - 1 in starts:
                    K.ring.split(dve, starts[i - 1] + 1)
                dve.wait_ge(S["emm"], 16 + i + 1)
                dve.wait_ge(S["egate"], 16)
                ps = K.ps[4 + i % 4][:, :]
                if b == 0:
                    dve.tensor_tensor(G[:, ch, :], G[:, ch, :], ps, ALU.mult).then_inc(S["eprod"], 1)
                else:
                    dve.tensor_tensor(tmp[:, ch % 2, :], G[:, KD + ch, :], ps, ALU.mult).then_inc(S["eprod"], 1)
                    dve.wait_ge(S["eprod"], i + 1)
                    link(dve.tensor_tensor(G[:, ch, :], G[:, ch, :], tmp[:, ch % 2, :], ALU.add))
                    link(high(dve, Gp[:, KD + ch, :], G[:, ch, :]))
                    low(dve, Gp[:, ch, :], G[:, ch, :], Gp[:, KD + ch, :]).then_inc(S["esum"], 1)
            for half in range(2):
                for t in range(NT):
                    j = half * NT + t
                    if j == 1:
                        K.ring.split(dve, w_out[1])
                    dve.wait_ge(S["emm"], 32 + j + 1)
                    o = K.x[:, t, half * 512:(half + 1) * 512]
                    dve.tensor_tensor(o, o, K.ps[j % 4][:, :], ALU.add).then_inc(S["eadd"], 1)


def route(nc, K):
    I = K.I
    with ExitStack() as ctx:
        names = "win lmm neg ex rec aff_t aff topped bmm bcop rl"
        S = sems(nc, ctx, names, "r")
        sbt = lambda n, s, dt=F32: ctx.enter_context(nc.sbuf_tensor(n, s, dt))
        wr, L, st = sbt("wr", [P, KD, N_EXP]), sbt("L", [P, NT, N_EXP]), sbt("rst", [P, 3, NT])
        aff, tv = sbt("aff", [N_EXP, T]), sbt("tv", [N_EXP, 4, CAP])
        ti = sbt("ti", [N_EXP, CAP], U32)
        sel = sbt("sel", [N_EXP, N_EXP, P])
        block = ctx.enter_context(nc.Block())

        @block.sync
        def _(sp):
            sp.dma_start(wr[:, :, :], I["w_router"][0].rearrange("(k p) e -> p k e", p=P)).then_inc(S["win"], 16)
            sp.dma_start(sel[:, :, :], I["c_sel"]).then_inc(S["win"], 16)
            sp.dma_start(K.tok[:, :], I["c_tok"]).then_inc(S["win"], 16)
            with nc.allow_non_contiguous_dma(reason="one gain per partition"):
                sp.dma_start(K.gf[:, :], I["norm_ffn_g"][0].rearrange("(k p) -> p k", p=P)).then_inc(S["win"], 16)
            sp.wait_ge(S["win"], 64)

        @block.tensor
        def _(pe):
            pe.wait_ge(S["win"], 64)
            for t in range(NT):
                for k in range(KD):
                    last = pe.matmul(K.ps[0][:, t * N_EXP:(t + 1) * N_EXP], K.hT[:, k, t * P:(t + 1) * P], wr[:, k, :],
                                     start=(k == 0), stop=(k == KD - 1))
            last.then_inc(S["lmm"], 1)
            pe.wait_ge(S["aff_t"], 1)
            for t in range(NT):
                last = pe.transpose(K.ps[1][0:N_EXP, t * P:(t + 1) * P], L[:, t, :], K.ident[:, :])
            last.then_inc(S["aff"], 1)
            pe.wait_ge(S["topped"], 1)
            for e in range(N_EXP):
                if e >= 2 * 4 and e % 2 == 0:
                    pe.wait_ge(S["bcop"], e // 2 - 3)
                last = pe.matmul(K.ps[2 + (e // 2) % 4][:, (e % 2) * 256:(e % 2) * 256 + 256], sel[:, e, :], tv[:, :, :],
                                 start=True, stop=True)
                if e % 2:
                    last.then_inc(S["bmm"], 1)

        @block.scalar
        def _(act):
            act.wait_ge(S["neg"], 1)
            for t in range(NT):
                last = nc.scalar.activation(L[:, t, :], K.ps[0][:, t * N_EXP:(t + 1) * N_EXP], ACT.Exp, bias=st[:, 0, t:t + 1],
                                            accum_out=st[:, 1, t:t + 1])
            last.then_inc(S["ex"], 1)
            for b in range(N_EXP // 2):
                act.wait_ge(S["bmm"], b + 1)
                nc.scalar.activation(K.IB[:, 2 * b:2 * b + 2, :], K.ps[2 + b % 4][:, :].rearrange("p (e c) -> p e c", e=2),
                                     ACT.Copy).then_inc(S["bcop"], 1)

        @block.vector
        def _(dve):
            link = linker(dve, S["rl"])
            dve.wait_ge(S["lmm"], 1)
            logits = K.ps[0][:, 0:NT * N_EXP].rearrange("p (t e) -> p t e", t=NT)
            dve.tensor_reduce(st[:, 0, :], logits, AX, ALU.max, negate=True).then_inc(S["neg"], 1)
            dve.wait_ge(S["ex"], 1)
            link(dve.reciprocal(st[:, 2, :], st[:, 1, :]))
            dve.tensor_tensor(L[:, :, :], L[:, :, :], st[:, 2, :].unsqueeze(2).to_broadcast([P, NT, N_EXP]), ALU.mult).then_inc(S["aff_t"], 1)
            dve.wait_ge(S["aff"], 1)
            link(dve.tensor_copy(aff[:, :], K.ps[1][0:N_EXP, :]))
            for r in range(CAP // 8):
                best = tv[:, 2, 8 * r:8 * r + 8]
                link(dve.max(best, aff[:, :]))
                link(dve.max_index(ti[:, 8 * r:8 * r + 8], best, aff[:, :]))
                if r + 1 < CAP // 8:
                    link(dve.match_replace(aff[:, :], best, aff[:, :], -1.0))
            dve.tensor_copy(tv[:, 3, :], tv[:, 2, :])
            dve.tensor_copy(tv[:, 0, :], ti[:, :])
            dve.tensor_copy(tv[:, 1, :], ti[:, :]).then_inc(S["topped"], 1)


def experts(nc, K, n0, load_upto):
    I = K.I
    H = 512
    names = ("w_used oh_ready gathered xs_copied xs_turned xsT_ready gate_sig gated hid_ready hid_turned hidT_ready "
             "ys_ready oht_turned oht_ready combined x_added")
    with ExitStack() as ctx:
        S = sems(nc, ctx, names, "m")
        sbt = lambda n, s: ctx.enter_context(nc.sbuf_tensor(n, s, F32))
        OH, OHV = sbt("OH", [P, NT, CAP]), sbt("OHV", [P, NT, P])
        XS = sbt("XS", [P, H])
        xsT = sbt("xsT", [P, 2, 4, 2, CAP])
        HS, hidT, ys = sbt("HS", [P, H]), sbt("hidT", [P, 4, 2, CAP]), sbt("ys", [P, H])
        OHT = sbt("OHT", [P, 2, NT, P])
        psO, psX, psT, psG, psU, psD = K.ps[0:6]
        psC = K.ps[6:8]
        srcs = (I["exp_w_gate"], I["exp_w_up"], I["exp_w_down"])
        slot = lambda j: K.ring.buf[:, j % RING, :].rearrange("p (k w) -> p k w", k=4)
        block = ctx.enter_context(nc.Block())
        LOOPS = N_EXP // 2 - 1

        def wait(eng, sem, value):
            if not isinstance(value, int) or value > 0:
                eng.wait_ge(sem, value)

        def load(sp, e, part, j):
            src = srcs[part // 2][0, bass.ds(e, 1), (part % 2) * H:(part % 2) * H + H, :]
            sp.dma_start(slot(j), src.rearrange("e (k p) w -> p (e k) w", p=P)).then_inc(K.ring.full[j % RING], 16)

        @block.sync
        def _(sp):
            if K.ring.issued < n0 + 4:
                for j in range(K.ring.issued - n0, 4):
                    load(sp, 0, j, j)
            with sp.Fori(0, LOOPS) as i:
                for j in range(12):
                    m = 4 + j
                    sp.wait_ge(S["w_used"], i * 12 + (j + 1))
                    load(sp, i * 2 + m // 6, m % 6, m)
            for j in range(12 * LOOPS + 4, 96):
                sp.wait_ge(S["w_used"], j - 3)
                load(sp, j // 6, j % 6, j)
            K.ring.issued = n0 + 96
            K.ring.used = {n0 + j: (S["w_used"], j + 1) for j in range(92, 96)}
            K.ring.load(sp, load_upto)

        def each(eng, steps):
            steps(0, 0, False)
            steps(1, 1, False)
            with eng.Fori(1, LOOPS) as i:
                for u in range(2):
                    steps(i * 2 + u, u, False)
            steps(N_EXP - 2, 0, False)
            steps(N_EXP - 1, 1, True)

        @block.tensor
        def _(pe):
            def gather(e):
                pe.wait_ge(S["oh_ready"], e + 1)
                wait(pe, S["xs_copied"], e)
                for t in range(NT):
                    for half in range(2):
                        last = pe.matmul(psX[64 * half:64 * half + 64, :], OH[:, t, :], K.xn[:, t, half * H:(half + 1) * H],
                                         start=(t == 0), stop=(t == NT - 1))
                last.then_inc(S["gathered"], 1)

            def turn_xs(e):
                pe.wait_ge(S["xs_copied"], e + 1)
                wait(pe, S["hidT_ready"], e)
                for c in range(4):
                    last = pe.transpose(psT[:, c * P:(c + 1) * P], XS[:, c * P:(c + 1) * P], K.ident[:, :])
                last.then_inc(S["xs_turned"], 1)

            def turn_oh(e):
                pe.wait_ge(S["oh_ready"], e + 1)
                wait(pe, S["oht_ready"], e)
                for t in range(NT):
                    last = pe.transpose(psO[:, t * P:(t + 1) * P], OHV[:, t, :], K.ident[:, :])
                last.then_inc(S["oht_turned"], 1)

            def halves(e, u, out, lhs, part):
                for ld in range(2):
                    j = 6 * u + 2 * part + ld
                    pe.wait_ge(K.ring.full[j % RING], (e - u) * 24 + 16 * (j // RING) + K.ring.landed[n0 + j % RING])
                    for kk in range(4):
                        k = 4 * ld + kk
                        for half in range(2):
                            last = pe.matmul(out[64 * half:64 * half + 64, :], lhs[:, k % 4, k // 4, :],
                                             slot(j)[:, kk, half * H:(half + 1) * H], start=(k == 0), stop=(k == KD - 1))
                    last.then_inc(S["w_used"], 1)

            def steps(e, u, final):
                pe.wait_ge(S["xsT_ready"], e + 1)
                wait(pe, S["hid_ready"], e)
                halves(e, u, psG, xsT[:, u], 0)
                halves(e, u, psU, xsT[:, u], 1)
                if not final:
                    gather(e + 1)
                pe.wait_ge(S["hid_ready"], e + 1)
                for c in range(4):
                    last = pe.transpose(psT[:, c * P:(c + 1) * P], HS[:, c * P:(c + 1) * P], K.ident[:, :])
                last.then_inc(S["hid_turned"], 1)
                pe.wait_ge(S["hidT_ready"], e + 1)
                wait(pe, S["ys_ready"], e)
                halves(e, u, psD, hidT, 2)
                if not final:
                    turn_xs(e + 1)
                    turn_oh(e + 1)
                pe.wait_ge(S["ys_ready"], e + 1)
                pe.wait_ge(S["oht_ready"], e + 1)
                for j in range(8):
                    t, half = j // 2, j % 2
                    if j >= 2:
                        wait(pe, S["x_added"], e * 8 + (j - 1))
                    else:
                        wait(pe, S["x_added"], e * 8)
                    rows = slice(64 * half, 64 * half + 64)
                    pe.matmul(psC[half][:, :], OHT[rows, u, t, :], ys[rows, :], start=True, stop=True).then_inc(S["combined"], 1)

            gather(0)
            turn_xs(0)
            turn_oh(0)
            each(pe, steps)

        @block.scalar
        def _(act):
            def copy_xs(e):
                act.wait_ge(S["gathered"], e + 1)
                wait(act, S["xs_turned"], e)
                nc.scalar.activation(XS[:, :], psX[:, :], ACT.Copy).then_inc(S["xs_copied"], 1)

            def copy_oh(e, u):
                act.wait_ge(S["oht_turned"], e + 1)
                nc.scalar.activation(OHT[:, u, :, :], psO[:, :].rearrange("p (t c) -> p t c", t=NT), ACT.Copy).then_inc(S["oht_ready"], 1)

            def steps(e, u, final):
                act.wait_ge(S["w_used"], e * 6 + 2)
                wait(act, S["hid_turned"], e)
                nc.scalar.activation(HS[:, :], psG[:, :], ACT.Sigmoid).then_inc(S["gate_sig"], 1)
                if not final:
                    copy_xs(e + 1)
                act.wait_ge(S["hid_turned"], e + 1)
                nc.scalar.activation(hidT[:, :, :, :], psT[:, :].rearrange("p (c h s) -> p c h s", c=4, h=2), ACT.Copy).then_inc(S["hidT_ready"], 1)
                act.wait_ge(S["w_used"], e * 6 + 6)
                wait(act, S["combined"], e * 8)
                nc.scalar.activation(ys[:, :], psD[:, :], ACT.Copy).then_inc(S["ys_ready"], 1)
                if not final:
                    copy_oh(e + 1, 1 - u)

            copy_xs(0)
            copy_oh(0, 0)
            each(act, steps)

        @block.vector
        def _(dve):
            def one_hots(e):
                wait(dve, S["gathered"], e)
                wait(dve, S["oht_turned"], e)
                for t in range(NT):
                    dve.tensor_scalar(OH[:, t, :], K.IB[:, bass.ds(e, 1), 0:CAP].rearrange("p a c -> p (a c)"),
                                      K.tok[:, t:t + 1], None, ALU.is_equal)
                    last = dve.scalar_tensor_tensor(
                        out=OHV[:, t, :], in0=K.IB[:, bass.ds(e, 1), 0:P].rearrange("p a c -> p (a c)"), scalar=K.tok[:, t:t + 1],
                        in1=K.IB[:, bass.ds(e, 1), P:2 * P].rearrange("p a c -> p (a c)"), op0=ALU.is_equal, op1=ALU.mult)
                last.then_inc(S["oh_ready"], 1)

            def scale_xs(e, u):
                dve.wait_ge(S["xs_turned"], e + 1)
                dve.tensor_tensor(xsT[:, u, :, :, :], psT[:, :].rearrange("p (c h s) -> p c h s", c=4, h=2),
                                  K.gf[:, :].rearrange("p (h c) -> p c h", h=2).unsqueeze(3).to_broadcast([P, 4, 2, CAP]), ALU.mult).then_inc(S["xsT_ready"], 1)

            def steps(e, u, final):
                if not final:
                    one_hots(e + 1)
                dve.wait_ge(S["gate_sig"], e + 1)
                dve.tensor_tensor(HS[:, :], HS[:, :], psG[:, :], ALU.mult).then_inc(S["gated"], 1)
                dve.wait_ge(S["gated"], e + 1)
                dve.wait_ge(S["w_used"], e * 6 + 4)
                dve.tensor_tensor(HS[:, :], HS[:, :], psU[:, :], ALU.mult).then_inc(S["hid_ready"], 1)
                if not final:
                    scale_xs(e + 1, 1 - u)
                for j in range(8):
                    t, half = j // 2, j % 2
                    dve.wait_ge(S["combined"], e * 8 + (j + 1))
                    o = K.x[:, t, half * H:(half + 1) * H]
                    dve.tensor_tensor(o, o, psC[half][:, :], ALU.add).then_inc(S["x_added"], 1)

            one_hots(0)
            scale_xs(0, 0)
            each(dve, steps)


def gain_norm(nc, K, tag, g, out_dram=None, keep_dram=None):
    dst = out_dram if out_dram is not None else keep_dram
    with ExitStack() as ctx:
        S = sems(nc, ctx, "g_in squared var_ok root_ok rec_ok scaled gained stored", tag)
        gb = ctx.enter_context(nc.sbuf_tensor("gb" + tag, [P, D], F32))
        sq = ctx.enter_context(nc.sbuf_tensor("sqg" + tag, [P, 2, D], F32))
        ss = ctx.enter_context(nc.sbuf_tensor("ssg" + tag, [P, 4, NT], F32))
        block = ctx.enter_context(nc.Block())

        @block.sync
        def _(sp):
            sp.dma_start(gb[:, :], g.rearrange("(a d) -> a d", a=1).to_broadcast([P, D])).then_inc(S["g_in"], 16)
            for t in range(NT):
                sp.wait_ge(S["gained"], t + 1)
                sp.dma_start(dst[t * P:(t + 1) * P, :], K.x[:, t, :]).then_inc(S["stored"], 16)
            sp.wait_ge(S["stored"], 16 * NT)

        @block.scalar
        def _(act):
            for t in range(NT):
                if t >= 2:
                    act.wait_ge(S["squared"], t - 1)
                nc.scalar.activation(sq[:, t % 2, :], K.x[:, t, :], ACT.Square, accum_out=ss[:, 0, t:t + 1]).then_inc(S["squared"], 1)
            act.wait_ge(S["var_ok"], 1)
            nc.scalar.activation(ss[:, 2, :], ss[:, 1, :], ACT.Sqrt).then_inc(S["root_ok"], 1)

        @block.vector
        def _(dve):
            dve.wait_ge(S["squared"], NT)
            dve.tensor_scalar(ss[:, 1, :], ss[:, 0, :], 1.0 / D, EPS, ALU.mult, ALU.add).then_inc(S["var_ok"], 1)
            dve.wait_ge(S["root_ok"], 1)
            dve.reciprocal(ss[:, 3, :], ss[:, 2, :]).then_inc(S["rec_ok"], 1)
            dve.wait_ge(S["rec_ok"], 1)
            dve.wait_ge(S["g_in"], 16)
            for t in range(NT):
                dve.scalar_tensor_tensor(out=K.x[:, t, :], in0=K.x[:, t, :], scalar=ss[:, 3, t:t + 1], in1=gb[:, :],
                                         op0=ALU.mult, op1=ALU.mult).then_inc(S["gained"], 1)


def mlstm_inputs(nc, K, n0, load_upto):
    I = K.I
    NC2 = 2 * D // P
    with ExitStack() as ctx:
        S = sems(nc, ctx, "mm par first tap sig act vcop wif gmm gcop rows e1 e2 bmm bcop cmm xl al", "I")
        sbt = lambda n, s: ctx.enter_context(nc.sbuf_tensor(n, s, F32))
        cw, cb = sbt("cw", [P, 5, NC2]), None
        acc = sbt("acc", [P, 2, T])
        sgb = sbt("sgb", [P, 2, T])
        wif = sbt("wif", [P, KD, 8])
        wif_high, wif_low = (ctx.enter_context(nc.sbuf_tensor(n, [P, KD, 8], F32R)) for n in ("wif_high", "wif_low"))
        bif = sbt("bif", [M_HEADS, 2])
        rows = sbt("rows", [M_HEADS, 6, T])
        mrow = sbt("mrow", [M_HEADS, 4, NT + 1])
        reset = sbt("reset", [M_HEADS, 2, T])
        K.ring.used = {n0 + i: (S["mm"], 4 * i + 4) for i in range(6)}
        block = ctx.enter_context(nc.Block())
        ig, lf, b, M, ex, wk = (rows[:, j, :] for j in range(6))

        @block.sync
        def _(sp):
            with nc.allow_non_contiguous_dma(reason="one tap per partition"):
                for j in range(4):
                    sp.dma_start(cw[:, j, :], I["conv_w_2"][0][j].rearrange("(c p) -> p c", p=P)).then_inc(S["par"], 16)
                sp.dma_start(cw[:, 4, :], I["conv_b_2"][0].rearrange("(c p) -> p c", p=P)).then_inc(S["par"], 16)
                sp.dma_start(wif[:, :, :], I["w_in_2"][0][:, IF_M:IF_M + 8].rearrange("(k p) w -> p k w", p=P)).then_inc(S["par"], 16)
                sp.dma_start(bif[:, :], I["b_gate_if_2"][0].rearrange("(j h) -> h j", j=2)).then_inc(S["par"], 16)
            sp.dma_start(reset[:, :, :], I["c_reset"]).then_inc(S["par"], 16)
            sp.dma_start(K.sel4[:, :, :], I["c_sel4"]).then_inc(S["par"], 16)
            sp.dma_start(K.causal[:, :], I["c_causal"]).then_inc(S["par"], 16)
            K.ring.load(sp, load_upto)
            sp.wait_ge(S["par"], 160)

        @block.tensor
        def _(pe):
            pe.wait_ge(S["wif"], 2)
            for j in range(2):
                for k in range(KD):
                    f = slice(4 * j, 4 * j + 4)
                    last = product(pe, K.ps[4 + j][0:M_HEADS, :], (wif_high[:, k, f], wif_low[:, k, f]), [t[:, k, :] for t in K.hp], k == 0, k == KD - 1)
            last.then_inc(S["gmm"], 1)
            for c in range(NC2):
                K.ring.wait(pe, n0 + c // 4, c % 4)
                if c >= 4:
                    pe.wait_ge(S["tap"], c - 3)
                mm_feature(pe, K.ps[c % 4][:, :], (K.ring, n0 + c // 4), slice((c % 4) * P, (c % 4) * P + P), K.hp, KD).then_inc(S["mm"], 1)
            for half in range(2):
                n = n0 + 4 + half
                for t in range(NT):
                    j = half * NT + t
                    if j < 4:
                        pe.wait_ge(S["tap"], 13 + j)
                    else:
                        pe.wait_ge(S["vcop"], j - 3)
                    mm_tokens(pe, K.ps[j % 4][:, :], (K.ring, n), slice(0, 512), K.hp, KD, t).then_inc(S["mm"], 1)
            pe.wait_ge(S["e2"], 1)
            for j, row in enumerate((M, ex)):
                for h in range(M_HEADS):
                    i = j * 4 + h
                    if i >= 2:
                        pe.wait_ge(S["bcop"], i - 1)
                    pe.matmul(K.ps[4 + i % 2][:, :], K.sel4[:, h, :], row, start=True, stop=True).then_inc(S["bmm"], 1)
            for q, row in enumerate((b, ig, wk)):
                for c in range(NT):
                    pe.transpose(K.ps[6][:, (q * NT + c) * 4:(q * NT + c) * 4 + 4], row[:, c * P:(c + 1) * P], K.ident[0:4, 0:4])
            for h in range(M_HEADS):
                last = pe.matmul(K.ps[6][:, 64 + 4 * h:68 + 4 * h], K.sel4[:, h, :], mrow[:, 2, 0:NT], start=True, stop=True)
            last.then_inc(S["cmm"], 1)

        @block.scalar
        def _(act):
            act.wait_ge(S["par"], 160)
            link = linker(act, S["al"])
            act.wait_ge(S["gcop"], 2)
            link(nc.scalar.activation(M, lf, ACT.Abs))
            link(nc.scalar.activation(M, M, ACT.Exp, scale=-1.0))
            nc.scalar.activation(M, M, ACT.Ln, bias=1.0).then_inc(S["e1"], 1)
            for c in range(NC2):
                dst = K.qmT[:, c, :] if c < 8 else K.kmT[:, c - 8, :]
                act.wait_ge(S["mm"], c + 1)
                if c >= 2:
                    act.wait_ge(S["act"], c - 1)
                nc.scalar.activation(acc[:, c % 2, :], K.ps[c % 4][:, :], ACT.Identity, scale=cw[:, 3, c:c + 1],
                                     bias=cw[:, 4, c:c + 1]).then_inc(S["first"], 1)
                act.wait_ge(S["tap"], c + 1)
                nc.scalar.activation(sgb[:, c % 2, :], acc[:, c % 2, :], ACT.Sigmoid).then_inc(S["sig"], 1)
            for j in range(8):
                t, half = j % 4, j // 4
                act.wait_ge(S["mm"], NC2 + j + 1)
                nc.scalar.activation(K.vm[:, t, 2 * half:2 * half + 2, 0:M_DH], K.ps[j % 4][:, :].rearrange("p (h d) -> p h d", h=2),
                                     ACT.Copy).then_inc(S["vcop"], 1)
            act.wait_ge(S["rows"], 1)
            nc.scalar.activation(ex, ex, ACT.Exp)
            nc.scalar.activation(mrow[:, 2, 0:NT], mrow[:, 2, 0:NT], ACT.Exp)
            nc.scalar.activation(wk, wk, ACT.Exp)
            nc.scalar.activation(b, b, ACT.Exp).then_inc(S["e2"], 1)
            for i in range(8):
                act.wait_ge(S["bmm"], i + 1)
                dst = K.MB if i < 4 else K.WI
                nc.scalar.activation(dst[:, i % 4, :], K.ps[4 + i % 2][:, :], ACT.Copy).then_inc(S["bcop"], 1)
            act.wait_ge(S["cmm"], 1)
            nc.scalar.activation(K.cols[:, :, :], K.ps[6][:, 0:48].rearrange("p (q c h) -> p q (c h)", q=3, c=NT), ACT.Copy)
            nc.scalar.activation(K.dec[:, :], K.ps[6][:, 64:80], ACT.Copy)

        @block.vector
        def _(dve):
            dve.wait_ge(S["par"], 160)
            high(dve, wif_high[:, :, :], wif[:, :, :]).then_inc(S["wif"], 1)
            dve.wait_ge(S["wif"], 1)
            low(dve, wif_low[:, :, :], wif[:, :, :], wif_high[:, :, :]).then_inc(S["wif"], 1)
            K.ring.split(dve, n0)
            K.ring.split(dve, n0 + 1)
            dve.wait_ge(S["gmm"], 1)
            dve.tensor_scalar(ig, K.ps[4][0:M_HEADS, :], bif[:, 0:1], None, ALU.add).then_inc(S["gcop"], 1)
            dve.tensor_scalar(lf, K.ps[5][0:M_HEADS, :], bif[:, 1:2], None, ALU.add).then_inc(S["gcop"], 1)
            link = linker(dve, S["xl"])
            dve.wait_ge(S["e1"], 1)
            link(dve.tensor_scalar(lf, lf, 0.0, None, ALU.min))
            link(dve.tensor_tensor(lf, lf, M, ALU.subtract))
            link(dve.tensor_tensor_scan(b, reset[:, 0, :], lf, 0.0, ALU.mult, ALU.add))
            link(dve.tensor_tensor(ig, ig, b, ALU.subtract))
            link(dve.memset(mrow[:, :, :], 0.0))
            for c in range(NT):
                cc = slice(c * P, (c + 1) * P)
                last = (c + 1) * P - 1
                link(dve.tensor_tensor_scan(M[:, cc], reset[:, 1, cc], ig[:, cc], mrow[:, 0, c:c + 1], ALU.add, ALU.max))
                link(dve.tensor_tensor(mrow[:, 0, c + 1:c + 2], M[:, last:last + 1], b[:, last:last + 1], ALU.add))
                dve.tensor_scalar(ex[:, cc], M[:, cc], -1.0, mrow[:, 0, c:c + 1], ALU.mult, ALU.add)
                dve.tensor_tensor(mrow[:, 2, c:c + 1], mrow[:, 0, c:c + 1], M[:, last:last + 1], ALU.subtract)
                link(dve.tensor_scalar(wk[:, cc], ig[:, cc], M[:, last:last + 1], None, ALU.subtract))
            dve.scalar_tensor_tensor(out=b, in0=b, scalar=-1.0, in1=M, op0=ALU.mult, op1=ALU.subtract).then_inc(S["rows"], 1)
            dve.memset(K.vm[:, :, :, M_DH:M_DH + 1], 1.0)
            for c in range(NC2):
                if c % 4 == 1 and c > 4:
                    K.ring.split(dve, n0 + c // 4 + 1)
                dst = K.qmT[:, c, :] if c < 8 else K.kmT[:, c - 8, :]
                a, ps = acc[:, c % 2, :], K.ps[c % 4]
                dve.wait_ge(S["first"], c + 1)
                for j in (2, 1, 0):
                    d = 3 - j
                    ins = dve.scalar_tensor_tensor(out=a[:, d:T], in0=ps[:, 0:T - d], scalar=cw[:, j, c:c + 1], in1=a[:, d:T],
                                                   op0=ALU.mult, op1=ALU.add)
                    if j:
                        link(ins)
                    else:
                        ins.then_inc(S["tap"], 1)
                dve.wait_ge(S["sig"], c + 1)
                dve.scalar_tensor_tensor(out=dst, in0=a, scalar=M_DH ** -0.5 if c < 8 else 1.0, in1=sgb[:, c % 2, :],
                                         op0=ALU.mult, op1=ALU.mult).then_inc(S["act"], 1)
            K.ring.split(dve, n0 + 5)


def mlstm_cell(nc, K):
    W1 = M_DH + 1
    N = NT * M_HEADS
    with ExitStack() as ctx:
        S = sems(nc, ctx, "sc kt num cup d1 w0 w wq kw den h c stat var root l", "L")
        sbt = lambda n, s: ctx.enter_context(nc.sbuf_tensor(n, s, F32))
        W, D1 = sbt("W", [P, 2, P]), sbt("D1", [P, 2, P])
        qI, kw = sbt("qI", [P, 2, 2, P]), sbt("kw", [P, 2, M_DH])
        C = sbt("C", [P, M_HEADS, 2, W1])
        den = sbt("den", [P, 2, N])
        bs, ba = sbt("bs", [P, N, 6]), sbt("ba", [P, N, 2])
        rs = sbt("rs", [P, N])
        block = ctx.enter_context(nc.Block())
        units = [(c, h) for c in range(NT) for h in range(M_HEADS)]
        psS, psK, psN, psC = K.ps[0:2], K.ps[2:4], K.ps[4:6], K.ps[6:8]
        G_, E_, K_ = 1, 0, 2

        @block.tensor
        def _(pe):
            def scores(i):
                c, h = units[i]
                cc = slice(c * P, (c + 1) * P)
                if i >= 2:
                    pe.wait_ge(S["w"], i - 1)
                    pe.wait_ge(S["kw"], i - 1)
                for j in range(2):
                    last = pe.matmul(psS[i % 2][:, 0:P], K.kmT[:, 2 * h + j, cc], K.qmT[:, 2 * h + j, cc], start=(j == 0), stop=(j == 1))
                last.then_inc(S["sc"], 1)
                for j in range(2):
                    last = pe.transpose(psK[i % 2][:, j * P:(j + 1) * P], K.kmT[:, 2 * h + j, cc], K.ident[:, :])
                last.then_inc(S["kt"], 1)

            scores(0)
            for i, (c, h) in enumerate(units):
                if i + 1 < N:
                    scores(i + 1)
                pe.wait_ge(S["w"], i + 1)
                if c:
                    pe.wait_ge(S["wq"], i - 3)
                    pe.wait_ge(S["c"], i - 3)
                if i >= 2:
                    pe.wait_ge(S["h"], i - 1)
                v = K.vm[:, c, h, :]
                last = pe.matmul(psN[i % 2][:, 0:W1], W[:, i % 2, :], v, start=True, stop=(c == 0))
                if c:
                    for j in range(2):
                        last = pe.matmul(psN[i % 2][:, 0:W1], qI[:, i % 2, j, :], C[:, h, j, :], start=False, stop=(j == 1))
                last.then_inc(S["num"], 1)
                if c < NT - 1:
                    pe.wait_ge(S["kw"], i + 1)
                    if i:
                        pe.wait_ge(S["c"], i)
                    for j in range(2):
                        last = pe.matmul(psC[j][:, 0:W1], kw[:, i % 2, j * P:(j + 1) * P], v, start=True, stop=True)
                    last.then_inc(S["cup"], 1)

        @block.scalar
        def _(act):
            for i, (c, h) in enumerate(units):
                act.wait_ge(S["d1"], i + 1)
                nc.scalar.activation(D1[:, i % 2, :], D1[:, i % 2, :], ACT.Exp, scale=-1.0).then_inc(S["w0"], 1)
                act.wait_ge(S["kt"], i + 1)
                if i >= 2:
                    act.wait_ge(S["cup"], min(i - 1, 12))
                nc.scalar.activation(kw[:, i % 2, :], psK[i % 2][:, 0:2 * P], ACT.Copy, scale=K.cols[:, K_, i:i + 1]).then_inc(S["kw"], 1)
            act.wait_ge(S["var"], 1)
            nc.scalar.activation(rs[:, :], rs[:, :], ACT.Sqrt).then_inc(S["root"], 1)

        @block.vector
        def _(dve):
            link = linker(dve, S["l"])

            def weights(i):
                c, h = units[i]
                cc = slice(c * P, (c + 1) * P)
                if i >= 2:
                    dve.wait_ge(S["num"], i - 1)
                    dve.wait_ge(S["w"], i - 1)
                dve.tensor_scalar(D1[:, i % 2, :], K.MB[:, h, cc], K.cols[:, G_, i:i + 1], 0.0, ALU.subtract, ALU.max).then_inc(S["d1"], 1)
                if c:
                    dve.tensor_tensor(qI[:, i % 2, :, :], K.qmT[:, 2 * h:2 * h + 2, cc],
                                      K.WI[:, h, cc].unsqueeze(1).to_broadcast([P, 2, P]), ALU.mult).then_inc(S["wq"], 1)
                dve.wait_ge(S["w0"], i + 1)
                link(dve.tensor_tensor(D1[:, i % 2, :], D1[:, i % 2, :], K.causal[:, :], ALU.mult))
                dve.wait_ge(S["sc"], i + 1)
                dve.tensor_tensor(W[:, i % 2, :], D1[:, i % 2, :], psS[i % 2][:, 0:P], ALU.mult).then_inc(S["w"], 1)

            weights(0)
            for i, (c, h) in enumerate(units):
                if i + 1 < N:
                    weights(i + 1)
                dve.wait_ge(S["num"], i + 1)
                a, r = den[:, 0, i:i + 1], den[:, 1, i:i + 1]
                dot = psN[i % 2][:, M_DH:W1]
                link(dve.tensor_scalar(a, dot, -1.0, K.cols[:, E_, i:i + 1], ALU.mult, ALU.max))
                link(dve.tensor_tensor(a, a, dot, ALU.max))
                link(dve.reciprocal(r, a))
                hm = K.hm[:, c, h, :]
                dve.tensor_scalar(hm, psN[i % 2][:, 0:M_DH], r, None, ALU.mult).then_inc(S["h"], 1)
                if c < NT - 1:
                    dve.wait_ge(S["cup"], i + 1)
                    for j in range(2):
                        if c == 0:
                            last = dve.tensor_copy(C[:, h, j, :], psC[j][:, 0:W1])
                        else:
                            last = dve.scalar_tensor_tensor(out=C[:, h, j, :], in0=C[:, h, j, :], scalar=K.dec[:, 4 * h + c:4 * h + c + 1],
                                                            in1=psC[j][:, 0:W1], op0=ALU.mult, op1=ALU.add)
                    last.then_inc(S["c"], 1)
                dve.wait_ge(S["h"], i + 1)
                link(dve.bn_stats(bs[:, i, :], hm))
                link(dve.bn_aggr(ba[:, i, :], bs[:, i, :]))
            dve.tensor_scalar(rs[:, :], ba[:, :, 1], EPS, None, ALU.add).then_inc(S["var"], 1)
            dve.wait_ge(S["root"], 1)
            link(dve.reciprocal(rs[:, :], rs[:, :]))
            for i, (c, h) in enumerate(units):
                hm = K.hm[:, c, h, :]
                dve.tensor_scalar(hm, hm, ba[:, i, 0:1], rs[:, i:i + 1], ALU.subtract, ALU.mult)


def mlstm_output(nc, K, n0, load_upto):
    I = K.I
    with ExitStack() as ctx:
        S = sems(nc, ctx, "mm sig tr out par", "O")
        so = ctx.enter_context(nc.sbuf_tensor("so", [P, 2, T], F32))
        gm = ctx.enter_context(nc.sbuf_tensor("gm", [P, KD], F32))
        K.ring.used = {n0 + i: (S["mm"], 4 * i + 4) for i in range(2)}
        block = ctx.enter_context(nc.Block())

        @block.sync
        def _(sp):
            with nc.allow_non_contiguous_dma(reason="one gain per partition"):
                sp.dma_start(gm[:, :], I["mlstm_norm_g_2"][0].rearrange("(c p) -> p c", p=P)).then_inc(S["par"], 16)
            K.ring.load(sp, load_upto)
            sp.wait_ge(S["par"], 16)

        @block.tensor
        def _(pe):
            for c in range(KD):
                K.ring.wait(pe, n0 + c // 4, c % 4)
                if c >= 2:
                    pe.wait_ge(S["sig"], c - 1)
                mm_feature(pe, K.ps[c % 2][:, :], (K.ring, n0 + c // 4), slice((c % 4) * P, (c % 4) * P + P), K.hp, KD).then_inc(S["mm"], 1)
                if c >= 2:
                    pe.wait_ge(S["out"], c - 1)
                for t in range(NT):
                    last = pe.transpose(K.ps[2 + c % 2][:, t * P:(t + 1) * P], K.hm[:, t, c // 2, (c % 2) * P:(c % 2) * P + P], K.ident[:, :])
                last.then_inc(S["tr"], 1)

        @block.scalar
        def _(act):
            for c in range(KD):
                act.wait_ge(S["mm"], c + 1)
                if c >= 2:
                    act.wait_ge(S["out"], c - 1)
                nc.scalar.activation(so[:, c % 2, :], K.ps[c % 2][:, :], ACT.Sigmoid).then_inc(S["sig"], 1)

        @block.vector
        def _(dve):
            K.ring.split(dve, n0)
            K.ring.split(dve, n0 + 1)
            dve.wait_ge(S["par"], 16)
            for c in range(KD):
                dve.wait_ge(S["tr"], c + 1)
                dve.wait_ge(S["sig"], c + 1)
                dve.scalar_tensor_tensor(out=K.ymT[:, c, :], in0=K.ps[2 + c % 2][:, :], scalar=gm[:, c:c + 1], in1=so[:, c % 2, :],
                                         op0=ALU.mult, op1=ALU.mult).then_inc(S["out"], 1)


def second_attention_inputs(nc, K, n0, load_upto):
    I = K.I
    with ExitStack() as ctx:
        S = sems(nc, ctx, "mm cop par one bmm bcop st", "Q")
        rb = ctx.enter_context(nc.sbuf_tensor("rb", [33, 24], F32))
        dist = ctx.enter_context(nc.sbuf_tensor("dist", [33, 640], F32))
        R = ctx.enter_context(nc.sbuf_tensor("R", [8, 640], F32))
        K.ring.used = {n0 + i: (S["mm"], 4 * i + 4) for i in range(9)}
        block = ctx.enter_context(nc.Block())

        @block.sync
        def _(sp):
            sp.wait_ge(S["one"], 1)
            sp.dma_start(rb[0:32, :], I["rel_bias_2"]).then_inc(S["par"], 16)
            sp.dma_start(K.flip[:, :], I["c_flip"]).then_inc(S["par"], 16)
            sp.dma_start(dist[:, :], I["c_dist"][:, 0, :]).then_inc(S["par"], 16)
            for g in range(3):
                if g:
                    sp.wait_ge(S["bmm"], g)
                    sp.dma_start(dist[:, :], I["c_dist"][:, g, :]).then_inc(S["par"], 16)
                K.ring.load(sp, n0 + 3 + g)
                sp.wait_ge(S["bcop"], g + 1)
                sp.dma_start(K.R_dram[g, :, :], R[:, :]).then_inc(S["st"], 16)
            sp.wait_ge(S["st"], 48)
            K.ring.load(sp, load_upto)

        @block.tensor
        def _(pe):
            for c in range(24):
                n = n0 + c // 4
                K.ring.wait(pe, n, c % 4)
                if c >= 4:
                    pe.wait_ge(S["cop"], c - 3)
                mm_feature(pe, K.ps[c % 4][:, :], (K.ring, n), slice((c % 4) * P, (c % 4) * P + P), K.hp, KD).then_inc(S["mm"], 1)
                if c in (4, 8, 12):
                    g = c // 4 - 1
                    pe.wait_ge(S["par"], 48 + 16 * g)
                    if g:
                        pe.wait_ge(S["bcop"], g)
                    pe.matmul(K.ps[4][0:8, :], rb[:, 8 * g:8 * g + 8], dist[:, 0:512], start=True, stop=True)
                    pe.matmul(K.ps[5][0:8, 0:128], rb[:, 8 * g:8 * g + 8], dist[:, 512:640], start=True, stop=True).then_inc(S["bmm"], 1)
            for j in range(12):
                s, t = j // NT, j % NT
                pe.wait_ge(S["cop"], 24 + j - 3)
                mm_tokens(pe, K.ps[j % 4][:, :], (K.ring, n0 + 6 + s), slice(0, 512), K.hp, KD, t).then_inc(S["mm"], 1)

        @block.scalar
        def _(act):
            for c in range(36):
                act.wait_ge(S["mm"], c + 1)
                ps = K.ps[c % 4][:, :]
                if c < 12:
                    ins = nc.scalar.activation(K.qa[:, c, :], ps, ACT.Copy, scale=0.125)
                elif c < 24:
                    ins = nc.scalar.activation(K.ka[:, c - 12, :], ps, ACT.Copy)
                else:
                    s, t = (c - 24) // NT, (c - 24) % NT
                    ins = nc.scalar.activation(K.va2[:, t, s * 512:(s + 1) * 512], ps, ACT.Copy)
                ins.then_inc(S["cop"], 1)

        @block.vector
        def _(dve):
            dve.memset(rb[:, :], 1.0).then_inc(S["one"], 1)
            K.ring.split(dve, n0)
            K.ring.split(dve, n0 + 1)
            for g in range(3):
                K.ring.split(dve, n0 + 2 + g)
                dve.wait_ge(S["bmm"], g + 1)
                if g:
                    dve.wait_ge(S["st"], 16 * g)
                dve.tensor_copy(R[:, 0:512], K.ps[4][0:8, :])
                dve.tensor_copy(R[:, 512:640], K.ps[5][0:8, 0:128]).then_inc(S["bcop"], 1)
            for n in range(n0 + 5, n0 + 9):
                K.ring.split(dve, n)


def feed_forward(nc, K, n0, load_upto):
    NF = FF2 // P
    rounds = [range(c, min(c + 4, NF)) for c in range(0, NF, 4)]
    down = n0 + 2 * len(rounds)
    with ExitStack() as ctx:
        S = sems(nc, ctx, "mm sig gated uped hid down fl", "F")
        hid, hid_low = twins(nc, ctx, "hid", [P, NF, T])
        hid_high = ctx.enter_context(nc.sbuf_tensor("hid_high", [P, NF, T], F32R))
        K.ring.used = {}
        for q, cs in enumerate(rounds):
            for j in range(2):
                K.ring.used[n0 + 2 * q + j] = (S["mm"], 8 * q + (j + 1) * len(cs))
            K.ring.used[down + q] = (S["down"], q + 1)
        block = ctx.enter_context(nc.Block())

        @block.sync
        def _(sp):
            K.ring.load(sp, load_upto)

        @block.tensor
        def _(pe):
            for q, cs in enumerate(rounds):
                for j in range(2):
                    n = n0 + 2 * q + j
                    for c in cs:
                        K.ring.wait(pe, n, c % 4)
                        if q:
                            pe.wait_ge(S["uped" if j else "gated"], c - 3)
                        mm_feature(pe, K.ps[4 * j + c % 4][:, :], (K.ring, n), slice((c % 4) * P, (c % 4) * P + P), K.hp,
                                   KD).then_inc(S["mm"], 1)
            pe.wait_ge(S["hid"], NF)
            for q, cs in enumerate(rounds):
                for f in cs:
                    K.ring.wait(pe, down + q, f % 4)
                    for t in range(NT):
                        for half in range(2):
                            last = product(pe, K.ps[2 * t + half][:, :], [x[:, f, t * P:(t + 1) * P] for x in (hid_high, hid_low)],
                                           K.ring.cut(down + q, f % 4, slice(half * 512, (half + 1) * 512)), f == 0, f == NF - 1)
                last.then_inc(S["down"], 1)

        @block.scalar
        def _(act):
            for q, cs in enumerate(rounds):
                for i, c in enumerate(cs):
                    act.wait_ge(S["mm"], 8 * q + i + 1)
                    nc.scalar.activation(hid[:, c, :], K.ps[c % 4][:, :], ACT.Sigmoid).then_inc(S["sig"], 1)

        @block.vector
        def _(dve):
            link = linker(dve, S["fl"])
            K.ring.split(dve, n0)
            K.ring.split(dve, n0 + 1)
            for q, cs in enumerate(rounds):
                for i, c in enumerate(cs):
                    if i == 1 and q:
                        K.ring.split(dve, n0 + 2 * q + 1)
                    dve.wait_ge(S["sig"], c + 1)
                    dve.tensor_tensor(hid[:, c, :], hid[:, c, :], K.ps[c % 4][:, :], ALU.mult).then_inc(S["gated"], 1)
                for i, c in enumerate(cs):
                    if i == 1:
                        K.ring.split(dve, n0 + 2 * q + 2)
                    dve.wait_ge(S["gated"], c + 1)
                    dve.wait_ge(S["mm"], 8 * q + len(cs) + i + 1)
                    dve.tensor_tensor(hid[:, c, :], hid[:, c, :], K.ps[4 + c % 4][:, :], ALU.mult).then_inc(S["uped"], 1)
                    dve.wait_ge(S["uped"], c + 1)
                    link(high(dve, hid_high[:, c, :], hid[:, c, :]))
                    low(dve, hid_low[:, c, :], hid[:, c, :], hid_high[:, c, :]).then_inc(S["hid"], 1)
            for q in range(1, len(rounds)):
                K.ring.split(dve, down + q)
            dve.wait_ge(S["down"], len(rounds))
            for t in range(NT):
                for half in range(2):
                    o = K.x[:, t, half * 512:(half + 1) * 512]
                    dve.tensor_tensor(o, o, K.ps[2 * t + half][:, :], ALU.add)


def build(nc, I, out):
    ctx = ExitStack()
    with ctx:
        sb = lambda n, s, dt=F32: ctx.enter_context(nc.sbuf_tensor(n, s, dt))
        K = Buffers()
        K.I = I
        K.ps = [ctx.enter_context(nc.psum_tensor(f"ps{i}", [P, 512], F32)) for i in range(8)]
        K.ring = R = Ring(nc, ctx)
        K.ident = sb("ident", [P, P])
        w_in = I["w_in"][0]
        b_first = [R.plan(w_in[:, c:min(c + 512, 2688)], KD, min(512, 2688 - c)) for c in range(0, 2688, 512)][0]
        e_first = len(R.loads)
        for c in range(0, 2 * D, 512):
            R.plan(w_in[:, 2688 + c:2688 + c + 512], KD, 512)
        R.plan(I["w_proj_rwkv"][0], 4, D)
        R.plan(I["w_proj_attn"][0], 4, D)
        for c in range(0, D, 512):
            R.plan(I["w_out"][0][:, c:c + 512], KD, 512, rows=True)
        moe_first = len(R.loads)
        for e in range(N_EXP):
            for w in ("exp_w_gate", "exp_w_up", "exp_w_down"):
                for half in range(2):
                    R.plan_whole(I[w][0, e, half * 512:half * 512 + 512, :], 4, D, len(R.loads) - moe_first)
        second = len(R.loads)
        w2 = I["w_in_2"][0]
        for c0, cols in ((Q_M, 1024), (K_M, 1024), (V_M, 1024), (O_M, 1024), (Q_A, 1536), (K_A, 1536), (V_A, 1536), (G_A, 2048)):
            for c in range(c0, c0 + cols, 512):
                R.plan(w2[:, c:c + 512], KD, 512, rows=c0 in (V_M, V_A))
        for c in range(0, D, 512):
            R.plan(I["w_proj_a_2"][0][:, c:c + 512], KD, 512)
        R.plan(I["w_proj_b_2"][0], 4, D)
        for c in range(0, D, 512):
            R.plan(I["w_out_2"][0][:, c:c + 512], KD, 512, rows=True)
        ffn = len(R.loads)
        for c in range(0, FF2, 512):
            w = min(512, FF2 - c)
            for name in ("w_gate_2", "w_up_2"):
                R.plan(I[name][0][:, c:c + w], KD, w)
        for f in range(0, FF2, 512):
            w = min(512, FF2 - f)
            R.plan(I["w_down_2"][0][f:f + w, :], w // P, D, rows=True)
        K.x = sb("x", [P, NT, D])
        xs = I["x"][0]
        S0 = sems(nc, ctx, "consts moved parted")
        with ExitStack() as one:
            sb1 = lambda n, s: one.enter_context(nc.sbuf_tensor(n, s, F32))
            with nc.Block() as block:
                @block.sync
                def _(sp):
                    sp.dma_start(K.ident[:, :], I["c_ident"]).then_inc(S0["consts"], 16)
                    sp.wait_ge(S0["consts"], 16)
            K.hT, h_low = twins(nc, one, "hT", [P, KD, T])
            K.yaT, ya_low = twins(nc, one, "yaT", [P, 4, T])
            K.u, u_parts = twins(nc, one, "u", [P, RC, T])
            with ExitStack() as att:
                sb2 = lambda n, s: att.enter_context(nc.sbuf_tensor(n, s, F32))
                K.qT, K.kT, K.va = sb2("qT", [P, 4, T]), sb2("kT", [P, 2, T]), sb2("va", [P, NT, P])
                K.sink = sb2("sink", [P, A_HEADS])
                with nc.sbuf_tensor("h_high", [P, KD, T], F32R) as hh, nc.sbuf_tensor("h_low", [P, KD, T], F32R) as hl:
                    K.hp = (hh, hl)
                    norm_transposed(nc, K, "1", K.x, I["norm_mix_g"][0], K.x, K.hT, xs, PAIR, K.hp)
                    first_projection(nc, K, b_first)
                K.absrel = sb2("absrel", [P, 3 * P])
                ya = sb2("ya", [P, NT, 512])
                with nc.Block() as block:
                    @block.sync
                    def _(sp):
                        sp.dma_start(K.absrel[:, :], I["c_absrel"]).then_inc(S0["consts"], 16)
                        sp.wait_ge(S0["consts"], 32)
                items = []
                for n in range(NT):
                    lo, hi = max(n - 1, 0), min(n + 1, NT - 1)
                    for h in range(A_HEADS):
                        b, g = 64 * (h % 2), h // 4
                        w = (hi - lo + 1) * P
                        r0 = (lo - (n - 1)) * P
                        items.append(dict(
                            segs=[(K.qT[b:b + 64, h // 2, n * P:(n + 1) * P], K.kT[b:b + 64, g, lo * P:(hi + 1) * P], w,
                                   K.absrel[:, r0:r0 + w], -(2.0 ** (-8.0 * (h + 1) / A_HEADS)))],
                            values=[K.va[:, kb, 64 * g:64 * g + 64] for kb in range(lo, hi + 1)],
                            sink=K.sink[:, h:h + 1], at=ya[:, n, 64 * h:64 * h + 64]))
                attention(nc, K, "A", items, ya, 3 * P, K.yaT)
            with ExitStack() as rw:
                sb2 = lambda n, s: rw.enter_context(nc.sbuf_tensor(n, s, F32))
                K.par = sb2("par", [P, 10, 4])
                K.wup, K.aup, K.gup = sb2("wup", [P, RW]), sb2("aup", [P, RW]), sb2("gup", [P, RW])
                K.masks, K.masks_t = sb2("masks", [P, 2, 2, P]), sb2("masks_t", [P, 2, 64])
                K.heads1, K.chunk0 = sb2("heads1", [P, P]), sb2("chunk0", [P, T])
                K.kk, K.ksum = sb2("kk", [P, 2, T]), sb2("ksum", [P, 2, T])
                K.SV = sb2("SV", [P, NCH, 2, 2, 64])
                K.Y = sb2("Y", [P, NCH, 2, 64])
                K.AR, K.BK = sb2("AR", [P, 2, NCH, 2, CHUNK]), sb2("BK", [P, 2, NCH, 2, CHUNK])
                K.DC = sb2("DC", [P, 2, NCH])
                K.tmp = [K.x[:, i, :].rearrange("p (c t) -> p c t", c=2) for i in range(4)]
                rwkv_setup(nc, K)
                for hf in range(2):
                    rwkv_keys(nc, K, hf)
                    for d in range(2):
                        rwkv_decays(nc, K, hf, d)
                        rwkv_chunks(nc, K, hf, d)
                    rwkv_output(nc, K, hf)
            K.yrT = K.u[:, 0:4, :]
            with nc.sbuf_tensor("h_high1", [P, KD, T], F32R) as hh:
                with nc.Block() as block:
                    @block.sync
                    def _(sp):
                        for t in range(NT):
                            sp.dma_start(K.x[:, t, :], xs[t * P:(t + 1) * P, :]).then_inc(S0["consts"], 16)
                        sp.wait_ge(S0["consts"], 32 + 16 * NT)

                    @block.vector
                    def _(dve):
                        high(dve, hh[:, :, :], K.hT[:, :, :]).then_inc(S0["parted"], 1)
                        dve.wait_ge(S0["parted"], 1)
                        low(dve, h_low[:, :, :], K.hT[:, :, :], hh[:, :, :])
                K.hp = (hh, h_low)
                merge_branches(nc, K, "E", [e_first + i for i in range(4)],
                               [(K.yrT, (u_parts[:, 4:8, :], u_parts[:, 0:4, :]), 4, [e_first + 4]),
                                (K.yaT[:, :, :], (u_parts[:, 8:12, :], ya_low[:, :, :]), 4, [e_first + 5])],
                               [e_first + 6, e_first + 7], moe_first + RING)
            K.x1 = K.x
        with ExitStack() as moe:
            sb1 = lambda n, s: moe.enter_context(nc.sbuf_tensor(n, s, F32))
            K.xn = sb1("xn", [P, NT, D])
            K.IB = sb1("IB", [P, N_EXP, 256])
            K.tok, K.gf = sb1("tok", [P, NT]), sb1("gf", [P, KD])
            with nc.sbuf_tensor("hT2", [P, KD, T], F32) as K.hT:
                norm_transposed(nc, K, "2", K.x, I["norm_ffn_g"][0], K.xn, K.hT)
                route(nc, K)
            experts(nc, K, moe_first, second + PAIR)
            K.x2 = K.x
        x3 = nc.dram_tensor("x3_dram", (T, D), F32, kind="Internal").ap()
        K.R_dram = nc.dram_tensor("bias_dram", (3, G2_HEADS, 640), F32, kind="Internal").ap()
        gain_norm(nc, K, "G1", I["norm_final_g"], keep_dram=x3)
        with ExitStack() as two:
            sb1 = lambda n, s: two.enter_context(nc.sbuf_tensor(n, s, F32))
            K.hT, h_low = twins(nc, two, "hT3", [P, KD, T])
            K.hp = (two.enter_context(nc.sbuf_tensor("h_high3", [P, KD, T], F32R)), h_low)
            norm_transposed(nc, K, "3", K.x, I["norm_mix_g_2"][0], K.x, K.hT, parts=K.hp)
            K.hm = K.x[:, :, :].rearrange("p t (h d) -> p t h d", h=M_HEADS)
            with ExitStack() as ml:
                sb2 = lambda n, s: ml.enter_context(nc.sbuf_tensor(n, s, F32))
                K.qmT, K.kmT = sb2("qmT", [P, KD, T]), sb2("kmT", [P, KD, T])
                K.vm = sb2("vm", [P, NT, M_HEADS, M_DH + 1])
                K.MB, K.WI = sb2("MB", [P, M_HEADS, T]), sb2("WI", [P, M_HEADS, T])
                K.cols, K.dec = sb2("cols", [P, 3, 16]), sb2("dec", [P, 16])
                K.sel4, K.causal = sb2("sel4", [4, 4, P]), sb2("causal", [P, P])
                mlstm_inputs(nc, K, second, second + 6 + PAIR)
                mlstm_cell(nc, K)
                K.ymT = K.qmT
                mlstm_output(nc, K, second + 6, second + 8 + PAIR)
                with nc.Block() as block:
                    @block.vector
                    def _(dve):
                        dve.tensor_copy(K.x[:, :, :].rearrange("p t (a b) -> p (t a) b", a=2), K.ymT[:, :, :])
            K.ymT = K.x[:, :, :].rearrange("p t (a b) -> p (t a) b", a=2)
            with_bias = ExitStack()
            BT, BT_parts = twins(nc, with_bias, "BT", [P, 2, 1280])
            K.ybT, yb_low = (t[:, :, :].rearrange("p a b -> p (a b)")[:, 0:4 * T].rearrange("p (c t) -> p c t", c=4)
                             for t in (BT, BT_parts))
            with ExitStack() as at:
                sb2 = lambda n, s: at.enter_context(nc.sbuf_tensor(n, s, F32))
                K.qa, K.ka, K.va2 = sb2("qa", [P, 12, T]), sb2("ka", [P, 12, T]), sb2("va2", [P, NT, 1536])
                K.flip = sb2("flip", [P, P])
                second_attention_inputs(nc, K, second + 8, second + 17 + PAIR)
                yb = sb2("yb", [P, NT, 512])
                items = []
                for h in range(G2_HEADS):
                    for n in range(NT):
                        segs, vals = [], []
                        for g, (lo, c0, w0) in enumerate(((max(n - 1, 0), 0, 256), (0, 256, 512), (0, 768, 512))):
                            ch, b = 4 * g + h // 2, 64 * (h % 2)
                            w = (n + 1 - lo) * P
                            segs.append((K.qa[b:b + 64, ch, n * P:(n + 1) * P], K.ka[b:b + 64, ch, lo * P:(n + 1) * P], w,
                                         BT[:, h % 2, c0 + w0 - w:c0 + w0], 1.0))
                            vals += [K.va2[:, kb, 512 * g + 64 * h:512 * g + 64 * h + 64] for kb in range(lo, n + 1)]
                        items.append(dict(segs=segs, values=vals, sink=None, at=yb[:, n, 64 * h:64 * h + 64]))
                attention(nc, K, "B", items, yb, 1280, K.ybT, flips=BT)
            with ExitStack() as mg:
                ym, ym_low = twins(nc, mg, "ym2", [P, KD, T])
                ym_high = mg.enter_context(nc.sbuf_tensor("ym_high", [P, KD, T], F32R))
                yb_high = mg.enter_context(nc.sbuf_tensor("yb_high", [P, 4, T], F32R))
                with nc.Block() as block:
                    @block.vector
                    def _(dve):
                        dve.tensor_copy(ym[:, :, :], K.ymT).then_inc(S0["moved"], 1)

                    @block.sync
                    def _(sp):
                        sp.wait_ge(S0["moved"], 1)
                        for t in range(NT):
                            sp.dma_start(K.x[:, t, :], x3[t * P:(t + 1) * P, :]).then_inc(S0["consts"], 16)
                        sp.wait_ge(S0["consts"], 32 + 32 * NT)
                merge_branches(nc, K, "H", [second + 17 + i for i in range(4)],
                               [(ym[:, :, :], (ym_high[:, :, :], ym_low[:, :, :]), KD, [second + 21, second + 22]),
                                (K.ybT, (yb_high[:, :, :], yb_low), 4, [second + 23])],
                               [second + 24, second + 25], ffn + PAIR)
            with_bias.close()
            K.x4 = K.x
            with nc.sbuf_tensor("xn4", [P, NT, D], F32) as xn4:
                norm_transposed(nc, K, "4", K.x, I["norm_ffn_g_2"][0], xn4, K.hT, parts=K.hp)
            feed_forward(nc, K, ffn, 10 ** 6)
        gain_norm(nc, K, "G2", I["norm_final_g_2"], out_dram=out)


def constants():
    rel = np.arange(3 * P)[None, :] - P - np.arange(P)[:, None]
    absrel = np.where(np.abs(rel) <= P, np.abs(rel), 1e33).astype(np.float32)
    s, t = np.arange(CHUNK)[:, None], np.arange(CHUNK)[None, :]
    masks, masks_t = np.zeros((P, 2, 2, P), np.float32), np.zeros((P, 2, CHUNK), np.float32)
    for d, (before, through) in enumerate(((s < t, s <= t), (s > t, s >= t))):
        for odd in range(2):
            b, k = slice(CHUNK * odd, CHUNK * odd + CHUNK), slice(CHUNK - CHUNK * odd, P - CHUNK * odd)
            masks[b, odd, d] = np.concatenate([-1.0 * before, 1.0 * through], 1)
            masks[k, odd, d] = np.concatenate([1.0 * before, 1.0 * through], 1)
            masks_t[b, d] = -1.0 * before.T
    heads1 = (np.arange(P)[:, None] // 64 == np.arange(P)[None, :] // 64).astype(np.float32)
    chunk0 = np.broadcast_to((np.arange(T) % CHUNK != 0).astype(np.float32), (P, T))
    reset = np.zeros((M_HEADS, 2, T), np.float32)
    reset[:, 0] = np.arange(T) % P != 0
    causal = (np.arange(P)[:, None] <= np.arange(P)[None, :]).astype(np.float32)
    dist = np.zeros((33, 3, 640), np.float32)
    for g, (window, dilation) in enumerate(WINDOWS):
        for r in range(640):
            n = 511 - r
            if n < 0 or n > window or n % dilation:
                dist[32, g, r] = -1e30
            else:
                large = 16 + int(np.float32(np.log(max(n, 16) / 16)) / np.float32(np.log(2048 / 16)) * np.float32(16))
                dist[n if n < 16 else min(large, 31), g, r] = 1.0
    return {"c_reset": reset, "c_causal": causal, "c_dist": dist, "c_flip": np.ascontiguousarray(np.eye(P, dtype=np.float32)[::-1]),
            "c_sel4": np.repeat(np.eye(M_HEADS, dtype=np.float32)[:, :, None], P, 2),
            "c_ident": np.eye(P, dtype=np.float32), "c_absrel": absrel, "c_masks": masks, "c_masks_t": masks_t,
            "c_sel": np.repeat(np.eye(N_EXP, dtype=np.float32)[:, :, None], P, 2),
            "c_tok": (np.arange(P)[:, None] + P * np.arange(NT)[None, :]).astype(np.float32),
            "c_heads1": heads1, "c_chunk0": chunk0}


_INS = ["x", "norm_mix_g", "w_in", "mu_prev", "mu_next", "w0_f", "w_up_f", "w0_b", "w_up_b", "a0_f", "a_up_f", "a0_b",
        "a_up_b", "g_up", "k_k", "k_a", "r_k", "ln_x_w", "ln_x_b", "attn_sink", "w_proj_rwkv", "w_proj_attn", "w_out",
        "norm_ffn_g", "w_router", "exp_w_gate", "exp_w_up", "exp_w_down", "norm_final_g", "norm_mix_g_2", "w_in_2",
        "b_gate_if_2", "conv_w_2", "conv_b_2", "mlstm_norm_g_2", "w_proj_a_2", "w_proj_b_2", "w_out_2",
        "norm_ffn_g_2", "w_gate_2", "w_up_2", "w_down_2", "rel_bias_2", "norm_final_g_2"]


def kernel(**inputs):
    import numpy as _np
    import concourse.bacc as _bacc
    from concourse.bass_utils import run_bass_kernel_spmd as _run

    nc = _bacc.Bacc("TRN2", target_bir_lowering=False, num_devices=1)
    arrays, aps = {}, {}
    for name, a in [(n, inputs[n]) for n in _INS] + list(constants().items()):
        a = _np.ascontiguousarray(a)
        arrays["in_" + name] = a
        aps[name] = nc.dram_tensor("in_" + name, a.shape, F32, kind="ExternalInput").ap()
    out = nc.dram_tensor("out_0", (1, T, D), F32, kind="ExternalOutput").ap()
    build(nc, aps, out[0])
    return _run(nc, [arrays], core_ids=[0]).results[0]["out_0"]
```

```python
import numpy as np
from contextlib import ExitStack

import concourse.bass as bass
from concourse import mybir

F32 = mybir.dt.float32
U32 = mybir.dt.uint32
I32 = mybir.dt.int32
F32R = mybir.dt.float32r
ALU = mybir.AluOpType
ACT = mybir.ActivationFunctionType
AX = mybir.AxisListType.X

P = 128
T = 512
D = 1024
NT = T // P
KD = D // P
EPS = 1e-6

R_HEADS, R_N = 8, 64
RW = R_HEADS * R_N
RWKV_COLS = 3 * RW + 128 + 4 * 64
RC = RWKV_COLS // P
CHUNK = 64
NCH = T // CHUNK
DECAY = float(np.exp(-0.5))
LNX_EPS = 64e-5
A_HEADS, A_DH = 8, 64
N_EXP, CAP, FF1 = 16, 64, 1024

M_HEADS, M_DH = 4, 256
G2_HEADS = 8
WINDOWS = ((128, 1), (512, 4), (2048, 16))
Q_M, K_M, V_M, IF_M = 0, 1024, 2048, 3072
O_M = IF_M + 2 * M_HEADS
Q_A = O_M + 1024
K_A = Q_A + 1536
V_A = K_A + 1536
G_A = V_A + 1536
FF2 = 2816

RING = 4
PAIR = 2
SLOT = KD * 512



def twins(nc, ctx, name, shape):
    at = -(-nc.sbuf_base // 32) * 32
    whole = ctx.enter_context(nc.sbuf_tensor(name, shape, F32))
    return whole, nc.alloc_sbuf_tensor_at(name + "_parts", shape, F32R, offset=at)


def high(dve, out, x):
    return dve.tensor_copy(out, x)


def low(dve, out, x, hi):
    return dve.tensor_tensor(out, x, hi.bitcast(F32), ALU.subtract)


def product(pe, ps, w, h, start, stop):
    (wh, wl), (hh, hl) = w, h
    pe.matmul(ps, wh, hh, start=start, stop=False)
    pe.matmul(ps, wh, hl, start=False, stop=False)
    return pe.matmul(ps, wl, hh, start=False, stop=stop)


class Ring:

    def __init__(self, nc, ctx):
        self.buf, self.parts = twins(nc, ctx, "ring", [P, RING, SLOT])
        self.full = [ctx.enter_context(nc.semaphore(f"ring_full{i}")) for i in range(RING)]
        self.ready = ctx.enter_context(nc.semaphore("ring_ready"))
        self.rounded = ctx.enter_context(nc.semaphore("ring_rounded"))
        self.loads, self.slots, self.landed, self.pieces = [], [], [], []
        self.count = [0] * RING
        self.total = 0
        self.issued = 0
        self.split_upto = 0
        self.used = {}

    def place(self, src, k, w, slot):
        self.count[slot] += 16
        self.loads.append((src, k, w))
        self.slots.append(slot)
        self.landed.append(self.count[slot])
        return len(self.loads) - 1

    def plan(self, src, k, w, rows=False):
        n = self.place(src, k, w, len(self.loads) % PAIR)
        num = min(4, k) if rows else min(4, w // P)
        step = (k if rows else w) // num
        cut = [(slice(i * step, (i + 1) * step), slice(0, w)) if rows else (slice(0, k), slice(i * step, (i + 1) * step))
               for i in range(num)]
        self.pieces.append((self.total, cut))
        self.total += num
        return n

    def plan_whole(self, src, k, w, j):
        self.pieces.append(None)
        return self.place(src, k, w, j % RING)

    def view(self, n, buf, slot):
        _, k, w = self.loads[n]
        return buf[:, slot, 0:k * w].rearrange("p (k w) -> p k w", k=k)

    def cut(self, n, k, cols):
        s = self.slots[n]
        return self.view(n, self.parts, PAIR + s)[:, k, cols], self.view(n, self.parts, s)[:, k, cols]

    def load(self, eng, upto):
        for n in range(self.issued, min(upto, len(self.loads))):
            last = n - PAIR if self.pieces[n] or self.pieces[n - PAIR] else n - 2 * PAIR
            if last in self.used:
                eng.wait_ge(*self.used[last])
            src, k, w = self.loads[n]
            eng.dma_start(self.view(n, self.buf, self.slots[n]), src.rearrange("(k p) w -> p k w", p=P)).then_inc(self.full[self.slots[n]], 16)
            self.issued = n + 1

    def split(self, dve, n, only=None):
        if n < self.split_upto:
            return
        s = self.slots[n]
        first, cut = self.pieces[n]
        todo = range(len(cut)) if only is None else (only,)
        if todo[0] == 0:
            dve.wait_ge(self.full[s], self.landed[n])
            if n - PAIR in self.used:
                dve.wait_ge(*self.used[n - PAIR])
        whole, hi, lo = self.view(n, self.buf, s), self.view(n, self.parts, PAIR + s), self.view(n, self.parts, s)

        def round_piece(i):
            k, w = cut[i]
            high(dve, hi[:, k, w], whole[:, k, w]).then_inc(self.rounded, 1)

        round_piece(todo[0])
        for i in todo:
            if i + 1 in todo:
                round_piece(i + 1)
            k, w = cut[i]
            dve.wait_ge(self.rounded, first + i + 1)
            low(dve, lo[:, k, w], whole[:, k, w], hi[:, k, w]).then_inc(self.ready, 1)
        if todo[-1] == len(cut) - 1:
            self.split_upto = n + 1

    def wait(self, pe, n, piece=None):
        first, cut = self.pieces[n]
        pe.wait_ge(self.ready, first + (len(cut) if piece is None else piece + 1))


def sems(nc, ctx, names, tag=""):
    made = {n: nc.alloc_semaphore(name=n + tag) for n in names.split()}

    def clear():
        for handle in made.values():
            nc.gpsimd.sem_clear(handle)
            nc.release_semaphore(handle)
    ctx.callback(clear)
    return made


class Buffers:
    pass


def linker(eng, sem):
    count = [0]

    def link(ins):
        count[0] += 1
        ins.then_inc(sem, 1)
        eng.wait_ge(sem, count[0])
    return link


GAINS = ("norm_mix_g", "norm_ffn_g", "norm_mix_g_2", "norm_ffn_g_2")
SMALL = 16 * (len(GAINS) + 1)


def norm_transposed(nc, K, tag, x, g, xn, hT, x_src=None, load_upto=0, parts=None, ahead=None):
    K.ring.used = {}
    with ExitStack() as ctx:
        S = sems(nc, ctx, "x_in0 x_in1 x_in2 x_in3 squared var_ok root_ok rec_ok xn_ok turned emptied highs", tag)
        sq = ctx.enter_context(nc.sbuf_tensor("sq" + tag, [P, D], F32))
        ss = ctx.enter_context(nc.sbuf_tensor("ss" + tag, [P, 4 * NT], F32))
        gc = K.gains[:, g, :]
        block = ctx.enter_context(nc.Block())

        def empty(eng, b):
            t, half = b // 2, b % 2
            eng.wait_ge(S["turned"], b + 1)
            for c in range(4):
                k = half * 4 + c
                o, ps = hT[:, k, t * P:(t + 1) * P], K.ps[b % 4][:, c * P:(c + 1) * P]
                if parts:
                    last = nc.scalar.activation(o, ps, ACT.Copy, scale=gc[:, k:k + 1])
                else:
                    last = eng.tensor_scalar(o, ps, gc[:, k:k + 1], None, ALU.mult)
            last.then_inc(S["emptied"], 1)

        @block.sync
        def _(sp):
            if x_src is not None:
                for t in range(NT):
                    sp.dma_start(x[:, t, :], x_src[t * P:(t + 1) * P, :]).then_inc(S[f"x_in{t}"], 16)
                sp.dma_start(K.ident[:, :], K.I["c_ident"]).then_inc(K.first_in, 16)
                with nc.allow_non_contiguous_dma(reason="one gain per partition"):
                    for i, name in enumerate(GAINS):
                        sp.dma_start(K.gains[:, i, :], K.I[name][0].rearrange("(k p) -> p k", p=P)).then_inc(K.small_in if i else K.first_in, 16)
                        if i == 0:
                            K.ring.load(sp, 1)
                sp.dma_start(K.w_router[:, :, :], K.I["w_router"][0].rearrange("(k p) e -> p k e", p=P)).then_inc(K.small_in, 16)
                sp.dma_start(K.tok[:, :], K.I["c_tok"]).then_inc(K.small_in, 16)
            K.ring.load(sp, load_upto)

        @block.scalar
        def _(act):
            def root(t):
                act.wait_ge(S["var_ok"], t + 1)
                nc.scalar.activation(ss[:, 2 * NT + t:2 * NT + t + 1], ss[:, NT + t:NT + t + 1], ACT.Sqrt).then_inc(S["root_ok"], 1)

            for t in range(NT):
                if x_src is not None:
                    act.wait_ge(S[f"x_in{t}"], 16)
                if t:
                    act.wait_ge(S["squared"], t)
                nc.scalar.activation(sq[:, :], x[:, t, :], ACT.Square, accum_out=ss[:, t:t + 1]).then_inc(S["squared"], 1)
                if t:
                    root(t - 1)
            root(NT - 1)
            if parts:
                act.wait_ge(*((K.first_in, 32) if x_src is not None else (K.small_in, SMALL)))
                for b in range(NT * 2):
                    empty(act, b)

        @block.vector
        def _(dve):
            for t in range(NT):
                col = lambda i: ss[:, i * NT + t:i * NT + t + 1]
                dve.wait_ge(S["squared"], t + 1)
                dve.tensor_scalar(col(1), col(0), 1.0 / D, EPS, ALU.mult, ALU.add).then_inc(S["var_ok"], 1)
                if ahead is not None:
                    K.ring.split(dve, ahead, t)
                dve.wait_ge(S["root_ok"], t + 1)
                dve.reciprocal(col(3), col(2)).then_inc(S["rec_ok"], 1)
                dve.wait_ge(S["rec_ok"], t + 1)
                dve.tensor_scalar(xn[:, t, :], x[:, t, :], col(3), None, ALU.mult).then_inc(S["xn_ok"], 1)
            if not parts:
                dve.wait_ge(K.small_in, SMALL)
                for b in range(NT * 2):
                    empty(dve, b)
            else:
                hi, lo = parts
                for b in range(NT * 2):
                    t, half = b // 2, b % 2
                    at = (slice(None), slice(4 * half, 4 * half + 4), slice(t * P, (t + 1) * P))
                    dve.wait_ge(S["emptied"], b + 1)
                    high(dve, hi[at], hT[at]).then_inc(S["highs"], 1)
                    dve.wait_ge(S["highs"], b + 1)
                    low(dve, lo[at], hT[at], hi[at])

        @block.tensor
        def _(pe):
            for b in range(NT * 2):
                t, half = b // 2, b % 2
                pe.wait_ge(S["xn_ok"], t + 1)
                if b == 0:
                    pe.wait_ge(K.first_in, 32)
                if b >= 4:
                    pe.wait_ge(S["emptied"], b - 3)
                for c in range(4):
                    k = half * 4 + c
                    last = pe.transpose(K.ps[b % 4][:, c * P:(c + 1) * P], xn[:, t, k * P:(k + 1) * P], K.ident[:, :])
                last.then_inc(S["turned"], 1)


def mm_feature(pe, ps, w, cols, hT, nk):
    ring, n = w
    for k in range(nk):
        last = product(pe, ps, ring.cut(n, k, cols), [t[:, k, :] for t in hT], k == 0, k == nk - 1)
    return last


def mm_tokens(pe, ps, w, cols, hT, nk, t, chunks=None):
    ring, n = w
    for k in range(nk):
        if chunks is not None:
            pe.wait_ge(chunks, k + 1)
        if t == 0:
            ring.wait(pe, n, k * len(ring.pieces[n][1]) // nk)
        last = product(pe, ps, [x[:, k, t * P:(t + 1) * P] for x in hT], ring.cut(n, k, cols), k == 0, k == nk - 1)
    return last


FLIP_SEGS = ((0, 256), (256, 512), (768, 512))


def load_biases(sp, K, flips, h):
    for g, (c0, w) in enumerate(FLIP_SEGS):
        base = K.R_dram[g, h:h + 1, 512 - w:512]
        src = bass.AP(tensor=base.tensor, offset=base.offset, ap=[[1, P], [1, w]])
        sp.dma_start(flips[:, h % 2, c0:c0 + w], src).then_inc(K.flip_in[h % 2], 16)


def attention(nc, K, tag, items, out, width, outT, flips=None):
    with ExitStack() as ctx:
        S = sems(nc, ctx, "scored biased maxed exped turned copied pved y_done chain o_turned o_copied flipped unflipped", tag)
        scored, biased, maxed, exped, turned = S["scored"], S["biased"], S["maxed"], S["exped"], S["turned"]
        copied, pved, y_done, chain, o_turned = S["copied"], S["pved"], S["y_done"], S["chain"], S["o_turned"]
        sbt = lambda n, s: ctx.enter_context(nc.sbuf_tensor(n + tag, s, F32))
        SB = 3
        if flips is None:
            Sb, PT = sbt("Sb", [P, SB, width]), sbt("PT", [P, 2, width])
        else:
            Sb, PT = (K.ring.buf[:, PAIR + i, 0:n * width].rearrange("p (s w) -> p s w", s=n) for i, n in ((0, SB), (1, 2)))
        N = len(items)
        nm, mx, den, rd, esk = (sbt(n, [P, N]) for n in ("anm", "amx", "aden", "ard", "aesk"))
        seg0, bank0 = [0], [0]
        for it in items:
            seg0.append(seg0[-1] + len(it["segs"]))
            bank0.append(bank0[-1] + -(-len(it["values"]) // 4))
        ps_s, ps_f, ps_t, ps_v = K.ps[0:3], K.ps[3], K.ps[4:6], K.ps[6:8]
        flip_segs = FLIP_SEGS
        block = ctx.enter_context(nc.Block())
        nout = out.shape[2] // P

        def key_blocks(i, b):
            return range(4 * b, min(4 * b + 4, len(items[i]["values"])))

        @block.sync
        def _(sp):
            if flips is None:
                return
            for h in range(2, G2_HEADS):
                sp.wait_ge(biased, seg0[NT * (h - 1)])
                load_biases(sp, K, flips, h)

        @block.tensor
        def _(pe):
            def flip(h, g):
                pe.wait_ge(K.flip_in[h % 2], 48 * (h // 2 + 1))
                if h or g:
                    pe.wait_ge(S["unflipped"], 3 * h + g)
                c0, w = flip_segs[g]
                pe.matmul(ps_f[:, 0:w], K.flip[:, :], flips[:, h % 2, c0:c0 + w], start=True, stop=True).then_inc(S["flipped"], 1)

            if flips is not None:
                for g in range(3):
                    flip(0, g)
            for i in range(N + 2):
                if i < N:
                    for j, (q, k, w, _, _) in enumerate(items[i]["segs"]):
                        g = seg0[i] + j
                        if g >= 3:
                            pe.wait_ge(biased, g - 2)
                        pe.matmul(ps_s[g % 3][:, 0:w], q, k, start=True, stop=True).then_inc(scored, 1)
                if flips is not None and i % NT and i // NT + 1 < G2_HEADS:
                    flip(i // NT + 1, i % NT - 1)
                if 1 <= i <= N:
                    pe.wait_ge(exped, i)
                    for b in range(bank0[i] - bank0[i - 1]):
                        g = bank0[i - 1] + b
                        if g >= 2:
                            pe.wait_ge(copied, g - 1)
                        for n, kb in enumerate(key_blocks(i - 1, b)):
                            last = pe.transpose(ps_t[g % 2][:, n * P:(n + 1) * P],
                                                Sb[:, (i - 1) % SB, kb * P:(kb + 1) * P], K.ident[:, :])
                        last.then_inc(turned, 1)
                if i >= 2:
                    j = i - 2
                    pe.wait_ge(copied, bank0[j + 1])
                    if j >= 2:
                        pe.wait_ge(y_done, j - 1)
                    vs = items[j]["values"]
                    for kb, v in enumerate(vs):
                        last = pe.matmul(ps_v[j % 2][:, 0:64], PT[:, j % 2, kb * P:(kb + 1) * P], v,
                                         start=(kb == 0), stop=(kb == len(vs) - 1))
                    last.then_inc(pved, 1)
            pe.wait_ge(y_done, N)
            for c in range(nout):
                if c >= 3:
                    pe.wait_ge(S["o_copied"], c - 2)
                for t in range(NT):
                    last = pe.transpose(ps_s[c % 3][:, t * P:(t + 1) * P], out[:, t, c * P:(c + 1) * P], K.ident[:, :])
                last.then_inc(o_turned, 1)

        @block.scalar
        def _(act):
            def unflip(h, g):
                act.wait_ge(S["flipped"], 3 * h + g + 1)
                c0, w = flip_segs[g]
                nc.scalar.activation(flips[:, h % 2, c0:c0 + w], ps_f[:, 0:w], ACT.Copy).then_inc(S["unflipped"], 1)

            if flips is not None:
                for g in range(3):
                    unflip(0, g)
            for i in range(N + 1):
                if flips is not None and i % NT and i // NT + 1 < G2_HEADS:
                    unflip(i // NT + 1, i % NT - 1)
                if i < N:
                    w = sum(s[2] for s in items[i]["segs"])
                    act.wait_ge(maxed, i + 1)
                    last = nc.scalar.activation(Sb[:, i % SB, 0:w], Sb[:, i % SB, 0:w], ACT.Exp,
                                                bias=nm[:, i:i + 1], accum_out=den[:, i:i + 1])
                    if items[i]["sink"] is not None:
                        last = nc.scalar.activation(esk[:, i:i + 1], nm[:, i:i + 1], ACT.Exp, bias=items[i]["sink"])
                    last.then_inc(exped, 1)
                if i >= 1:
                    j = i - 1
                    if j >= 2:
                        act.wait_ge(pved, j - 1)
                    for b in range(bank0[j + 1] - bank0[j]):
                        g = bank0[j] + b
                        act.wait_ge(turned, g + 1)
                        kb = key_blocks(j, b)
                        nc.scalar.activation(PT[:, j % 2, kb[0] * P:(kb[-1] + 1) * P],
                                             ps_t[g % 2][:, 0:len(kb) * P], ACT.Copy).then_inc(copied, 1)
            for c in range(nout):
                act.wait_ge(o_turned, c + 1)
                nc.scalar.activation(outT[:, c, :], ps_s[c % 3][:, :], ACT.Copy).then_inc(S["o_copied"], 1)

        @block.vector
        def _(dve):
            link = linker(dve, chain)
            for i in range(N + 2):
                if i < N:
                    if flips is not None:
                        dve.wait_ge(S["unflipped"], 3 * (i // NT + 1))
                    if i >= SB:
                        dve.wait_ge(turned, bank0[i - SB + 1])
                    c0 = 0
                    for j, (q, k, w, bias, scale) in enumerate(items[i]["segs"]):
                        g = seg0[i] + j
                        dve.wait_ge(scored, g + 1)
                        o = Sb[:, i % SB, c0:c0 + w]
                        dve.scalar_tensor_tensor(out=o, in0=bias, scalar=scale, in1=ps_s[g % 3][:, 0:w],
                                                 op0=ALU.mult, op1=ALU.add).then_inc(biased, 1)
                        c0 += w
                    dve.wait_ge(biased, seg0[i + 1])
                    if items[i]["sink"] is not None:
                        link(dve.tensor_reduce(mx[:, i:i + 1], Sb[:, i % SB, 0:c0], AX, ALU.max))
                        dve.tensor_scalar(nm[:, i:i + 1], mx[:, i:i + 1], items[i]["sink"], -1.0,
                                          ALU.max, ALU.mult).then_inc(maxed, 1)
                    else:
                        dve.tensor_reduce(nm[:, i:i + 1], Sb[:, i % SB, 0:c0], AX, ALU.max, negate=True).then_inc(maxed, 1)
                if i >= 2:
                    j = i - 2
                    dve.wait_ge(exped, j + 1)
                    d = den[:, j:j + 1]
                    if items[j]["sink"] is not None:
                        link(dve.tensor_tensor(esk[:, j:j + 1], esk[:, j:j + 1], d, ALU.add))
                        d = esk[:, j:j + 1]
                    link(dve.reciprocal(rd[:, j:j + 1], d))
                    dve.wait_ge(pved, j + 1)
                    dve.tensor_scalar(items[j]["at"], ps_v[j % 2][:, 0:64], rd[:, j:j + 1], None,
                                      ALU.mult).then_inc(y_done, 1)


def first_projection(nc, K, first):
    I = K.I
    nch = 21
    with ExitStack() as ctx:
        S = sems(nc, ctx, "bmm bmu bc0 bscaled bprev bevac")
        mu = ctx.enter_context(nc.sbuf_tensor("mu", [P, 3, RC], F32))
        K.ring.used = {first + i: (S["bmm"], min(4 * i + 4, nch)) for i in range(6)}
        block = ctx.enter_context(nc.Block())

        @block.sync
        def _(sp):
            with nc.allow_non_contiguous_dma(reason="one mixing weight per partition"):
                sp.dma_start(mu[:, 0, :], I["mu_prev"][0].rearrange("(c p) -> p c", p=P)).then_inc(S["bmu"], 16)
                sp.dma_start(mu[:, 1, :], I["mu_next"][0].rearrange("(c p) -> p c", p=P)).then_inc(S["bmu"], 16)
                sp.dma_start(K.sink[:, :], I["attn_sink"].to_broadcast([P, A_HEADS])).then_inc(S["bmu"], 16)
            sp.dma_start(K.absrel[:, :], I["c_absrel"]).then_inc(S["bmu"], 16)
            K.ring.load(sp, first + 5 + PAIR)
            sp.wait_ge(S["bscaled"], 20)
            sp.dma_start(K.kT[64:128, 0, :], K.kT[0:64, 0, :]).then_inc(S["bmu"], 16)
            sp.dma_start(K.kT[0:64, 1, :], K.kT[64:128, 1, :]).then_inc(S["bmu"], 16)
            K.ring.load(sp, first + 6 + PAIR)
            sp.wait_ge(S["bmu"], 96)

        @block.tensor
        def _(pe):
            for c in range(nch):
                n = first + c // 4
                K.ring.wait(pe, n, c % 4)
                if c >= 4:
                    pe.wait_ge(S["bevac"] if c - 4 < RC else S["bscaled"], c - 3)
                w = K.ring, n
                ps = K.ps[c % 4]
                cw = (c % 4) * P
                if c < 20:
                    last = mm_feature(pe, ps[:, :], w, slice(cw, cw + P), K.hp, KD)
                else:
                    for t in range(NT):
                        last = mm_tokens(pe, ps[:, t * P:(t + 1) * P], w, slice(0, P), K.hp, KD, t)
                last.then_inc(S["bmm"], 1)

        @block.scalar
        def _(act):
            act.wait_ge(S["bc0"], 2)
            for c in range(nch):
                act.wait_ge(S["bmm"], c + 1)
                ps = K.ps[c % 4]
                if c < RC:
                    nc.scalar.activation(K.u[:, c, :], ps[:, :], ACT.Copy, scale=mu[:, 2, c:c + 1]).then_inc(S["bscaled"], 1)
                elif c < 19:
                    nc.scalar.activation(K.qT[:, c - RC, :], ps[:, :], ACT.Copy, scale=A_DH ** -0.5).then_inc(S["bscaled"], 1)
                elif c == 19:
                    nc.scalar.activation(K.kT[0:64, 0, :], ps[0:64, :], ACT.Copy)
                    nc.scalar.activation(K.kT[64:128, 1, :], ps[64:128, :], ACT.Copy).then_inc(S["bscaled"], 1)
                else:
                    nc.scalar.activation(K.va[:, :, :], ps[:, :].rearrange("p (t d) -> p t d", t=NT), ACT.Copy).then_inc(S["bscaled"], 1)

        @block.vector
        def _(dve):
            K.ring.split(dve, first)
            dve.wait_ge(S["bmu"], 64)
            dve.tensor_tensor(mu[:, 2, :], mu[:, 0, :], mu[:, 1, :], ALU.add).then_inc(S["bc0"], 1)
            dve.wait_ge(S["bc0"], 1)
            dve.tensor_scalar(mu[:, 2, :], mu[:, 2, :], -1.0, 1.0, ALU.mult, ALU.add).then_inc(S["bc0"], 1)
            K.ring.split(dve, first + 1)
            for c in range(nch):
                if c % 4 == 1 and 4 < c:
                    K.ring.split(dve, first + c // 4 + 1)
                if c >= RC:
                    continue
                dve.wait_ge(S["bscaled"], c + 1)
                u, ps = K.u[:, c, :], K.ps[c % 4]
                dve.scalar_tensor_tensor(out=u[:, 1:T], in0=ps[:, 0:T - 1], scalar=mu[:, 0, c:c + 1], in1=u[:, 1:T],
                                         op0=ALU.mult, op1=ALU.add).then_inc(S["bprev"], 1)
                dve.wait_ge(S["bprev"], c + 1)
                dve.scalar_tensor_tensor(out=u[:, 0:T - 1], in0=ps[:, 1:T], scalar=mu[:, 1, c:c + 1],
                                         in1=u[:, 0:T - 1], op0=ALU.mult, op1=ALU.add).then_inc(S["bevac"], 1)


def rwkv_setup(nc, K):
    I = K.I
    K.ring.used = {}
    with ExitStack() as ctx:
        S = sems(nc, ctx, "rpar rth")
        block = ctx.enter_context(nc.Block())
        cols = "w0_f w0_b a0_f a0_b k_k k_a k_a r_k ln_x_w ln_x_b".split()

        @block.sync
        def _(sp):
            n = 0
            with nc.allow_non_contiguous_dma(reason="one parameter per partition"):
                for j, name in enumerate(cols):
                    src = I[name][0] if name != "r_k" else I[name][0].rearrange("h n -> (h n)")
                    sp.dma_start(K.par[:, j, :], src.rearrange("(c p) -> p c", p=P)).then_inc(S["rpar"], 16)
            for dst, src in ((K.wup[0:64, :], I["w_up_f"][0]), (K.wup[64:128, :], I["w_up_b"][0]),
                             (K.aup[0:64, :], I["a_up_f"][0]), (K.aup[64:128, :], I["a_up_b"][0]),
                             (K.gup[:, :], I["g_up"][0]), (K.masks[:, :, :, :], I["c_masks"]),
                             (K.masks_t[:, :, :], I["c_masks_t"]), (K.heads1[:, :], I["c_heads1"]),
                             (K.chunk0[:, :], I["c_chunk0"])):
                sp.dma_start(dst, src).then_inc(S["rpar"], 16)
            sp.wait_ge(S["rpar"], 16 * (len(cols) + 9))

        @block.gpsimd
        def _(pool):
            for t in (K.PX, K.PT, K.XF):
                pool.memset(t[:, :, :, :], 0.0)

        @block.scalar
        def _(act):
            nc.scalar.activation(K.u[:, 13, :], K.u[:, 13, :], ACT.Tanh)
            nc.scalar.activation(K.u[:, 12, :], K.u[:, 12, :], ACT.Sigmoid)

        @block.vector
        def _(dve):
            dve.wait_ge(S["rpar"], 16 * (len(cols) + 9))
            dve.tensor_scalar(K.par[:, 6, :], K.par[:, 5, :], -1.0, 1.0, ALU.mult, ALU.add)


W0, A0, GAIN_KK, GAIN_KA, GAIN_K1, GAIN_RK, LN_W, LN_B = 0, 2, 4, 5, 6, 7, 8, 9


def rwkv_keys(nc, K, hf):
    tag = f"k{hf}"
    with ExitStack() as ctx:
        S = sems(nc, ctx, "scaled squared summed rooted turned kl", tag)
        block = ctx.enter_context(nc.Block())
        raw, sq = K.tmp[0], K.tmp[1]
        uf = K.u[:, :, :].rearrange("p c t -> p (c t)")

        @block.vector
        def _(dve):
            for c in range(2):
                cp = 2 * hf + c
                dve.tensor_scalar(raw[:, c, :], K.u[:, 4 + cp, :], K.par[:, GAIN_KK, cp:cp + 1], None, ALU.mult).then_inc(S["scaled"], 1)
            link = linker(dve, S["kl"])
            for c in range(2):
                dve.wait_ge(S["rooted"], c + 1)
                link(dve.tensor_scalar(sq[:, c, :], sq[:, c, :], 1e-12, None, ALU.max))
                link(dve.reciprocal(sq[:, c, :], sq[:, c, :]))
                dve.tensor_tensor(K.kk[:, c, :], raw[:, c, :], sq[:, c, :], ALU.mult)

        @block.scalar
        def _(act):
            for c in range(2):
                act.wait_ge(S["scaled"], c + 1)
                nc.scalar.activation(sq[:, c, :], raw[:, c, :], ACT.Square).then_inc(S["squared"], 1)
            for c in range(2):
                act.wait_ge(S["summed"], c + 1)
                nc.scalar.activation(sq[:, c, :], K.ps[c][:, :], ACT.Sqrt).then_inc(S["rooted"], 1)
            for b in range(6):
                c, q = b // 3, 4 * (b % 3)
                act.wait_ge(S["turned"], b + 1)
                ps = K.ps[2 + b].rearrange("p (w f) -> p w f", f=P)
                if q < NCH:
                    nc.scalar.activation(K.SV[64:128, q:q + 4, c, 0, :], ps[64:128, :, 0:64], ACT.Copy)
                lo, hi = max(q, 1), min(q + 4, NCH + 1)
                nc.scalar.activation(K.SV[0:64, lo - 1:hi - 1, c, 1, :], ps[0:64, lo - q:hi - q, 64:128], ACT.Copy)

        @block.tensor
        def _(pe):
            for b in range(6):
                c, q = b // 3, 4 * (b % 3)
                for w in range(q, min(q + 4, NCH + 1)):
                    t0 = (8 + 2 * hf + c) * T + 64 * w - 64
                    last = pe.transpose(K.ps[2 + b][:, (w - q) * P:(w - q + 1) * P], uf[:, t0:t0 + P], K.ident[:, :])
                last.then_inc(S["turned"], 1)
            for c in range(2):
                pe.wait_ge(S["squared"], c + 1)
                pe.matmul(K.ps[c][:, :], K.heads1[:, :], sq[:, c, :], start=True, stop=True).then_inc(S["summed"], 1)


def rates(K, d):
    return (K.tmp[0] if d == 0 else K.rates1[0], K.tmp[2] if d == 0 else K.rates1[1], K.tmp[1], K.tmp[3])


def by_chunk(t):
    return t[:, :, :].rearrange("p c (n s) -> p c n s", s=CHUNK)


def decays_on_scalar(nc, K, S, d, act):
    sg, a, cs, e1 = rates(K, d)
    act.wait_ge(S["sums"], 1)
    e2 = cs if d == 0 else sg
    last = CHUNK - 1 if d == 0 else 0
    AR, BK = K.AR[d], K.BK[d]
    for c in range(2):
        nc.scalar.activation(AR[:, c, :, 0, :], by_chunk(e1)[:, c], ACT.Exp, scale=-DECAY)
        nc.scalar.activation(AR[:, c, :, 1, :], by_chunk(e2)[:, c], ACT.Exp, scale=-DECAY)
        yield
        nc.scalar.activation(K.DC[d][:, c, :], by_chunk(e2)[:, c, :, last], ACT.Exp, scale=-DECAY)
        nc.scalar.activation(BK[:, c, :, 0, :], by_chunk(e2)[:, c], ACT.Exp, scale=DECAY)
        nc.scalar.activation(BK[:, c, :, 1, :], by_chunk(e2)[:, c], ACT.Exp, scale=DECAY).then_inc(S["expd"], 1)
        yield


def decays_on_vector(K, S, hf, d, dve, link):
    sg, a, cs, e1 = rates(K, d)
    v4 = by_chunk
    r, k = K.u[:, 2 * hf:2 * hf + 2, :], K.u[:, 4 + 2 * hf:6 + 2 * hf, :]
    for c in range(2):
        if d == 0:
            dve.wait_ge(S["gated"], 2 * c + 1)
        link(dve.tensor_tensor_scan(cs[:, c, :], K.chunk0[:, :], sg[:, c, :], 0.0, ALU.mult, ALU.add))
        yield
    if d == 0:
        dve.tensor_tensor(e1[:, :, :], cs[:, :, :], sg[:, :, :], ALU.subtract).then_inc(S["sums"], 1)
    else:
        for c in range(2):
            link(dve.tensor_tensor(v4(e1)[:, c], v4(cs)[:, c, :, CHUNK - 1:CHUNK].to_broadcast([P, NCH, CHUNK]),
                                   v4(cs)[:, c], ALU.subtract))
            yield
        dve.tensor_tensor(sg[:, :, :], e1[:, :, :], sg[:, :, :], ALU.add).then_inc(S["sums"], 1)
    yield
    if d == 0:
        dve.wait_ge(S["gated"], 4)
    dve.wait_ge(S["sums"], 1)
    ak = cs if d == 1 else sg
    link(dve.tensor_tensor(ak[:, :, :], a[:, :, :], K.kk[:, :, :], ALU.mult))
    yield
    for c in range(2):
        cp = 2 * hf + c
        link(dve.tensor_scalar(a[:, c, :], a[:, c, :], K.par[:, GAIN_KA, cp:cp + 1], K.par[:, GAIN_K1, cp:cp + 1],
                               ALU.mult, ALU.add))
    yield
    link(dve.tensor_tensor(a[:, :, :], a[:, :, :], k, ALU.mult))
    yield
    if d == 0:
        link(dve.tensor_copy(K.ksum[:, :, :], a[:, :, :]))
    else:
        link(dve.tensor_tensor(K.ksum[:, :, :], K.ksum[:, :, :], a[:, :, :], ALU.add))
    yield
    for c in range(2):
        dve.wait_ge(S["expd"], c + 1)
        v3 = lambda t: t.rearrange("p (n s) -> p n s", s=CHUNK)
        AR, BK = K.AR[d], K.BK[d]
        dve.tensor_tensor(AR[:, c, :, 0, :], AR[:, c, :, 0, :], v4(K.kk)[:, c], ALU.mult)
        dve.tensor_tensor(AR[:, c, :, 1, :], AR[:, c, :, 1, :], v3(r[:, c, :]), ALU.mult)
        yield
        for par in range(2):
            rows = slice(64 * par, 64 * par + 64)
            for j, factor in ((par, ak), (1 - par, a)):
                o = BK[rows, c, :, j, :]
                ins = dve.tensor_tensor(o, o, v4(factor)[rows, c], ALU.mult)
            if c and par:
                ins.then_inc(S["made"], 1)
            yield


def rwkv_decays(nc, K, hf):
    tag = f"d{hf}"
    with ExitStack() as ctx:
        S = sems(nc, ctx, "lora gated sums expd made dl", tag)
        block = ctx.enter_context(nc.Block())

        @block.tensor
        def _(pe):
            for d in range(2):
                rows = slice(64 * d, 64 * d + 64)
                for c in range(2):
                    f = slice((2 * hf + c) * P, (2 * hf + c + 1) * P)
                    pe.matmul(K.ps[4 * d + c][:, :], K.wup[rows, f], K.u[rows, 13, :], start=True, stop=True).then_inc(S["lora"], 1)
                    pe.matmul(K.ps[4 * d + 2 + c][:, :], K.aup[rows, f], K.u[rows, 14, :], start=True, stop=True).then_inc(S["lora"], 1)

        @block.scalar
        def _(act):
            for d in range(2):
                sg, a, _, _ = rates(K, d)
                for c in range(2):
                    cp = 2 * hf + c
                    act.wait_ge(S["lora"], 4 * d + 2 * c + 2)
                    nc.scalar.activation(sg[:, c, :], K.ps[4 * d + c][:, :], ACT.Sigmoid, bias=K.par[:, W0 + d, cp:cp + 1]).then_inc(S["gated"], 1)
                    nc.scalar.activation(a[:, c, :], K.ps[4 * d + 2 + c][:, :], ACT.Sigmoid, bias=K.par[:, A0 + d, cp:cp + 1]).then_inc(S["gated"], 1)
            for _ in decays_on_scalar(nc, K, S, 0, act):
                pass

        @block.vector
        def _(dve):
            for _ in decays_on_vector(K, S, hf, 0, dve, linker(dve, S["dl"])):
                pass


def rwkv_chunks(nc, K, hf, ahead=None):
    tag = f"c{hf}"
    names = ("cleared sums expd made dl bk_mm products masked bk_turned powered0 powered1 p_copied0 p_copied1 x_added0 x_added1 r_ready r_copied n_ready "
             "n_copied state_mm state_ok y_copied cl")
    ROUNDS = 6
    with ExitStack() as ctx:
        S = sems(nc, ctx, names, tag)
        powered, p_copied, x_added = ([S[n + "0"], S[n + "1"]] for n in ("powered", "p_copied", "x_added"))
        sbt = lambda n, s: ctx.enter_context(nc.sbuf_tensor(n + tag, s, F32))
        M = sbt("M", [P, 2, 2, 2, P])
        PX, PT, XF = K.PX, K.PT, K.XF
        PB, X = PX[:, :, :, 0:P], PX[:, :, :, P:192]
        STEPS = 2 * NCH
        BKT = sbt("BKT", [P, 2, 2, P])
        RH = sbt("RH", [P, 2, 64])
        ST = sbt("ST", [P, 2, 64])
        block = ctx.enter_context(nc.Block())
        psM, psP, psQ, psC, psN = K.ps[0:2], K.ps[2:4], K.ps[4:6], K.ps[6], K.ps[7]
        MT, BT, R_, Y_, U_ = 256, 256, 0, 128, 256
        chunk = lambda s: s if s < NCH else STEPS - 1 - s
        pair = lambda t, w: t.rearrange("p (c w) -> p c w", w=w)
        halves = ((0, slice(0, 64)), (1, slice(64, 128)))

        @block.tensor
        def _(pe):
            def products(s):
                ch, q = chunk(s), s % 2
                AR, BK = K.AR[s // NCH], K.BK[s // NCH]
                if s == NCH:
                    pe.wait_ge(S["made"], 1)
                if s:
                    pe.wait_ge(S["masked"], s)
                if s >= 2:
                    pe.wait_ge(p_copied[q], 5 * (s // 2))
                for c in range(2):
                    for par, rows in halves:
                        pe.matmul(psM[par][:, c * P:(c + 1) * P], BK[rows, c, ch, :, :], AR[rows, c, ch, :, :],
                                  start=True, stop=True)
                for c in range(2):
                    for par, rows in halves:
                        last = pe.matmul(psM[par][rows, MT + c * 64:MT + c * 64 + 64], AR[rows, c, ch, 0, :],
                                         BK[rows, c, ch, par, :], start=True, stop=True)
                last.then_inc(S["products"], 1)
                for c in range(2):
                    last = pe.transpose(psQ[q][:, BT + c * P:BT + (c + 1) * P], BK[:, c, ch, :, :], K.ident[:, :])
                last.then_inc(S["bk_mm"], 1)

            def power(s, r):
                q, n = s % 2, s // 2
                if r == 0:
                    pe.wait_ge(S["masked"], s + 1)
                    pe.wait_ge(S["bk_turned"], s + 1)
                if n or r:
                    pe.wait_ge(p_copied[q], 5 * n + r)
                    pe.wait_ge(x_added[q], 6 * n + r)
                for c in range(2):
                    o = psP[q][:, c * 192:c * 192 + 192]
                    w = slice(0 if r < ROUNDS - 1 else P, 192 if r else P)
                    last = pe.matmul(o[:, w], PT[:, q, c, :], PX[:, q, c, w], start=True, stop=True)
                    if r < ROUNDS - 1:
                        last = pe.matmul(psQ[q][:, c * P:(c + 1) * P], PB[:, q, c, :], PT[:, q, c, :], start=True, stop=True)
                last.then_inc(powered[q], 1)

            def solve_in(s):
                ch, q = chunk(s), s % 2
                AR = K.AR[s // NCH]
                pe.wait_ge(S["masked"], s + 1)
                pe.wait_ge(S["state_ok"], s + 1)
                if s:
                    pe.wait_ge(S["y_copied"], s)
                if s == 0 or s >= NCH:
                    pe.wait_ge(S["cleared"], 2 if s == 0 else 2 * (ch + 2))
                for c in range(2):
                    for par, rows in halves:
                        o = psC[rows, R_ + c * 64:R_ + c * 64 + 64]
                        pe.matmul(o, M[:, q, c, par, 0:64], K.SV[:, ch, c, par, :], start=True, stop=False)
                        last = pe.matmul(o, AR[rows, c, ch, 0, :], ST[rows, c, :], start=False, stop=True)
                last.then_inc(S["r_ready"], 1)

            def solve(s):
                q = s % 2
                pe.wait_ge(S["r_copied"], s + 1)
                pe.wait_ge(x_added[q], 6 * (s // 2 + 1))
                for c in range(2):
                    last = pe.matmul(psN[:, c * 64:c * 64 + 64], XF[:, q, c, :], RH[:, c, :], start=True, stop=True)
                last.then_inc(S["n_ready"], 1)

            def finish(s):
                ch, q = chunk(s), s % 2
                AR = K.AR[s // NCH]
                pe.wait_ge(S["n_copied"], s + 1)
                for c in range(2):
                    for par, rows in halves:
                        o = psC[rows, Y_ + c * 64:Y_ + c * 64 + 64]
                        pe.matmul(o, M[:, q, c, par, 64:128], K.SV[:, ch, c, par, :], start=True, stop=False)
                        pe.matmul(o, AR[rows, c, ch, 1, :], ST[rows, c, :], start=False, stop=True)
                for c in range(2):
                    for par, rows in halves:
                        last = pe.matmul(psC[rows, U_ + c * 64:U_ + c * 64 + 64], BKT[:, q, c, rows],
                                         K.SV[:, ch, c, par, :], start=True, stop=True)
                last.then_inc(S["state_mm"], 1)

            products(0)
            products(1)
            for r in range(ROUNDS):
                power(0, r)
                power(1, r)
            solve_in(0)
            solve(0)
            for s in range(0, STEPS, 2):
                more = s + 2 < STEPS
                finish(s)
                if more:
                    products(s + 2)
                solve_in(s + 1)
                if more:
                    power(s + 2, 0)
                solve(s + 1)
                if more:
                    power(s + 2, 1)
                finish(s + 1)
                if more:
                    products(s + 3)
                    for r in range(ROUNDS):
                        if r + 2 < ROUNDS:
                            power(s + 2, r + 2)
                        if r == ROUNDS - 2:
                            solve_in(s + 2)
                        if r == ROUNDS - 1:
                            solve(s + 2)
                        power(s + 3, r)

        @block.gpsimd
        def _(pool):
            for par, rows in halves:
                pool.memset(K.SV[rows, :, :, par, :], 0.0).then_inc(S["cleared"], 1)
            for s in range(NCH):
                pool.wait_ge(S["state_mm"], s + 1)
                for par, rows in halves:
                    pool.memset(K.SV[rows, s, :, par, :], 0.0).then_inc(S["cleared"], 1)

        @block.scalar
        def _(act):
            reverse = decays_on_scalar(nc, K, S, 1, act)

            def turn(s):
                act.wait_ge(S["bk_mm"], s + 1)
                if s >= 2:
                    act.wait_ge(S["state_mm"], s - 1)
                nc.scalar.activation(BKT[:, s % 2, :, :], pair(psQ[s % 2][:, BT:BT + 256], P), ACT.Copy).then_inc(S["bk_turned"], 1)

            def copy_transposes(s, r):
                q = s % 2
                act.wait_ge(powered[q], 6 * (s // 2) + r + 1)
                nc.scalar.activation(PT[:, q, :, :], pair(psQ[q][:, 0:256], P), ACT.Copy).then_inc(p_copied[q], 1)

            def negate(s):
                act.wait_ge(S["r_ready"], s + 1)
                nc.scalar.activation(RH[:, :, :], pair(psC[:, R_:R_ + 128], 64), ACT.Copy, scale=-1.0).then_inc(S["r_copied"], 1)

            turn(0)
            turn(1)
            for r in range(ROUNDS - 1):
                copy_transposes(0, r)
                copy_transposes(1, r)
            negate(0)
            for s in range(0, STEPS, 2):
                more = s + 2 < STEPS
                if more:
                    turn(s + 2)
                negate(s + 1)
                if more:
                    copy_transposes(s + 2, 0)
                    copy_transposes(s + 2, 1)
                    turn(s + 3)
                    for r in range(ROUNDS - 1):
                        if r + 2 < ROUNDS - 1:
                            copy_transposes(s + 2, r + 2)
                        if r == ROUNDS - 2:
                            negate(s + 2)
                        copy_transposes(s + 3, r)
                        if s and r % 2 == 0:
                            next(reverse, None)

        @block.vector
        def _(dve):
            link = linker(dve, S["cl"])
            reverse = decays_on_vector(K, S, hf, 1, dve, linker(dve, S["dl"]))
            dve.memset(ST[:, :, :], 0.0).then_inc(S["state_ok"], 1)

            def mask(s):
                q, d = s % 2, s // NCH
                dve.wait_ge(S["products"], s + 1)
                if s >= 2:
                    dve.wait_ge(S["state_mm"], s - 1)
                    dve.wait_ge(x_added[q], 6 * (s // 2))
                for par, rows in halves:
                    dve.tensor_tensor(PT[rows, q, :, rows], pair(psM[par][rows, MT:MT + 128], 64),
                                      K.masks_t[rows, d, :].unsqueeze(1).to_broadcast([64, 2, 64]), ALU.mult)
                    last = dve.tensor_tensor(M[:, q, :, par, :], pair(psM[par][:, 0:256], P),
                                             K.masks[:, par, d, :].unsqueeze(1).to_broadcast([P, 2, P]), ALU.mult)
                link(last)
                for par, rows in halves:
                    dve.tensor_copy(PB[rows, q, :, rows], M[rows, q, :, par, 0:64])
                    last = dve.tensor_tensor(X[rows, q, :, :], M[rows, q, :, par, 0:64],
                                             K.ident[rows, rows].unsqueeze(1).to_broadcast([64, 2, 64]), ALU.add)
                last.then_inc(S["masked"], 1)

            def add_x(s, r):
                q = s % 2
                dve.wait_ge(powered[q], 6 * (s // 2) + r + 1)
                if r == ROUNDS - 1 and s >= 2:
                    dve.wait_ge(S["n_ready"], s - 1)
                if s >= 2 or r:
                    dve.wait_ge(x_added[q], 6 * (s // 2) + r)
                prod = pair(psP[q][:, 0:384], 192)
                if r == ROUNDS - 1:
                    for par, rows in halves:
                        last = dve.tensor_tensor(XF[rows, q, :, rows], X[rows, q, :, :], prod[rows, :, P:192], ALU.add)
                else:
                    if r < ROUNDS - 2:
                        last = dve.tensor_copy(PB[:, q, :, :], prod[:, :, 0:P])
                    if r:
                        last = dve.tensor_tensor(X[:, q, :, :], X[:, q, :, :], prod[:, :, P:192], ALU.add)
                last.then_inc(x_added[q], 1)

            def take_n(s):
                dve.wait_ge(S["n_ready"], s + 1)
                for par, rows in halves:
                    last = dve.tensor_copy(K.SV[rows, chunk(s), :, par, :], pair(psN[rows, 0:128], 64))
                last.then_inc(S["n_copied"], 1)

            def take_state(s):
                dve.wait_ge(S["state_mm"], s + 1)
                if s == NCH - 1:
                    dve.memset(ST[:, :, :], 0.0).then_inc(S["state_ok"], 1)
                else:
                    DC = K.DC[s // NCH]
                    link(dve.tensor_tensor(ST[:, :, :], ST[:, :, :], pair(psC[:, U_:U_ + 128], 64), ALU.add))
                    dve.tensor_tensor(ST[:, :, :], ST[:, :, :], DC[:, :, chunk(s):chunk(s) + 1].to_broadcast([P, 2, 64]),
                                      ALU.mult).then_inc(S["state_ok"], 1)
                y, prod = K.Y[:, chunk(s), :, :], pair(psC[:, Y_:Y_ + 128], 64)
                if s < NCH:
                    last = dve.tensor_copy(y, prod)
                else:
                    dve.wait_ge(S["y_copied"], chunk(s) + 1)
                    last = dve.tensor_tensor(y, y, prod, ALU.add)
                last.then_inc(S["y_copied"], 1)

            mask(0)
            mask(1)
            for r in range(ROUNDS):
                add_x(0, r)
                add_x(1, r)
            take_n(0)
            for s in range(0, STEPS, 2):
                more = s + 2 < STEPS
                take_state(s)
                if more:
                    mask(s + 2)
                    add_x(s + 2, 0)
                if ahead is not None and s >= NCH:
                    K.ring.split(dve, ahead, (s - NCH) // 2)
                take_n(s + 1)
                if more:
                    add_x(s + 2, 1)
                take_state(s + 1)
                if more:
                    mask(s + 3)
                    for r in range(ROUNDS):
                        if r + 2 < ROUNDS:
                            add_x(s + 2, r + 2)
                        if r == ROUNDS - 1:
                            take_n(s + 2)
                        add_x(s + 3, r)
                        next(reverse, None)


def rwkv_output(nc, K, hf):
    tag = f"o{hf}"
    with ExitStack() as ctx:
        S = sems(nc, ctx, "centred sqd vard rooted normed turned scaled bonus gate ol", tag)
        Y = K.Y[:, :, :, :].rearrange("p n c f -> p (n c) f")
        NG = 2 * NCH
        block = ctx.enter_context(nc.Block())
        sq = K.AR[0][:, 0, :, :, :].rearrange("p a b c -> p (a b) c")
        st = K.BK[0][:, 0, 0, 0, :]
        mean, rstd = st[:, 0:NG], st[:, NG:2 * NG]
        tb = K.tmp[0]
        z = K.tmp[1]

        @block.vector
        def _(dve):
            link = linker(dve, S["ol"])
            link(dve.tensor_reduce(mean, Y, AX, ALU.add))
            link(dve.tensor_scalar(mean, mean, 1.0 / 64, None, ALU.mult))
            dve.tensor_tensor(Y, Y, mean.unsqueeze(2).to_broadcast([P, NG, 64]), ALU.subtract).then_inc(S["centred"], 1)
            for c in range(2):
                cp = 2 * hf + c
                dve.scalar_tensor_tensor(out=tb[:, c, :], in0=K.u[:, cp, :], scalar=K.par[:, GAIN_RK, cp:cp + 1],
                                         in1=K.ksum[:, c, :], op0=ALU.mult, op1=ALU.mult).then_inc(S["bonus"], 1)
            dve.wait_ge(S["sqd"], 1)
            link(dve.tensor_reduce(rstd, sq, AX, ALU.add))
            dve.tensor_scalar(rstd, rstd, 1.0 / 64, LNX_EPS, ALU.mult, ALU.add).then_inc(S["vard"], 1)
            dve.wait_ge(S["rooted"], 1)
            link(dve.reciprocal(rstd, rstd))
            dve.tensor_tensor(Y, Y, rstd.unsqueeze(2).to_broadcast([P, NG, 64]), ALU.mult).then_inc(S["normed"], 1)
            for c in range(2):
                cp = 2 * hf + c
                dve.wait_ge(S["gate"], 2 * c + 2)
                bo = tb[:, c, :]
                link(dve.tensor_tensor(bo, K.u[:, 8 + cp, :], K.ps[2 + c][:, :], ALU.mult))
                dve.wait_ge(S["scaled"], c + 1)
                link(dve.tensor_tensor(z[:, c, :], z[:, c, :], bo, ALU.add))
                dve.tensor_tensor(K.u[:, cp, :], z[:, c, :], K.ps[4 + c][:, :], ALU.mult)

        @block.scalar
        def _(act):
            act.wait_ge(S["centred"], 1)
            nc.scalar.activation(sq, Y, ACT.Square).then_inc(S["sqd"], 1)
            act.wait_ge(S["vard"], 1)
            nc.scalar.activation(rstd, rstd, ACT.Sqrt).then_inc(S["rooted"], 1)
            for c in range(2):
                cp = 2 * hf + c
                act.wait_ge(S["turned"], c + 1)
                nc.scalar.activation(z[:, c, :], K.ps[c][:, :], ACT.Identity, scale=K.par[:, LN_W, cp:cp + 1],
                                     bias=K.par[:, LN_B, cp:cp + 1]).then_inc(S["scaled"], 1)

        @block.tensor
        def _(pe):
            for c in range(2):
                cp = 2 * hf + c
                pe.wait_ge(S["bonus"], c + 1)
                pe.matmul(K.ps[2 + c][:, :], K.heads1[:, :], tb[:, c, :], start=True, stop=True).then_inc(S["gate"], 1)
                pe.matmul(K.ps[4 + c][:, :], K.gup[:, cp * P:(cp + 1) * P], K.u[:, 12, :], start=True, stop=True).then_inc(S["gate"], 1)
            pe.wait_ge(S["normed"], 1)
            for c in range(2):
                for ch in range(NCH):
                    for b in (0, 64):
                        last = pe.matmul(K.ps[c][b:b + 64, ch * 64:ch * 64 + 64], K.Y[b:b + 64, ch, c, :],
                                         K.ident[b:b + 64, b:b + 64], start=True, stop=True)
                last.then_inc(S["turned"], 1)


def merge_branches(nc, K, tag, gates, proj, w_out, load_upto, x_src, whole_h=None, x_holds_y=False):
    with ExitStack() as ctx:
        names = "emm egate ehhigh ehpart eypart eprod emerged ehigh esum eadd el ex_in"
        S = sems(nc, ctx, names, tag)
        G, Gp = twins(nc, ctx, "G" + tag, [P, 2 * KD, T])
        tmp = ctx.enter_context(nc.sbuf_tensor("gt" + tag, [P, 2, T], F32))
        groups = [(b, ch) for b in range(2) for ch in range(KD)]
        starts = {}
        K.ring.used = {n: (S["emm"], 4 * i + 4) for i, n in enumerate(gates)}
        for b, (_, _, _, loads) in enumerate(proj):
            per = KD // len(loads)
            for i, n in enumerate(loads):
                starts[8 * b + per * i] = n
                K.ring.used[n] = (S["emm"], 16 + 8 * b + per * (i + 1))
        for i, n in enumerate(w_out):
            starts[16 + 4 * i] = n
            K.ring.used[n] = (S["emm"], 32 + 4 * i + 4)
        block = ctx.enter_context(nc.Block())

        @block.sync
        def _(sp):
            if x_holds_y:
                sp.wait_ge(S["eypart"], 1)
            for t in range(NT):
                sp.dma_start(K.x[:, t, :], x_src[t * P:(t + 1) * P, :]).then_inc(S["ex_in"], 16)
            K.ring.load(sp, load_upto)

        @block.tensor
        def _(pe):
            for c in range(16):
                n = gates[c // 4]
                if whole_h is not None and c == 0:
                    pe.wait_ge(S["ehpart"], KD // 2)
                K.ring.wait(pe, n, c % 4)
                if c >= 4:
                    pe.wait_ge(S["egate"], c - 3)
                mm_feature(pe, K.ps[c % 4][:, :], (K.ring, n), slice((c % 4) * P, (c % 4) * P + P), K.hp, KD).then_inc(S["emm"], 1)
            for i, (b, ch) in enumerate(groups):
                _, parts, nk, loads = proj[b]
                per = KD // len(loads)
                n, f = loads[ch // per], ch % per
                K.ring.wait(pe, n, f * 4 // per)
                if ch == 0:
                    pe.wait_ge(S["eypart"], b + 1)
                if i >= 4:
                    pe.wait_ge(S["eprod"], i - 3)
                mm_feature(pe, K.ps[4 + i % 4][:, :], (K.ring, n), slice(f * P, f * P + P), parts, nk).then_inc(S["emm"], 1)
            for half in range(2):
                for t in range(NT):
                    j = half * NT + t
                    if j >= 4:
                        pe.wait_ge(S["eadd"], j - 3)
                    mm_tokens(pe, K.ps[j % 4][:, :], (K.ring, w_out[half]), slice(0, 512), (Gp[:, KD:2 * KD, :], Gp[:, 0:KD, :]),
                              KD, t, S["esum"] if j == 0 else None).then_inc(S["emm"], 1)

        @block.scalar
        def _(act):
            if whole_h is not None:
                for k in range(0, KD, 2):
                    nc.scalar.activation(K.hp[0][:, k:k + 2, :], whole_h[:, k:k + 2, :], ACT.Copy).then_inc(S["ehhigh"], 1)
            for c in range(16):
                act.wait_ge(S["emm"], c + 1)
                nc.scalar.activation(G[:, c, :], K.ps[c % 4][:, :], ACT.Sigmoid).then_inc(S["egate"], 1)
            for ch in range(KD):
                act.wait_ge(S["emerged"], ch + 1)
                nc.scalar.activation(Gp[:, KD + ch, :], G[:, ch, :], ACT.Copy).then_inc(S["ehigh"], 1)

        @block.vector
        def _(dve):
            link = linker(dve, S["el"])
            if whole_h is not None:
                hi, lo = K.hp
                for k in range(0, KD, 2):
                    dve.wait_ge(S["ehhigh"], k // 2 + 1)
                    low(dve, lo[:, k:k + 2, :], whole_h[:, k:k + 2, :], hi[:, k:k + 2, :]).then_inc(S["ehpart"], 1)
            K.ring.split(dve, gates[0])
            K.ring.split(dve, gates[1])
            for yT, (hi, lo), _, _ in proj:
                link(high(dve, hi, yT))
                low(dve, lo, yT, hi).then_inc(S["eypart"], 1)
            for n in range(gates[2], gates[3] + 2):
                K.ring.split(dve, n)

            def part_sum(ch):
                dve.wait_ge(S["ehigh"], ch + 1)
                low(dve, Gp[:, ch, :], G[:, ch, :], Gp[:, KD + ch, :]).then_inc(S["esum"], 1)

            for i, (b, ch) in enumerate(groups):
                if i - 1 in starts and i < 8:
                    K.ring.split(dve, starts[i - 1] + 1)
                if i == 12:
                    K.ring.split(dve, w_out[0])
                dve.wait_ge(S["emm"], 16 + i + 1)
                dve.wait_ge(S["egate"], 16)
                ps = K.ps[4 + i % 4][:, :]
                if b == 0:
                    dve.tensor_tensor(G[:, ch, :], G[:, ch, :], ps, ALU.mult).then_inc(S["eprod"], 1)
                else:
                    if ch:
                        part_sum(ch - 1)
                    dve.tensor_tensor(tmp[:, ch % 2, :], G[:, KD + ch, :], ps, ALU.mult).then_inc(S["eprod"], 1)
                    dve.wait_ge(S["eprod"], i + 1)
                    dve.tensor_tensor(G[:, ch, :], G[:, ch, :], tmp[:, ch % 2, :], ALU.add).then_inc(S["emerged"], 1)
            part_sum(KD - 1)
            dve.wait_ge(S["ex_in"], 16 * NT)
            for half in range(2):
                for t in range(NT):
                    j = half * NT + t
                    if j == 1:
                        K.ring.split(dve, w_out[1])
                    dve.wait_ge(S["emm"], 32 + j + 1)
                    o = K.x[:, t, half * 512:(half + 1) * 512]
                    dve.tensor_tensor(o, o, K.ps[j % 4][:, :], ALU.add).then_inc(S["eadd"], 1)


def route(nc, K):
    I = K.I
    with ExitStack() as ctx:
        names = "win lmm neg ex rec aff_t aff topped bmm bcop rl"
        S = sems(nc, ctx, names, "r")
        sbt = lambda n, s, dt=F32: ctx.enter_context(nc.sbuf_tensor(n, s, dt))
        L, st = sbt("L", [P, NT, N_EXP]), sbt("rst", [P, 3, NT])
        aff, tv = sbt("aff", [N_EXP, T]), sbt("tv", [N_EXP, 4, CAP])
        ti = sbt("ti", [N_EXP, CAP], U32)
        sel = sbt("sel", [N_EXP, N_EXP, P])
        block = ctx.enter_context(nc.Block())

        @block.sync
        def _(sp):
            sp.dma_start(sel[:, :, :], I["c_sel"]).then_inc(S["win"], 16)

        @block.tensor
        def _(pe):
            for t in range(NT):
                for k in range(KD):
                    last = pe.matmul(K.ps[0][:, t * N_EXP:(t + 1) * N_EXP], K.hT[:, k, t * P:(t + 1) * P], K.w_router[:, k, :],
                                     start=(k == 0), stop=(k == KD - 1))
            last.then_inc(S["lmm"], 1)
            pe.wait_ge(S["aff_t"], 1)
            for t in range(NT):
                last = pe.transpose(K.ps[1][0:N_EXP, t * P:(t + 1) * P], L[:, t, :], K.ident[:, :])
            last.then_inc(S["aff"], 1)
            pe.wait_ge(S["topped"], 1)
            pe.wait_ge(S["win"], 16)
            for e in range(N_EXP):
                if e >= 2 * 4 and e % 2 == 0:
                    pe.wait_ge(S["bcop"], e // 2 - 3)
                last = pe.matmul(K.ps[2 + (e // 2) % 4][:, (e % 2) * 256:(e % 2) * 256 + 256], sel[:, e, :], tv[:, :, :],
                                 start=True, stop=True)
                if e % 2:
                    last.then_inc(S["bmm"], 1)

        @block.scalar
        def _(act):
            act.wait_ge(S["neg"], 1)
            for t in range(NT):
                last = nc.scalar.activation(L[:, t, :], K.ps[0][:, t * N_EXP:(t + 1) * N_EXP], ACT.Exp, bias=st[:, 0, t:t + 1],
                                            accum_out=st[:, 1, t:t + 1])
            last.then_inc(S["ex"], 1)
            for b in range(N_EXP // 2):
                act.wait_ge(S["bmm"], b + 1)
                nc.scalar.activation(K.IB[:, 2 * b:2 * b + 2, :], K.ps[2 + b % 4][:, :].rearrange("p (e c) -> p e c", e=2),
                                     ACT.Copy).then_inc(S["bcop"], 1)

        @block.vector
        def _(dve):
            link = linker(dve, S["rl"])
            dve.wait_ge(S["lmm"], 1)
            logits = K.ps[0][:, 0:NT * N_EXP].rearrange("p (t e) -> p t e", t=NT)
            dve.tensor_reduce(st[:, 0, :], logits, AX, ALU.max, negate=True).then_inc(S["neg"], 1)
            dve.wait_ge(S["ex"], 1)
            link(dve.reciprocal(st[:, 2, :], st[:, 1, :]))
            dve.tensor_tensor(L[:, :, :], L[:, :, :], st[:, 2, :].unsqueeze(2).to_broadcast([P, NT, N_EXP]), ALU.mult).then_inc(S["aff_t"], 1)
            dve.wait_ge(S["aff"], 1)
            link(dve.tensor_copy(aff[:, :], K.ps[1][0:N_EXP, :]))
            for r in range(CAP // 8):
                best = tv[:, 2, 8 * r:8 * r + 8]
                link(dve.max(best, aff[:, :]))
                link(dve.max_index(ti[:, 8 * r:8 * r + 8], best, aff[:, :]))
                if r + 1 < CAP // 8:
                    link(dve.match_replace(aff[:, :], best, aff[:, :], -1.0))
            dve.tensor_copy(tv[:, 3, :], tv[:, 2, :])
            dve.tensor_copy(tv[:, 0, :], ti[:, :])
            dve.tensor_copy(tv[:, 1, :], ti[:, :]).then_inc(S["topped"], 1)


def experts(nc, K, n0, load_upto):
    I = K.I
    H = 512
    names = ("w_used oh_ready gathered xs_copied xs_turned xsT_ready gate_sig gated hid_ready hid_turned hidT_ready "
             "ys_ready oht_turned oht_ready combined x_added")
    with ExitStack() as ctx:
        S = sems(nc, ctx, names, "m")
        sbt = lambda n, s: ctx.enter_context(nc.sbuf_tensor(n, s, F32))
        OH, OHV = sbt("OH", [P, NT, CAP]), sbt("OHV", [P, NT, P])
        XS = sbt("XS", [P, H])
        xsT = sbt("xsT", [P, 2, 4, 2, CAP])
        HS, hidT, ys = sbt("HS", [P, H]), sbt("hidT", [P, 4, 2, CAP]), sbt("ys", [P, H])
        OHT = sbt("OHT", [P, 2, NT, P])
        psO, psX, psT, psG, psU, psD = K.ps[0:6]
        psC = K.ps[6:8]
        srcs = (I["exp_w_gate"], I["exp_w_up"], I["exp_w_down"])
        slot = lambda j: K.ring.buf[:, j % RING, :].rearrange("p (k w) -> p k w", k=4)
        block = ctx.enter_context(nc.Block())
        LOOPS = N_EXP // 2 - 1

        def wait(eng, sem, value):
            if not isinstance(value, int) or value > 0:
                eng.wait_ge(sem, value)

        def load(sp, e, part, j):
            src = srcs[part // 2][0, bass.ds(e, 1), (part % 2) * H:(part % 2) * H + H, :]
            sp.dma_start(slot(j), src.rearrange("e (k p) w -> p (e k) w", p=P)).then_inc(K.ring.full[j % RING], 16)

        @block.sync
        def _(sp):
            if K.ring.issued < n0 + 4:
                for j in range(K.ring.issued - n0, 4):
                    load(sp, 0, j, j)
            with sp.Fori(0, LOOPS) as i:
                for j in range(12):
                    m = 4 + j
                    sp.wait_ge(S["w_used"], i * 12 + (j + 1))
                    load(sp, i * 2 + m // 6, m % 6, m)
            for j in range(12 * LOOPS + 4, 96):
                sp.wait_ge(S["w_used"], j - 3)
                load(sp, j // 6, j % 6, j)
            K.ring.issued = n0 + 96
            K.ring.used = {n0 + j: (S["w_used"], j + 1) for j in range(92, 96)}
            K.ring.load(sp, load_upto)

        def each(eng, steps):
            steps(0, 0, False)
            steps(1, 1, False)
            with eng.Fori(1, LOOPS) as i:
                for u in range(2):
                    steps(i * 2 + u, u, False)
            steps(N_EXP - 2, 0, False)
            steps(N_EXP - 1, 1, True)

        @block.tensor
        def _(pe):
            def gather(e):
                pe.wait_ge(S["oh_ready"], e + 1)
                wait(pe, S["xs_copied"], e)
                for t in range(NT):
                    for half in range(2):
                        last = pe.matmul(psX[64 * half:64 * half + 64, :], OH[:, t, :], K.xn[:, t, half * H:(half + 1) * H],
                                         start=(t == 0), stop=(t == NT - 1))
                last.then_inc(S["gathered"], 1)

            def turn_xs(e):
                pe.wait_ge(S["xs_copied"], e + 1)
                wait(pe, S["hidT_ready"], e)
                for c in range(4):
                    last = pe.transpose(psT[:, c * P:(c + 1) * P], XS[:, c * P:(c + 1) * P], K.ident[:, :])
                last.then_inc(S["xs_turned"], 1)

            def turn_oh(e):
                pe.wait_ge(S["oh_ready"], e + 1)
                wait(pe, S["oht_ready"], e)
                for t in range(NT):
                    last = pe.transpose(psO[:, t * P:(t + 1) * P], OHV[:, t, :], K.ident[:, :])
                last.then_inc(S["oht_turned"], 1)

            def halves(e, u, out, lhs, part):
                for ld in range(2):
                    j = 6 * u + 2 * part + ld
                    pe.wait_ge(K.ring.full[j % RING], (e - u) * 24 + 16 * (j // RING) + K.ring.landed[n0 + j % RING])
                    for kk in range(4):
                        k = 4 * ld + kk
                        for half in range(2):
                            last = pe.matmul(out[64 * half:64 * half + 64, :], lhs[:, k % 4, k // 4, :],
                                             slot(j)[:, kk, half * H:(half + 1) * H], start=(k == 0), stop=(k == KD - 1))
                    last.then_inc(S["w_used"], 1)

            def steps(e, u, final):
                pe.wait_ge(S["xsT_ready"], e + 1)
                wait(pe, S["hid_ready"], e)
                halves(e, u, psG, xsT[:, u], 0)
                halves(e, u, psU, xsT[:, u], 1)
                if not final:
                    gather(e + 1)
                pe.wait_ge(S["hid_ready"], e + 1)
                for c in range(4):
                    last = pe.transpose(psT[:, c * P:(c + 1) * P], HS[:, c * P:(c + 1) * P], K.ident[:, :])
                last.then_inc(S["hid_turned"], 1)
                pe.wait_ge(S["hidT_ready"], e + 1)
                wait(pe, S["ys_ready"], e)
                halves(e, u, psD, hidT, 2)
                if not final:
                    turn_xs(e + 1)
                    turn_oh(e + 1)
                pe.wait_ge(S["ys_ready"], e + 1)
                pe.wait_ge(S["oht_ready"], e + 1)
                for j in range(8):
                    t, half = j // 2, j % 2
                    if j >= 2:
                        wait(pe, S["x_added"], e * 8 + (j - 1))
                    else:
                        wait(pe, S["x_added"], e * 8)
                    rows = slice(64 * half, 64 * half + 64)
                    pe.matmul(psC[half][:, :], OHT[rows, u, t, :], ys[rows, :], start=True, stop=True).then_inc(S["combined"], 1)

            gather(0)
            turn_xs(0)
            turn_oh(0)
            each(pe, steps)

        @block.scalar
        def _(act):
            def copy_xs(e):
                act.wait_ge(S["gathered"], e + 1)
                wait(act, S["xs_turned"], e)
                nc.scalar.activation(XS[:, :], psX[:, :], ACT.Copy).then_inc(S["xs_copied"], 1)

            def copy_oh(e, u):
                act.wait_ge(S["oht_turned"], e + 1)
                nc.scalar.activation(OHT[:, u, :, :], psO[:, :].rearrange("p (t c) -> p t c", t=NT), ACT.Copy).then_inc(S["oht_ready"], 1)

            def steps(e, u, final):
                act.wait_ge(S["w_used"], e * 6 + 2)
                wait(act, S["hid_turned"], e)
                nc.scalar.activation(HS[:, :], psG[:, :], ACT.Sigmoid).then_inc(S["gate_sig"], 1)
                if not final:
                    copy_xs(e + 1)
                act.wait_ge(S["hid_turned"], e + 1)
                nc.scalar.activation(hidT[:, :, :, :], psT[:, :].rearrange("p (c h s) -> p c h s", c=4, h=2), ACT.Copy).then_inc(S["hidT_ready"], 1)
                act.wait_ge(S["w_used"], e * 6 + 6)
                wait(act, S["combined"], e * 8)
                nc.scalar.activation(ys[:, :], psD[:, :], ACT.Copy).then_inc(S["ys_ready"], 1)
                if not final:
                    copy_oh(e + 1, 1 - u)

            copy_xs(0)
            copy_oh(0, 0)
            each(act, steps)

        @block.vector
        def _(dve):
            def one_hots(e):
                wait(dve, S["gathered"], e)
                wait(dve, S["oht_turned"], e)
                for t in range(NT):
                    dve.tensor_scalar(OH[:, t, :], K.IB[:, bass.ds(e, 1), 0:CAP].rearrange("p a c -> p (a c)"),
                                      K.tok[:, t:t + 1], None, ALU.is_equal)
                    last = dve.scalar_tensor_tensor(
                        out=OHV[:, t, :], in0=K.IB[:, bass.ds(e, 1), 0:P].rearrange("p a c -> p (a c)"), scalar=K.tok[:, t:t + 1],
                        in1=K.IB[:, bass.ds(e, 1), P:2 * P].rearrange("p a c -> p (a c)"), op0=ALU.is_equal, op1=ALU.mult)
                last.then_inc(S["oh_ready"], 1)

            def scale_xs(e, u):
                dve.wait_ge(S["xs_turned"], e + 1)
                dve.tensor_tensor(xsT[:, u, :, :, :], psT[:, :].rearrange("p (c h s) -> p c h s", c=4, h=2),
                                  K.gf[:, :].rearrange("p (h c) -> p c h", h=2).unsqueeze(3).to_broadcast([P, 4, 2, CAP]), ALU.mult).then_inc(S["xsT_ready"], 1)

            def steps(e, u, final):
                if not final:
                    one_hots(e + 1)
                dve.wait_ge(S["gate_sig"], e + 1)
                dve.tensor_tensor(HS[:, :], HS[:, :], psG[:, :], ALU.mult).then_inc(S["gated"], 1)
                dve.wait_ge(S["gated"], e + 1)
                dve.wait_ge(S["w_used"], e * 6 + 4)
                dve.tensor_tensor(HS[:, :], HS[:, :], psU[:, :], ALU.mult).then_inc(S["hid_ready"], 1)
                if not final:
                    scale_xs(e + 1, 1 - u)
                for j in range(8):
                    t, half = j // 2, j % 2
                    dve.wait_ge(S["combined"], e * 8 + (j + 1))
                    o = K.x[:, t, half * H:(half + 1) * H]
                    dve.tensor_tensor(o, o, psC[half][:, :], ALU.add).then_inc(S["x_added"], 1)

            one_hots(0)
            scale_xs(0, 0)
            each(dve, steps)


def gain_norm(nc, K, tag, g, out_dram=None, keep_dram=None):
    dst = out_dram if out_dram is not None else keep_dram
    with ExitStack() as ctx:
        S = sems(nc, ctx, "g_in squared var_ok root_ok rec_ok scaled gained stored", tag)
        gb = ctx.enter_context(nc.sbuf_tensor("gb" + tag, [P, D], F32))
        sq = ctx.enter_context(nc.sbuf_tensor("sqg" + tag, [P, 2, D], F32))
        ss = ctx.enter_context(nc.sbuf_tensor("ssg" + tag, [P, 4, NT], F32))
        block = ctx.enter_context(nc.Block())

        @block.sync
        def _(sp):
            sp.dma_start(gb[:, :], g.rearrange("(a d) -> a d", a=1).to_broadcast([P, D])).then_inc(S["g_in"], 16)
            for t in range(NT):
                sp.wait_ge(S["gained"], t + 1)
                sp.dma_start(dst[t * P:(t + 1) * P, :], K.x[:, t, :]).then_inc(S["stored"], 16)
            sp.wait_ge(S["stored"], 16 * NT)

        @block.scalar
        def _(act):
            def root(t):
                act.wait_ge(S["var_ok"], t + 1)
                nc.scalar.activation(ss[:, 2, t:t + 1], ss[:, 1, t:t + 1], ACT.Sqrt).then_inc(S["root_ok"], 1)

            for t in range(NT):
                if t >= 2:
                    act.wait_ge(S["squared"], t - 1)
                nc.scalar.activation(sq[:, t % 2, :], K.x[:, t, :], ACT.Square, accum_out=ss[:, 0, t:t + 1]).then_inc(S["squared"], 1)
                if t:
                    root(t - 1)
            root(NT - 1)

        @block.vector
        def _(dve):
            for t in range(NT):
                col = lambda i: ss[:, i, t:t + 1]
                dve.wait_ge(S["squared"], t + 1)
                dve.tensor_scalar(col(1), col(0), 1.0 / D, EPS, ALU.mult, ALU.add).then_inc(S["var_ok"], 1)
                dve.wait_ge(S["root_ok"], t + 1)
                dve.reciprocal(col(3), col(2)).then_inc(S["rec_ok"], 1)
                dve.wait_ge(S["rec_ok"], t + 1)
                if t == 0:
                    dve.wait_ge(S["g_in"], 16)
                dve.scalar_tensor_tensor(out=K.x[:, t, :], in0=K.x[:, t, :], scalar=col(3), in1=gb[:, :],
                                         op0=ALU.mult, op1=ALU.mult).then_inc(S["gained"], 1)


def mlstm_inputs(nc, K, n0, load_upto):
    I = K.I
    NC2 = 2 * D // P
    with ExitStack() as ctx:
        S = sems(nc, ctx, "mm par wif_in first tap sig act vcop wif gmm gcop rows e1 e2 bmm bcop cmm xl al", "I")
        sbt = lambda n, s: ctx.enter_context(nc.sbuf_tensor(n, s, F32))
        cw, cb = sbt("cw", [P, 5, NC2]), None
        acc = sbt("acc", [P, 2, T])
        sgb = sbt("sgb", [P, 2, T])
        wif = sbt("wif", [P, KD, 8])
        wif_high, wif_low = (ctx.enter_context(nc.sbuf_tensor(n, [P, KD, 8], F32R)) for n in ("wif_high", "wif_low"))
        bif = sbt("bif", [M_HEADS, 2])
        rows = sbt("rows", [M_HEADS, 6, T])
        mrow = sbt("mrow", [M_HEADS, 4, NT + 1])
        reset = sbt("reset", [M_HEADS, 2, T])
        K.ring.used = {n0 + i: (S["mm"], 4 * i + 4) for i in range(6)}
        block = ctx.enter_context(nc.Block())
        ig, lf, b, M, ex, wk = (rows[:, j, :] for j in range(6))

        @block.sync
        def _(sp):
            with nc.allow_non_contiguous_dma(reason="one tap per partition"):
                sp.dma_start(wif[:, :, :], I["w_in_2"][0][:, IF_M:IF_M + 8].rearrange("(k p) w -> p k w", p=P)).then_inc(S["wif_in"], 16)
                for j in range(4):
                    sp.dma_start(cw[:, j, :], I["conv_w_2"][0][j].rearrange("(c p) -> p c", p=P)).then_inc(S["par"], 16)
                sp.dma_start(cw[:, 4, :], I["conv_b_2"][0].rearrange("(c p) -> p c", p=P)).then_inc(S["par"], 16)
                sp.dma_start(bif[:, :], I["b_gate_if_2"][0].rearrange("(j h) -> h j", j=2)).then_inc(S["par"], 16)
            sp.dma_start(reset[:, :, :], I["c_reset"]).then_inc(S["par"], 16)
            sp.dma_start(K.sel4[:, :, :], I["c_sel4"]).then_inc(S["par"], 16)
            sp.dma_start(K.causal[:, :], I["c_causal"]).then_inc(S["par"], 16)
            K.ring.load(sp, load_upto)
            sp.wait_ge(S["par"], 144)

        @block.tensor
        def _(pe):
            for c in range(NC2):
                K.ring.wait(pe, n0 + c // 4, c % 4)
                if c >= 4:
                    pe.wait_ge(S["tap"], c - 3)
                mm_feature(pe, K.ps[c % 4][:, :], (K.ring, n0 + c // 4), slice((c % 4) * P, (c % 4) * P + P), K.hp, KD).then_inc(S["mm"], 1)
            pe.wait_ge(S["wif"], 2)
            for j in range(2):
                for k in range(KD):
                    f = slice(4 * j, 4 * j + 4)
                    last = product(pe, K.ps[4 + j][0:M_HEADS, :], (wif_high[:, k, f], wif_low[:, k, f]), [t[:, k, :] for t in K.hp], k == 0, k == KD - 1)
            last.then_inc(S["gmm"], 1)
            for half in range(2):
                n = n0 + 4 + half
                for t in range(NT):
                    j = half * NT + t
                    if j < 4:
                        pe.wait_ge(S["tap"], 13 + j)
                    else:
                        pe.wait_ge(S["vcop"], j - 3)
                    mm_tokens(pe, K.ps[j % 4][:, :], (K.ring, n), slice(0, 512), K.hp, KD, t).then_inc(S["mm"], 1)
            pe.wait_ge(S["e2"], 1)
            for j, row in enumerate((M, ex)):
                for h in range(M_HEADS):
                    i = j * 4 + h
                    if i >= 2:
                        pe.wait_ge(S["bcop"], i - 1)
                    pe.matmul(K.ps[4 + i % 2][:, :], K.sel4[:, h, :], row, start=True, stop=True).then_inc(S["bmm"], 1)
            for q, row in enumerate((b, ig, wk)):
                for c in range(NT):
                    pe.transpose(K.ps[6][:, (q * NT + c) * 4:(q * NT + c) * 4 + 4], row[:, c * P:(c + 1) * P], K.ident[0:4, 0:4])
            for h in range(M_HEADS):
                last = pe.matmul(K.ps[6][:, 64 + 4 * h:68 + 4 * h], K.sel4[:, h, :], mrow[:, 2, 0:NT], start=True, stop=True)
            last.then_inc(S["cmm"], 1)

        @block.scalar
        def _(act):
            act.wait_ge(S["par"], 144)
            link = linker(act, S["al"])
            for c in range(NC2):
                dst = K.qmT[:, c, :] if c < 8 else K.kmT[:, c - 8, :]
                act.wait_ge(S["mm"], c + 1)
                if c >= 2:
                    act.wait_ge(S["act"], c - 1)
                nc.scalar.activation(acc[:, c % 2, :], K.ps[c % 4][:, :], ACT.Identity, scale=cw[:, 3, c:c + 1],
                                     bias=cw[:, 4, c:c + 1]).then_inc(S["first"], 1)
                act.wait_ge(S["tap"], c + 1)
                nc.scalar.activation(sgb[:, c % 2, :], acc[:, c % 2, :], ACT.Sigmoid).then_inc(S["sig"], 1)
            act.wait_ge(S["gcop"], 2)
            link(nc.scalar.activation(M, lf, ACT.Abs))
            link(nc.scalar.activation(M, M, ACT.Exp, scale=-1.0))
            nc.scalar.activation(M, M, ACT.Ln, bias=1.0).then_inc(S["e1"], 1)
            for j in range(8):
                if j == 7:
                    act.wait_ge(S["rows"], 1)
                    nc.scalar.activation(ex, ex, ACT.Exp)
                    nc.scalar.activation(mrow[:, 2, 0:NT], mrow[:, 2, 0:NT], ACT.Exp)
                    nc.scalar.activation(wk, wk, ACT.Exp)
                    nc.scalar.activation(b, b, ACT.Exp).then_inc(S["e2"], 1)
                t, half = j % 4, j // 4
                act.wait_ge(S["mm"], NC2 + j + 1)
                nc.scalar.activation(K.vm[:, t, 2 * half:2 * half + 2, 0:M_DH], K.ps[j % 4][:, :].rearrange("p (h d) -> p h d", h=2),
                                     ACT.Copy).then_inc(S["vcop"], 1)
            for i in range(8):
                act.wait_ge(S["bmm"], i + 1)
                dst = K.MB if i < 4 else K.WI
                nc.scalar.activation(dst[:, i % 4, :], K.ps[4 + i % 2][:, :], ACT.Copy).then_inc(S["bcop"], 1)
            act.wait_ge(S["cmm"], 1)
            nc.scalar.activation(K.cols[:, :, :], K.ps[6][:, 0:48].rearrange("p (q c h) -> p q (c h)", q=3, c=NT), ACT.Copy)
            nc.scalar.activation(K.dec[:, :], K.ps[6][:, 64:80], ACT.Copy)

        @block.vector
        def _(dve):
            dve.wait_ge(S["wif_in"], 16)
            high(dve, wif_high[:, :, :], wif[:, :, :]).then_inc(S["wif"], 1)
            dve.wait_ge(S["wif"], 1)
            low(dve, wif_low[:, :, :], wif[:, :, :], wif_high[:, :, :]).then_inc(S["wif"], 1)
            K.ring.split(dve, n0)
            K.ring.split(dve, n0 + 1)
            dve.wait_ge(S["par"], 144)

            def log_gates():
                dve.wait_ge(S["gmm"], 1)
                dve.tensor_scalar(ig, K.ps[4][0:M_HEADS, :], bif[:, 0:1], None, ALU.add).then_inc(S["gcop"], 1)
                dve.tensor_scalar(lf, K.ps[5][0:M_HEADS, :], bif[:, 1:2], None, ALU.add).then_inc(S["gcop"], 1)
                dve.wait_ge(S["e1"], 1)
                link(dve.tensor_scalar(lf, lf, 0.0, None, ALU.min))
                link(dve.tensor_tensor(lf, lf, M, ALU.subtract))
                link(dve.tensor_tensor_scan(b, reset[:, 0, :], lf, 0.0, ALU.mult, ALU.add))
                link(dve.tensor_tensor(ig, ig, b, ALU.subtract))
                link(dve.memset(mrow[:, :, :], 0.0))
                for c in range(NT):
                    cc = slice(c * P, (c + 1) * P)
                    last = (c + 1) * P - 1
                    link(dve.tensor_tensor_scan(M[:, cc], reset[:, 1, cc], ig[:, cc], mrow[:, 0, c:c + 1], ALU.add, ALU.max))
                    link(dve.tensor_tensor(mrow[:, 0, c + 1:c + 2], M[:, last:last + 1], b[:, last:last + 1], ALU.add))
                    dve.tensor_scalar(ex[:, cc], M[:, cc], -1.0, mrow[:, 0, c:c + 1], ALU.mult, ALU.add)
                    dve.tensor_tensor(mrow[:, 2, c:c + 1], mrow[:, 0, c:c + 1], M[:, last:last + 1], ALU.subtract)
                    link(dve.tensor_scalar(wk[:, cc], ig[:, cc], M[:, last:last + 1], None, ALU.subtract))
                dve.scalar_tensor_tensor(out=b, in0=b, scalar=-1.0, in1=M, op0=ALU.mult, op1=ALU.subtract).then_inc(S["rows"], 1)

            link = linker(dve, S["xl"])
            dve.memset(K.vm[:, :, :, M_DH:M_DH + 1], 1.0)
            for c in range(NC2):
                if c % 4 == 1 and c > 4:
                    K.ring.split(dve, n0 + c // 4 + 1)
                dst = K.qmT[:, c, :] if c < 8 else K.kmT[:, c - 8, :]
                a, ps = acc[:, c % 2, :], K.ps[c % 4]
                dve.wait_ge(S["first"], c + 1)
                for j in (2, 1, 0):
                    d = 3 - j
                    ins = dve.scalar_tensor_tensor(out=a[:, d:T], in0=ps[:, 0:T - d], scalar=cw[:, j, c:c + 1], in1=a[:, d:T],
                                                   op0=ALU.mult, op1=ALU.add)
                    if j:
                        link(ins)
                    else:
                        ins.then_inc(S["tap"], 1)
                dve.wait_ge(S["sig"], c + 1)
                dve.scalar_tensor_tensor(out=dst, in0=a, scalar=M_DH ** -0.5 if c < 8 else 1.0, in1=sgb[:, c % 2, :],
                                         op0=ALU.mult, op1=ALU.mult).then_inc(S["act"], 1)
            K.ring.split(dve, n0 + 5)
            log_gates()
            for n in (n0 + 6, n0 + 7):
                K.ring.split(dve, n)


def mlstm_cell(nc, K):
    W1 = M_DH + 1
    N = NT * M_HEADS
    with ExitStack() as ctx:
        S = sems(nc, ctx, "sc kt num cup d1 w0 w wq kw den h c stat var root l", "L")
        sbt = lambda n, s: ctx.enter_context(nc.sbuf_tensor(n, s, F32))
        W, D1 = sbt("W", [P, 2, P]), sbt("D1", [P, 2, P])
        qI, kw = sbt("qI", [P, 2, 2, P]), sbt("kw", [P, 2, M_DH])
        C = sbt("C", [P, M_HEADS, 2, W1])
        den = sbt("den", [P, 2, N])
        bs, ba = sbt("bs", [P, N, 6]), sbt("ba", [P, N, 2])
        rs = sbt("rs", [P, N])
        block = ctx.enter_context(nc.Block())
        units = [(c, h) for c in range(NT) for h in range(M_HEADS)]
        psS, psK, psN, psC = K.ps[0:2], K.ps[2:4], K.ps[4:6], K.ps[6:8]
        G_, E_, K_ = 1, 0, 2

        @block.tensor
        def _(pe):
            def scores(i):
                c, h = units[i]
                cc = slice(c * P, (c + 1) * P)
                if i >= 2:
                    pe.wait_ge(S["w"], i - 1)
                    pe.wait_ge(S["kw"], i - 1)
                for j in range(2):
                    last = pe.matmul(psS[i % 2][:, 0:P], K.kmT[:, 2 * h + j, cc], K.qmT[:, 2 * h + j, cc], start=(j == 0), stop=(j == 1))
                last.then_inc(S["sc"], 1)
                for j in range(2):
                    last = pe.transpose(psK[i % 2][:, j * P:(j + 1) * P], K.kmT[:, 2 * h + j, cc], K.ident[:, :])
                last.then_inc(S["kt"], 1)

            scores(0)
            for i, (c, h) in enumerate(units):
                if i + 1 < N:
                    scores(i + 1)
                pe.wait_ge(S["w"], i + 1)
                if c:
                    pe.wait_ge(S["wq"], i - 3)
                    pe.wait_ge(S["c"], i - 3)
                if i >= 2:
                    pe.wait_ge(S["h"], i - 1)
                v = K.vm[:, c, h, :]
                last = pe.matmul(psN[i % 2][:, 0:W1], W[:, i % 2, :], v, start=True, stop=(c == 0))
                if c:
                    for j in range(2):
                        last = pe.matmul(psN[i % 2][:, 0:W1], qI[:, i % 2, j, :], C[:, h, j, :], start=False, stop=(j == 1))
                last.then_inc(S["num"], 1)
                if c < NT - 1:
                    pe.wait_ge(S["kw"], i + 1)
                    if i:
                        pe.wait_ge(S["c"], i)
                    for j in range(2):
                        last = pe.matmul(psC[j][:, 0:W1], kw[:, i % 2, j * P:(j + 1) * P], v, start=True, stop=True)
                    last.then_inc(S["cup"], 1)

        @block.scalar
        def _(act):
            for i, (c, h) in enumerate(units):
                act.wait_ge(S["d1"], i + 1)
                nc.scalar.activation(D1[:, i % 2, :], D1[:, i % 2, :], ACT.Exp, scale=-1.0).then_inc(S["w0"], 1)
                act.wait_ge(S["kt"], i + 1)
                if i >= 2:
                    act.wait_ge(S["cup"], min(i - 1, 12))
                nc.scalar.activation(kw[:, i % 2, :], psK[i % 2][:, 0:2 * P], ACT.Copy, scale=K.cols[:, K_, i:i + 1]).then_inc(S["kw"], 1)
            act.wait_ge(S["var"], 1)
            nc.scalar.activation(rs[:, :], rs[:, :], ACT.Sqrt).then_inc(S["root"], 1)

        @block.vector
        def _(dve):
            link = linker(dve, S["l"])

            def weights(i):
                c, h = units[i]
                cc = slice(c * P, (c + 1) * P)
                if i >= 2:
                    dve.wait_ge(S["num"], i - 1)
                    dve.wait_ge(S["w"], i - 1)
                dve.tensor_scalar(D1[:, i % 2, :], K.MB[:, h, cc], K.cols[:, G_, i:i + 1], 0.0, ALU.subtract, ALU.max).then_inc(S["d1"], 1)
                if c:
                    dve.tensor_tensor(qI[:, i % 2, :, :], K.qmT[:, 2 * h:2 * h + 2, cc],
                                      K.WI[:, h, cc].unsqueeze(1).to_broadcast([P, 2, P]), ALU.mult).then_inc(S["wq"], 1)
                dve.wait_ge(S["w0"], i + 1)
                link(dve.tensor_tensor(D1[:, i % 2, :], D1[:, i % 2, :], K.causal[:, :], ALU.mult))
                dve.wait_ge(S["sc"], i + 1)
                dve.tensor_tensor(W[:, i % 2, :], D1[:, i % 2, :], psS[i % 2][:, 0:P], ALU.mult).then_inc(S["w"], 1)

            weights(0)
            for i, (c, h) in enumerate(units):
                if i + 1 < N:
                    weights(i + 1)
                dve.wait_ge(S["num"], i + 1)
                a, r = den[:, 0, i:i + 1], den[:, 1, i:i + 1]
                dot = psN[i % 2][:, M_DH:W1]
                link(dve.tensor_scalar(a, dot, -1.0, K.cols[:, E_, i:i + 1], ALU.mult, ALU.max))
                link(dve.tensor_tensor(a, a, dot, ALU.max))
                link(dve.reciprocal(r, a))
                hm = K.hm[:, c, h, :]
                dve.tensor_scalar(hm, psN[i % 2][:, 0:M_DH], r, None, ALU.mult).then_inc(S["h"], 1)
                if c < NT - 1:
                    dve.wait_ge(S["cup"], i + 1)
                    for j in range(2):
                        if c == 0:
                            last = dve.tensor_copy(C[:, h, j, :], psC[j][:, 0:W1])
                        else:
                            last = dve.scalar_tensor_tensor(out=C[:, h, j, :], in0=C[:, h, j, :], scalar=K.dec[:, 4 * h + c:4 * h + c + 1],
                                                            in1=psC[j][:, 0:W1], op0=ALU.mult, op1=ALU.add)
                    last.then_inc(S["c"], 1)
                dve.wait_ge(S["h"], i + 1)
                link(dve.bn_stats(bs[:, i, :], hm))
                link(dve.bn_aggr(ba[:, i, :], bs[:, i, :]))
            dve.tensor_scalar(rs[:, :], ba[:, :, 1], EPS, None, ALU.add).then_inc(S["var"], 1)
            dve.wait_ge(S["root"], 1)
            link(dve.reciprocal(rs[:, :], rs[:, :]))
            for i, (c, h) in enumerate(units):
                hm = K.hm[:, c, h, :]
                dve.tensor_scalar(hm, hm, ba[:, i, 0:1], rs[:, i:i + 1], ALU.subtract, ALU.mult)


def mlstm_output(nc, K, n0, load_upto):
    I = K.I
    with ExitStack() as ctx:
        S = sems(nc, ctx, "mm sig tr out par", "O")
        so = ctx.enter_context(nc.sbuf_tensor("so", [P, 2, T], F32))
        gm = ctx.enter_context(nc.sbuf_tensor("gm", [P, KD], F32))
        K.ring.used = {n0 + i: (S["mm"], 4 * i + 4) for i in range(2)}
        block = ctx.enter_context(nc.Block())

        @block.sync
        def _(sp):
            with nc.allow_non_contiguous_dma(reason="one gain per partition"):
                sp.dma_start(gm[:, :], I["mlstm_norm_g_2"][0].rearrange("(c p) -> p c", p=P)).then_inc(S["par"], 16)
            K.ring.load(sp, load_upto)
            sp.wait_ge(S["par"], 16)

        @block.tensor
        def _(pe):
            for c in range(KD):
                K.ring.wait(pe, n0 + c // 4, c % 4)
                if c >= 2:
                    pe.wait_ge(S["sig"], c - 1)
                mm_feature(pe, K.ps[c % 2][:, :], (K.ring, n0 + c // 4), slice((c % 4) * P, (c % 4) * P + P), K.hp, KD).then_inc(S["mm"], 1)
                if c >= 2:
                    pe.wait_ge(S["out"], c - 1)
                for t in range(NT):
                    last = pe.transpose(K.ps[2 + c % 2][:, t * P:(t + 1) * P], K.hm[:, t, c // 2, (c % 2) * P:(c % 2) * P + P], K.ident[:, :])
                last.then_inc(S["tr"], 1)

        @block.scalar
        def _(act):
            for c in range(KD):
                act.wait_ge(S["mm"], c + 1)
                if c >= 2:
                    act.wait_ge(S["out"], c - 1)
                nc.scalar.activation(so[:, c % 2, :], K.ps[c % 2][:, :], ACT.Sigmoid).then_inc(S["sig"], 1)

        @block.vector
        def _(dve):
            K.ring.split(dve, n0)
            K.ring.split(dve, n0 + 1)
            dve.wait_ge(S["par"], 16)
            for c in range(KD):
                if c == 7:
                    K.ring.split(dve, n0 + 2)
                dve.wait_ge(S["tr"], c + 1)
                dve.wait_ge(S["sig"], c + 1)
                dve.scalar_tensor_tensor(out=K.ymT[:, c, :], in0=K.ps[2 + c % 2][:, :], scalar=gm[:, c:c + 1], in1=so[:, c % 2, :],
                                         op0=ALU.mult, op1=ALU.mult).then_inc(S["out"], 1)


def second_attention_inputs(nc, K, n0, load_upto, flips):
    I = K.I
    with ExitStack() as ctx:
        S = sems(nc, ctx, "mm cop par one bmm bcop st", "Q")
        rb = ctx.enter_context(nc.sbuf_tensor("rb", [33, 24], F32))
        dist = ctx.enter_context(nc.sbuf_tensor("dist", [33, 640], F32))
        R = ctx.enter_context(nc.sbuf_tensor("R", [8, 640], F32))
        K.ring.used = {n0 + i: (S["mm"], 4 * i + 4) for i in range(9)}
        block = ctx.enter_context(nc.Block())

        @block.sync
        def _(sp):
            sp.wait_ge(S["one"], 1)
            sp.dma_start(rb[0:32, :], I["rel_bias_2"]).then_inc(S["par"], 16)
            sp.dma_start(K.flip[:, :], I["c_flip"]).then_inc(S["par"], 16)
            sp.dma_start(dist[:, :], I["c_dist"][:, 0, :]).then_inc(S["par"], 16)
            for g in range(3):
                if g:
                    sp.wait_ge(S["bmm"], g)
                    sp.dma_start(dist[:, :], I["c_dist"][:, g, :]).then_inc(S["par"], 16)
                K.ring.load(sp, n0 + 3 + g)
                sp.wait_ge(S["bcop"], g + 1)
                sp.dma_start(K.R_dram[g, :, :], R[:, :]).then_inc(S["st"], 16)
            sp.wait_ge(S["st"], 48)
            for h in range(2):
                load_biases(sp, K, flips, h)
            K.ring.load(sp, load_upto)

        @block.tensor
        def _(pe):
            for c in range(24):
                n = n0 + c // 4
                K.ring.wait(pe, n, c % 4)
                if c >= 4:
                    pe.wait_ge(S["cop"], c - 3)
                mm_feature(pe, K.ps[c % 4][:, :], (K.ring, n), slice((c % 4) * P, (c % 4) * P + P), K.hp, KD).then_inc(S["mm"], 1)
                if c in (4, 8, 12):
                    g = c // 4 - 1
                    pe.wait_ge(S["par"], 48 + 16 * g)
                    if g:
                        pe.wait_ge(S["bcop"], g)
                    pe.matmul(K.ps[4][0:8, :], rb[:, 8 * g:8 * g + 8], dist[:, 0:512], start=True, stop=True)
                    pe.matmul(K.ps[5][0:8, 0:128], rb[:, 8 * g:8 * g + 8], dist[:, 512:640], start=True, stop=True).then_inc(S["bmm"], 1)
            for j in range(12):
                s, t = j // NT, j % NT
                pe.wait_ge(S["cop"], 24 + j - 3)
                mm_tokens(pe, K.ps[j % 4][:, :], (K.ring, n0 + 6 + s), slice(0, 512), K.hp, KD, t).then_inc(S["mm"], 1)

        @block.scalar
        def _(act):
            for c in range(36):
                act.wait_ge(S["mm"], c + 1)
                ps = K.ps[c % 4][:, :]
                if c < 12:
                    ins = nc.scalar.activation(K.qa[:, c, :], ps, ACT.Copy, scale=0.125)
                elif c < 24:
                    ins = nc.scalar.activation(K.ka[:, c - 12, :], ps, ACT.Copy)
                else:
                    s, t = (c - 24) // NT, (c - 24) % NT
                    ins = nc.scalar.activation(K.va2[:, t, s * 512:(s + 1) * 512], ps, ACT.Copy)
                ins.then_inc(S["cop"], 1)

        @block.vector
        def _(dve):
            dve.memset(rb[:, :], 1.0).then_inc(S["one"], 1)
            K.ring.split(dve, n0)
            K.ring.split(dve, n0 + 1)
            for g in range(3):
                K.ring.split(dve, n0 + 2 + g)
                dve.wait_ge(S["bmm"], g + 1)
                if g:
                    dve.wait_ge(S["st"], 16 * g)
                dve.tensor_copy(R[:, 0:512], K.ps[4][0:8, :])
                dve.tensor_copy(R[:, 512:640], K.ps[5][0:8, 0:128]).then_inc(S["bcop"], 1)
            for n in range(n0 + 5, n0 + 9):
                K.ring.split(dve, n)


def feed_forward(nc, K, n0, load_upto):
    NF = FF2 // P
    rounds = [range(c, min(c + 4, NF)) for c in range(0, NF, 4)]
    down = n0 + 2 * len(rounds)
    with ExitStack() as ctx:
        S = sems(nc, ctx, "mm sig gated uped hid down fl", "F")
        hid, hid_low = twins(nc, ctx, "hid", [P, NF, T])
        hid_high = ctx.enter_context(nc.sbuf_tensor("hid_high", [P, NF, T], F32R))
        K.ring.used = {}
        for q, cs in enumerate(rounds):
            for j in range(2):
                K.ring.used[n0 + 2 * q + j] = (S["mm"], 8 * q + (j + 1) * len(cs))
            K.ring.used[down + q] = (S["down"], q + 1)
        block = ctx.enter_context(nc.Block())

        @block.sync
        def _(sp):
            K.ring.load(sp, load_upto)

        @block.tensor
        def _(pe):
            for q, cs in enumerate(rounds):
                for j in range(2):
                    n = n0 + 2 * q + j
                    for c in cs:
                        K.ring.wait(pe, n, c % 4)
                        if q:
                            pe.wait_ge(S["uped" if j else "gated"], c - 3)
                        mm_feature(pe, K.ps[4 * j + c % 4][:, :], (K.ring, n), slice((c % 4) * P, (c % 4) * P + P), K.hp,
                                   KD).then_inc(S["mm"], 1)
            pe.wait_ge(S["gated"], NF)
            for q, cs in enumerate(rounds):
                for f in cs:
                    K.ring.wait(pe, down + q, f % 4)
                    pe.wait_ge(S["hid"], f + 1)
                    for t in range(NT):
                        if f == 0 and t == 2:
                            pe.wait_ge(S["uped"], NF)
                        for half in range(2):
                            last = product(pe, K.ps[2 * t + half][:, :], [x[:, f, t * P:(t + 1) * P] for x in (hid_high, hid_low)],
                                           K.ring.cut(down + q, f % 4, slice(half * 512, (half + 1) * 512)), f == 0, f == NF - 1)
                last.then_inc(S["down"], 1)

        @block.scalar
        def _(act):
            for q, cs in enumerate(rounds):
                for i, c in enumerate(cs):
                    act.wait_ge(S["mm"], 8 * q + i + 1)
                    nc.scalar.activation(hid[:, c, :], K.ps[c % 4][:, :], ACT.Sigmoid).then_inc(S["sig"], 1)

        @block.vector
        def _(dve):
            link = linker(dve, S["fl"])
            K.ring.split(dve, n0)
            K.ring.split(dve, n0 + 1)
            for q, cs in enumerate(rounds):
                for i, c in enumerate(cs):
                    if i == 1 and q:
                        K.ring.split(dve, n0 + 2 * q + 1)
                    dve.wait_ge(S["sig"], c + 1)
                    dve.tensor_tensor(hid[:, c, :], hid[:, c, :], K.ps[c % 4][:, :], ALU.mult).then_inc(S["gated"], 1)
                for i, c in enumerate(cs):
                    if i == 1:
                        K.ring.split(dve, n0 + 2 * q + 2)
                    dve.wait_ge(S["gated"], c + 1)
                    dve.wait_ge(S["mm"], 8 * q + len(cs) + i + 1)
                    dve.tensor_tensor(hid[:, c, :], hid[:, c, :], K.ps[4 + c % 4][:, :], ALU.mult).then_inc(S["uped"], 1)
                    dve.wait_ge(S["uped"], c + 1)
                    link(high(dve, hid_high[:, c, :], hid[:, c, :]))
                    low(dve, hid_low[:, c, :], hid[:, c, :], hid_high[:, c, :]).then_inc(S["hid"], 1)
            for q in range(1, len(rounds)):
                K.ring.split(dve, down + q)
            dve.wait_ge(S["down"], len(rounds))
            for t in range(NT):
                for half in range(2):
                    o = K.x[:, t, half * 512:(half + 1) * 512]
                    dve.tensor_tensor(o, o, K.ps[2 * t + half][:, :], ALU.add)


def build(nc, I, out):
    ctx = ExitStack()
    with ctx:
        sb = lambda n, s, dt=F32: ctx.enter_context(nc.sbuf_tensor(n, s, dt))
        K = Buffers()
        K.I = I
        K.ps = [ctx.enter_context(nc.psum_tensor(f"ps{i}", [P, 512], F32)) for i in range(8)]
        K.ring = R = Ring(nc, ctx)
        K.ident = sb("ident", [P, P])
        w_in = I["w_in"][0]
        b_first = [R.plan(w_in[:, c:min(c + 512, 2688)], KD, min(512, 2688 - c)) for c in range(0, 2688, 512)][0]
        e_first = len(R.loads)
        for c in range(0, 2 * D, 512):
            R.plan(w_in[:, 2688 + c:2688 + c + 512], KD, 512)
        R.plan(I["w_proj_rwkv"][0], 4, D)
        R.plan(I["w_proj_attn"][0], 4, D)
        for c in range(0, D, 512):
            R.plan(I["w_out"][0][:, c:c + 512], KD, 512, rows=True)
        moe_first = len(R.loads)
        for e in range(N_EXP):
            for w in ("exp_w_gate", "exp_w_up", "exp_w_down"):
                for half in range(2):
                    R.plan_whole(I[w][0, e, half * 512:half * 512 + 512, :], 4, D, len(R.loads) - moe_first)
        second = len(R.loads)
        w2 = I["w_in_2"][0]
        for c0, cols in ((Q_M, 1024), (K_M, 1024), (V_M, 1024), (O_M, 1024), (Q_A, 1536), (K_A, 1536), (V_A, 1536), (G_A, 2048)):
            for c in range(c0, c0 + cols, 512):
                R.plan(w2[:, c:c + 512], KD, 512, rows=c0 in (V_M, V_A))
        for c in range(0, D, 512):
            R.plan(I["w_proj_a_2"][0][:, c:c + 512], KD, 512)
        R.plan(I["w_proj_b_2"][0], 4, D)
        for c in range(0, D, 512):
            R.plan(I["w_out_2"][0][:, c:c + 512], KD, 512, rows=True)
        ffn = len(R.loads)
        for c in range(0, FF2, 512):
            w = min(512, FF2 - c)
            for name in ("w_gate_2", "w_up_2"):
                R.plan(I[name][0][:, c:c + w], KD, w)
        for f in range(0, FF2, 512):
            w = min(512, FF2 - f)
            R.plan(I["w_down_2"][0][f:f + w, :], w // P, D, rows=True)
        K.x = sb("x", [P, NT, D])
        xs = I["x"][0]
        K.gains, K.w_router = sb("gains", [P, len(GAINS), KD]), sb("w_router", [P, KD, N_EXP])
        K.tok = sb("tok", [P, NT])
        S0 = sems(nc, ctx, "first small flip_in0 flip_in1")
        K.first_in, K.small_in, K.flip_in = S0["first"], S0["small"], (S0["flip_in0"], S0["flip_in1"])
        with ExitStack() as one:
            sb1 = lambda n, s: one.enter_context(nc.sbuf_tensor(n, s, F32))
            K.hT, h_low = twins(nc, one, "hT", [P, KD, T])
            K.yaT, ya_low = twins(nc, one, "yaT", [P, 4, T])
            K.u, u_parts = twins(nc, one, "u", [P, RC, T])
            with ExitStack() as att:
                sb2 = lambda n, s: att.enter_context(nc.sbuf_tensor(n, s, F32))
                K.qT, K.kT, K.va = sb2("qT", [P, 4, T]), sb2("kT", [P, 2, T]), sb2("va", [P, NT, P])
                K.sink, K.absrel = sb2("sink", [P, A_HEADS]), sb2("absrel", [P, 3 * P])
                with nc.sbuf_tensor("h_high", [P, KD, T], F32R) as hh, nc.sbuf_tensor("h_low", [P, KD, T], F32R) as hl:
                    K.hp = (hh, hl)
                    norm_transposed(nc, K, "1", K.x, 0, K.x, K.hT, xs, PAIR, K.hp)
                    first_projection(nc, K, b_first)
                ya = sb2("ya", [P, NT, 512])
                items = []
                for n in range(NT):
                    lo, hi = max(n - 1, 0), min(n + 1, NT - 1)
                    for h in range(A_HEADS):
                        b, g = 64 * (h % 2), h // 4
                        w = (hi - lo + 1) * P
                        r0 = (lo - (n - 1)) * P
                        items.append(dict(
                            segs=[(K.qT[b:b + 64, h // 2, n * P:(n + 1) * P], K.kT[b:b + 64, g, lo * P:(hi + 1) * P], w,
                                   K.absrel[:, r0:r0 + w], -(2.0 ** (-8.0 * (h + 1) / A_HEADS)))],
                            values=[K.va[:, kb, 64 * g:64 * g + 64] for kb in range(lo, hi + 1)],
                            sink=K.sink[:, h:h + 1], at=ya[:, n, 64 * h:64 * h + 64]))
                attention(nc, K, "A", items, ya, 3 * P, K.yaT)
            with ExitStack() as rw:
                sb2 = lambda n, s: rw.enter_context(nc.sbuf_tensor(n, s, F32))
                K.par = sb2("par", [P, 10, 4])
                K.wup, K.aup, K.gup = sb2("wup", [P, RW]), sb2("aup", [P, RW]), sb2("gup", [P, RW])
                K.masks, K.masks_t = sb2("masks", [P, 2, 2, P]), sb2("masks_t", [P, 2, 64])
                K.heads1, K.chunk0 = sb2("heads1", [P, P]), sb2("chunk0", [P, T])
                K.kk, K.ksum = sb2("kk", [P, 2, T]), sb2("ksum", [P, 2, T])
                K.SV = sb2("SV", [P, NCH, 2, 2, 64])
                K.Y = sb2("Y", [P, NCH, 2, 64])
                reverse = K.ring.buf[:, RING - 1, :].rearrange("p (i c n j s) -> p i c n j s", i=2, c=2, n=NCH, j=2)
                K.AR = (sb2("AR", [P, 2, NCH, 2, CHUNK]), reverse[:, 0])
                K.BK = (sb2("BK", [P, 2, NCH, 2, CHUNK]), reverse[:, 1])
                K.rates1 = [K.ring.buf[:, PAIR, i * 2 * T:(i + 1) * 2 * T].rearrange("p (c t) -> p c t", c=2) for i in range(2)]
                K.DC = (sb2("DC0", [P, 2, NCH]), sb2("DC1", [P, 2, NCH]))
                K.PX, K.PT, K.XF = sb2("PX", [P, 2, 2, P + 64]), sb2("PT", [P, 2, 2, P]), sb2("XF", [P, 2, 2, P])
                K.tmp = [K.x[:, i, :].rearrange("p (c t) -> p c t", c=2) for i in range(4)]
                rwkv_setup(nc, K)
                for hf in range(2):
                    rwkv_keys(nc, K, hf)
                    rwkv_decays(nc, K, hf)
                    rwkv_chunks(nc, K, hf, e_first if hf else None)
                    rwkv_output(nc, K, hf)
            K.yrT = K.u[:, 0:4, :]
            with nc.sbuf_tensor("h_high1", [P, KD, T], F32R) as hh:
                K.hp = (hh, h_low)
                merge_branches(nc, K, "E", [e_first + i for i in range(4)],
                               [(K.yrT, (u_parts[:, 4:8, :], u_parts[:, 0:4, :]), 4, [e_first + 4]),
                                (K.yaT[:, :, :], (u_parts[:, 8:12, :], ya_low[:, :, :]), 4, [e_first + 5])],
                               [e_first + 6, e_first + 7], moe_first + RING, xs, whole_h=K.hT)
            K.x1 = K.x
        with ExitStack() as moe:
            sb1 = lambda n, s: moe.enter_context(nc.sbuf_tensor(n, s, F32))
            K.xn = sb1("xn", [P, NT, D])
            K.IB = sb1("IB", [P, N_EXP, 256])
            K.gf = K.gains[:, 1, :]
            with nc.sbuf_tensor("hT2", [P, KD, T], F32) as K.hT:
                norm_transposed(nc, K, "2", K.x, 1, K.xn, K.hT)
                route(nc, K)
            experts(nc, K, moe_first, second + PAIR)
            K.x2 = K.x
        x3 = nc.dram_tensor("x3_dram", (T, D), F32, kind="Internal").ap()
        K.R_dram = nc.dram_tensor("bias_dram", (3, G2_HEADS, 640), F32, kind="Internal").ap()
        gain_norm(nc, K, "G1", I["norm_final_g"], keep_dram=x3)
        with ExitStack() as two:
            sb1 = lambda n, s: two.enter_context(nc.sbuf_tensor(n, s, F32))
            K.hT, h_low = twins(nc, two, "hT3", [P, KD, T])
            K.hp = (two.enter_context(nc.sbuf_tensor("h_high3", [P, KD, T], F32R)), h_low)
            norm_transposed(nc, K, "3", K.x, 2, K.x, K.hT, parts=K.hp, ahead=second)
            K.hm = K.x[:, :, :].rearrange("p t (h d) -> p t h d", h=M_HEADS)
            with ExitStack() as ml:
                sb2 = lambda n, s: ml.enter_context(nc.sbuf_tensor(n, s, F32))
                K.qmT, K.kmT = sb2("qmT", [P, KD, T]), sb2("kmT", [P, KD, T])
                K.vm = sb2("vm", [P, NT, M_HEADS, M_DH + 1])
                K.MB, K.WI = sb2("MB", [P, M_HEADS, T]), sb2("WI", [P, M_HEADS, T])
                K.cols, K.dec = sb2("cols", [P, 3, 16]), sb2("dec", [P, 16])
                K.sel4, K.causal = sb2("sel4", [4, 4, P]), sb2("causal", [P, P])
                mlstm_inputs(nc, K, second, second + 6 + PAIR)
                mlstm_cell(nc, K)
                K.ymT = K.qmT
                mlstm_output(nc, K, second + 6, second + 8 + PAIR)
                with nc.Block() as block:
                    @block.vector
                    def _(dve):
                        dve.tensor_copy(K.x[:, :, :].rearrange("p t (a b) -> p (t a) b", a=2), K.ymT[:, :, :])
            K.ymT = K.x[:, :, :].rearrange("p t (a b) -> p (t a) b", a=2)
            with_bias = ExitStack()
            BT, BT_parts = twins(nc, with_bias, "BT", [P, 2, 1280])
            K.ybT, yb_low = (t[:, :, :].rearrange("p a b -> p (a b)")[:, 0:4 * T].rearrange("p (c t) -> p c t", c=4)
                             for t in (BT, BT_parts))
            with ExitStack() as at:
                sb2 = lambda n, s: at.enter_context(nc.sbuf_tensor(n, s, F32))
                K.qa, K.ka, K.va2 = sb2("qa", [P, 12, T]), sb2("ka", [P, 12, T]), sb2("va2", [P, NT, 1536])
                K.flip = sb2("flip", [P, P])
                second_attention_inputs(nc, K, second + 8, second + 17 + PAIR, BT)
                yb = sb2("yb", [P, NT, 512])
                items = []
                for h in range(G2_HEADS):
                    for n in range(NT):
                        segs, vals = [], []
                        for g, (lo, c0, w0) in enumerate(((max(n - 1, 0), 0, 256), (0, 256, 512), (0, 768, 512))):
                            ch, b = 4 * g + h // 2, 64 * (h % 2)
                            w = (n + 1 - lo) * P
                            segs.append((K.qa[b:b + 64, ch, n * P:(n + 1) * P], K.ka[b:b + 64, ch, lo * P:(n + 1) * P], w,
                                         BT[:, h % 2, c0 + w0 - w:c0 + w0], 1.0))
                            vals += [K.va2[:, kb, 512 * g + 64 * h:512 * g + 64 * h + 64] for kb in range(lo, n + 1)]
                        items.append(dict(segs=segs, values=vals, sink=None, at=yb[:, n, 64 * h:64 * h + 64]))
                attention(nc, K, "B", items, yb, 1280, K.ybT, flips=BT)
            with ExitStack() as mg:
                sb2 = lambda n, k: mg.enter_context(nc.sbuf_tensor(n, [P, k, T], F32R))
                ym_high, ym_low, yb_high = sb2("ym_high", KD), sb2("ym_low", KD), sb2("yb_high", 4)
                merge_branches(nc, K, "H", [second + 17 + i for i in range(4)],
                               [(K.ymT, (ym_high[:, :, :], ym_low[:, :, :]), KD, [second + 21, second + 22]),
                                (K.ybT, (yb_high[:, :, :], yb_low), 4, [second + 23])],
                               [second + 24, second + 25], ffn + PAIR, x3, x_holds_y=True)
            with_bias.close()
            K.x4 = K.x
            with nc.sbuf_tensor("xn4", [P, NT, D], F32) as xn4:
                norm_transposed(nc, K, "4", K.x, 3, xn4, K.hT, parts=K.hp, ahead=ffn)
            feed_forward(nc, K, ffn, 10 ** 6)
        gain_norm(nc, K, "G2", I["norm_final_g_2"], out_dram=out)


def constants():
    rel = np.arange(3 * P)[None, :] - P - np.arange(P)[:, None]
    absrel = np.where(np.abs(rel) <= P, np.abs(rel), 1e33).astype(np.float32)
    s, t = np.arange(CHUNK)[:, None], np.arange(CHUNK)[None, :]
    masks, masks_t = np.zeros((P, 2, 2, P), np.float32), np.zeros((P, 2, CHUNK), np.float32)
    for d, (before, through) in enumerate(((s < t, s <= t), (s > t, s >= t))):
        for odd in range(2):
            b, k = slice(CHUNK * odd, CHUNK * odd + CHUNK), slice(CHUNK - CHUNK * odd, P - CHUNK * odd)
            masks[b, odd, d] = np.concatenate([-1.0 * before, 1.0 * through], 1)
            masks[k, odd, d] = np.concatenate([1.0 * before, 1.0 * through], 1)
            masks_t[b, d] = -1.0 * before.T
    heads1 = (np.arange(P)[:, None] // 64 == np.arange(P)[None, :] // 64).astype(np.float32)
    chunk0 = np.broadcast_to((np.arange(T) % CHUNK != 0).astype(np.float32), (P, T))
    reset = np.zeros((M_HEADS, 2, T), np.float32)
    reset[:, 0] = np.arange(T) % P != 0
    causal = (np.arange(P)[:, None] <= np.arange(P)[None, :]).astype(np.float32)
    dist = np.zeros((33, 3, 640), np.float32)
    for g, (window, dilation) in enumerate(WINDOWS):
        for r in range(640):
            n = 511 - r
            if n < 0 or n > window or n % dilation:
                dist[32, g, r] = -1e30
            else:
                large = 16 + int(np.float32(np.log(max(n, 16) / 16)) / np.float32(np.log(2048 / 16)) * np.float32(16))
                dist[n if n < 16 else min(large, 31), g, r] = 1.0
    return {"c_reset": reset, "c_causal": causal, "c_dist": dist, "c_flip": np.ascontiguousarray(np.eye(P, dtype=np.float32)[::-1]),
            "c_sel4": np.repeat(np.eye(M_HEADS, dtype=np.float32)[:, :, None], P, 2),
            "c_ident": np.eye(P, dtype=np.float32), "c_absrel": absrel, "c_masks": masks, "c_masks_t": masks_t,
            "c_sel": np.repeat(np.eye(N_EXP, dtype=np.float32)[:, :, None], P, 2),
            "c_tok": (np.arange(P)[:, None] + P * np.arange(NT)[None, :]).astype(np.float32),
            "c_heads1": heads1, "c_chunk0": chunk0}


_INS = ["x", "norm_mix_g", "w_in", "mu_prev", "mu_next", "w0_f", "w_up_f", "w0_b", "w_up_b", "a0_f", "a_up_f", "a0_b",
        "a_up_b", "g_up", "k_k", "k_a", "r_k", "ln_x_w", "ln_x_b", "attn_sink", "w_proj_rwkv", "w_proj_attn", "w_out",
        "norm_ffn_g", "w_router", "exp_w_gate", "exp_w_up", "exp_w_down", "norm_final_g", "norm_mix_g_2", "w_in_2",
        "b_gate_if_2", "conv_w_2", "conv_b_2", "mlstm_norm_g_2", "w_proj_a_2", "w_proj_b_2", "w_out_2",
        "norm_ffn_g_2", "w_gate_2", "w_up_2", "w_down_2", "rel_bias_2", "norm_final_g_2"]


def kernel(**inputs):
    import numpy as _np
    import concourse.bacc as _bacc
    from concourse.bass_utils import run_bass_kernel_spmd as _run

    nc = _bacc.Bacc("TRN2", target_bir_lowering=False, num_devices=1)
    arrays, aps = {}, {}
    for name, a in [(n, inputs[n]) for n in _INS] + list(constants().items()):
        a = _np.ascontiguousarray(a)
        arrays["in_" + name] = a
        aps[name] = nc.dram_tensor("in_" + name, a.shape, F32, kind="ExternalInput").ap()
    out = nc.dram_tensor("out_0", (1, T, D), F32, kind="ExternalOutput").ap()
    build(nc, aps, out[0])
    return _run(nc, [arrays], core_ids=[0]).results[0]["out_0"]
```
